# Optimizing a Trainium2 kernel written in Bass

```python
import math
import jax
import jax.numpy as jnp
from jax import lax
import numpy as np

D_MODEL = 1024
BATCH = 1
SEQ = 1024
DEPTH = 1
DEC_BATCH = 8
DEC_SEQ = 4
PAST_LEN = 1024
PAGE_SIZE = 128

D_MIX = D_MODEL
D_A = D_MIX // 2
A_GROUPS = 8
A_GDIM = D_A // A_GROUPS
CHUNK = 128
D_B = D_MIX - D_A
NSA_HEADS = 8
HEAD_DIM = D_B // NSA_HEADS
NSA_KV_HEADS = 2
HPG = NSA_HEADS // NSA_KV_HEADS
KV_DIM = NSA_KV_HEADS * HEAD_DIM
CMP_LEN = 32
CMP_STRIDE = 16
CMP_HID = 2 * HEAD_DIM
SEL_BLOCK = 64
SEL_TOP = 16
WINDOW = 512
QBLOCK = 128
REL_BUCKETS = 32
REL_MAX_DIST = 128
MEM_LEN = 256
XA_HEADS = 4
XA_HEAD_DIM = D_MODEL // XA_HEADS
D_FF = 2816
CONV_W = 3
D_IN = 2 * D_A + D_B + 6 * KV_DIM + 3 * NSA_HEADS
NORM_EPS = 1e-6
NEG_INF = -1e30
FORCE_BONUS = 1e4

kernel_name = 'nsa_gmlp_hybrid_step'

def _rmsnorm(x, g):
    xf = x.astype(jnp.float32)
    y = xf * lax.rsqrt(jnp.mean(xf * xf, axis=-1, keepdims=True) + NORM_EPS)
    return y.astype(x.dtype) * g

def _layernorm(x, g, b):
    xf = x.astype(jnp.float32)
    mu = jnp.mean(xf, axis=-1, keepdims=True)
    var = jnp.mean(jnp.square(xf - mu), axis=-1, keepdims=True)
    return ((xf - mu) * lax.rsqrt(var + NORM_EPS)).astype(x.dtype) * g + b

def _masked_softmax(logits, mask):
    p = jax.nn.softmax(jnp.where(mask, logits, NEG_INF), axis=-1)
    return p * mask

def _t5_bucket(dist):
    n = jnp.maximum(dist, 0)
    max_exact = REL_BUCKETS // 2
    nf = jnp.maximum(n, 1).astype(jnp.float32)
    large = max_exact + (jnp.log(nf / max_exact) / math.log(REL_MAX_DIST / max_exact)
                         * (REL_BUCKETS - max_exact)).astype(jnp.int32)
    large = jnp.minimum(large, REL_BUCKETS - 1)
    return jnp.where(n < max_exact, n, large)

def _rel_bias(dist, table):
    return jnp.moveaxis(table[_t5_bucket(dist)], -1, -3)

def _split_in(z):
    n, t = z.shape[:2]
    o2 = 2 * D_A
    o3 = o2 + D_B
    o4 = o3 + 6 * KV_DIM
    u = z[..., :D_A]
    v = z[..., D_A:o2]
    q = z[..., o2:o3].reshape(n, t, NSA_HEADS, HEAD_DIM)
    kv = z[..., o3:o4].reshape(n, t, 6, NSA_KV_HEADS, HEAD_DIM)
    gates = jax.nn.sigmoid(z[..., o4:].reshape(n, t, NSA_HEADS, 3))
    return (u, v, q, kv[:, :, 0], kv[:, :, 1], kv[:, :, 2], kv[:, :, 3],
            kv[:, :, 4], kv[:, :, 5], gates)

def _sgu(u, v, w_s, b_s):
    n, t = u.shape[:2]
    tc = min(t, CHUNK)
    n_c = t // tc
    causal = jnp.tril(jnp.ones((tc, tc), dtype=w_s.dtype))
    w = w_s[:, :tc, :tc] * causal
    vb = v.reshape(n, n_c, tc, A_GROUPS, A_GDIM)
    mixed = jnp.einsum('gts,ncsgd->nctgd', w, vb) + b_s[:, :tc].T[None, None, :, :, None]
    return u * mixed.reshape(n, t, D_A)

def _gmlp_mixer(u, v, p):
    u = jax.nn.gelu(u)
    v = _layernorm(jax.nn.gelu(v), p['ln_v_g'], p['ln_v_b'])
    return _sgu(u, v, p['w_s'], p['b_s']), v

def _compress(rows, w1, b1, w2, b2, pe):
    n, L = rows.shape[:2]
    n_sub = L // CMP_STRIDE
    sub = rows[:, :n_sub * CMP_STRIDE].reshape(n, n_sub, CMP_STRIDE, NSA_KV_HEADS, HEAD_DIM)
    first = jnp.einsum('nspgd,pdh->nsgh', sub, w1[:CMP_STRIDE])
    second = jnp.einsum('nspgd,pdh->nsgh', sub, w1[CMP_STRIDE:])
    hid = first[:, :-1] + second[:, 1:] + (jnp.einsum('pd,pdh->h', pe, w1) + b1)
    return jnp.einsum('ncgh,hd->ncgd', jax.nn.gelu(hid), w2) + b2

def _compress_kv(k_rows, v_rows, p):
    kc = _compress(k_rows, p['w_cmp1_k'], p['b_cmp1_k'], p['w_cmp2_k'], p['b_cmp2_k'], p['pe_cmp_k'])
    vc = _compress(v_rows, p['w_cmp1_v'], p['b_cmp1_v'], p['w_cmp2_v'], p['b_cmp2_v'], p['pe_cmp_v'])
    return kc, vc

def _sel_blocks(rows):
    n, L = rows.shape[:2]
    n_sel = -(-L // SEL_BLOCK)
    rows = jnp.pad(rows, ((0, 0), (0, n_sel * SEL_BLOCK - L), (0, 0), (0, 0)))
    return rows.reshape(n, n_sel, SEL_BLOCK, NSA_KV_HEADS, HEAD_DIM).transpose(0, 3, 1, 2, 4)

def _cmp_sel_overlap(n_cmp, n_sel):
    c0 = jnp.arange(n_cmp, dtype=jnp.int32)[:, None] * CMP_STRIDE
    s0 = jnp.arange(n_sel, dtype=jnp.int32)[None, :] * SEL_BLOCK
    return ((c0 < s0 + SEL_BLOCK) & (c0 + CMP_LEN > s0)).astype(jnp.float32)

def _cmp_sel_attend(q, q_pos, kc, vc, ks_blk, vs_blk, rel_bias):
    n, tq = q.shape[:2]
    n_cmp = kc.shape[1]
    n_sel = ks_blk.shape[2]
    scale = HEAD_DIM ** -0.5
    qg = q.reshape(n, tq, NSA_KV_HEADS, HPG, HEAD_DIM)
    cmp_end = jnp.arange(n_cmp, dtype=jnp.int32) * CMP_STRIDE + (CMP_LEN - 1)
    d_cmp = q_pos[:, None] - cmp_end[None, :]
    b_cmp = _rel_bias(d_cmp, rel_bias).reshape(NSA_KV_HEADS, HPG, tq, n_cmp).astype(jnp.float32)
    l_cmp = jnp.einsum('nqghd,ncgd->nghqc', qg, kc).astype(jnp.float32) * scale + b_cmp
    p_cmp = _masked_softmax(l_cmp, d_cmp >= 0)
    o_cmp = jnp.einsum('nghqc,ncgd->nqghd', p_cmp.astype(vc.dtype), vc)
    imp = jnp.einsum('nghqc,cs->ngqs', p_cmp, _cmp_sel_overlap(n_cmp, n_sel))
    blk = jnp.arange(n_sel, dtype=jnp.int32)[None, :]
    cur = (q_pos // SEL_BLOCK)[:, None]
    valid = blk * SEL_BLOCK <= q_pos[:, None]
    forced = (blk == 0) | (blk == cur) | (blk == cur - 1)
    score = jnp.where(valid, imp + FORCE_BONUS * forced, NEG_INF)
    n_top = min(SEL_TOP, n_sel)
    top_val, top_idx = lax.top_k(score, n_top)
    picked = top_val > 0.5 * NEG_INF
    n_ix = jnp.arange(n)[:, None, None, None]
    g_ix = jnp.arange(NSA_KV_HEADS)[None, :, None, None]
    k_sel = ks_blk[n_ix, g_ix, top_idx]
    v_sel = vs_blk[n_ix, g_ix, top_idx]
    k_pos = top_idx[..., None] * SEL_BLOCK + jnp.arange(SEL_BLOCK, dtype=jnp.int32)
    d_sel = q_pos[:, None, None] - k_pos
    m_sel = (picked[..., None] & (d_sel >= 0)).reshape(n, NSA_KV_HEADS, 1, tq, n_top * SEL_BLOCK)
    table = rel_bias.reshape(REL_BUCKETS, NSA_KV_HEADS, HPG)
    b_sel = table[_t5_bucket(d_sel), g_ix[..., None]]
    b_sel = jnp.moveaxis(b_sel, -1, 2).reshape(n, NSA_KV_HEADS, HPG, tq, n_top * SEL_BLOCK)
    l_sel = jnp.einsum('nqghd,ngqkpd->nghqkp', qg, k_sel).astype(jnp.float32)
    l_sel = l_sel.reshape(n, NSA_KV_HEADS, HPG, tq, n_top * SEL_BLOCK) * scale + b_sel.astype(jnp.float32)
    p_sel = _masked_softmax(l_sel, m_sel).reshape(n, NSA_KV_HEADS, HPG, tq, n_top, SEL_BLOCK)
    o_sel = jnp.einsum('nghqkp,ngqkpd->nqghd', p_sel.astype(v_sel.dtype), v_sel)
    return (o_cmp.reshape(n, tq, NSA_HEADS, HEAD_DIM), o_sel.reshape(n, tq, NSA_HEADS, HEAD_DIM))

def _window_attend(q, k, v, q_pos, k_pos, rel_bias):
    n, tq = q.shape[:2]
    s = k.shape[1]
    qg = q.reshape(n, tq, NSA_KV_HEADS, HPG, HEAD_DIM)
    dist = q_pos[:, None] - k_pos[None, :]
    bias = _rel_bias(dist, rel_bias).reshape(NSA_KV_HEADS, HPG, tq, s).astype(jnp.float32)
    logits = jnp.einsum('nqghd,nsgd->nghqs', qg, k).astype(jnp.float32) * HEAD_DIM ** -0.5 + bias
    mask = (dist >= 0) & (dist < WINDOW) & (k_pos[None, :] >= 0)
    p = _masked_softmax(logits, mask)
    o = jnp.einsum('nghqs,nsgd->nqghd', p.astype(v.dtype), v)
    return o.reshape(n, tq, NSA_HEADS, HEAD_DIM)

def _gate_branches(g, o_cmp, o_sel, o_win):
    return g[..., 0:1] * o_cmp + g[..., 1:2] * o_sel + g[..., 2:3] * o_win

def _nsa_prompt(q, kc_rows, vc_rows, ks, vs, kw, vw, gates, p, rel_bias):
    b, t = q.shape[:2]
    kc, vc = _compress_kv(kc_rows, vc_rows, p)
    ks_blk = _sel_blocks(ks)
    vs_blk = _sel_blocks(vs)
    pad = ((0, 0), (WINDOW, 0), (0, 0), (0, 0))
    kw_pad = jnp.pad(kw, pad)
    vw_pad = jnp.pad(vw, pad)
    n_qb = t // QBLOCK
    q_blocks = q.reshape(b, n_qb, QBLOCK, NSA_HEADS, HEAD_DIM).transpose(1, 0, 2, 3, 4)
    g_blocks = gates.reshape(b, n_qb, QBLOCK, NSA_HEADS, 3).transpose(1, 0, 2, 3, 4)

    def block(args):
        qb, gb, c = args
        start = c * QBLOCK
        q_pos = start + jnp.arange(QBLOCK, dtype=jnp.int32)
        o_cmp, o_sel = _cmp_sel_attend(qb, q_pos, kc, vc, ks_blk, vs_blk, rel_bias)
        k_band = lax.dynamic_slice_in_dim(kw_pad, start, WINDOW + QBLOCK, axis=1)
        v_band = lax.dynamic_slice_in_dim(vw_pad, start, WINDOW + QBLOCK, axis=1)
        k_pos = start - WINDOW + jnp.arange(WINDOW + QBLOCK, dtype=jnp.int32)
        o_win = _window_attend(qb, k_band, v_band, q_pos, k_pos, rel_bias)
        return _gate_branches(gb, o_cmp, o_sel, o_win)

    out = lax.map(block, (q_blocks, g_blocks, jnp.arange(n_qb, dtype=jnp.int32)))
    return out.transpose(1, 0, 2, 3, 4).reshape(b, t, D_B)

def _gather_pages(pool, page_table):
    n, n_pages = page_table.shape
    g = pool[page_table]
    return g.reshape((n, n_pages * pool.shape[1]) + pool.shape[2:])

def _nsa_sample(q, kc_new, vc_new, ks_new, vs_new, kw_new, vw_new, gates, pool_cmp_k, pool_cmp_v,
                pool_sel_k, pool_sel_v, win_k, win_v, page_table, p, rel_bias):
    n, tn = q.shape[:2]
    past = page_table.shape[1] * pool_cmp_k.shape[1]

    def full(pool, new):
        return jnp.concatenate([_gather_pages(pool, page_table), new], axis=1)

    kc, vc = _compress_kv(full(pool_cmp_k, kc_new), full(pool_cmp_v, vc_new), p)
    ks_blk = _sel_blocks(full(pool_sel_k, ks_new))
    vs_blk = _sel_blocks(full(pool_sel_v, vs_new))
    q_pos = past + jnp.arange(tn, dtype=jnp.int32)
    o_cmp, o_sel = _cmp_sel_attend(q, q_pos, kc, vc, ks_blk, vs_blk, rel_bias)
    win_buf = win_k.shape[1]
    kw_ext = jnp.concatenate([win_k, kw_new], axis=1)
    vw_ext = jnp.concatenate([win_v, vw_new], axis=1)
    k_pos = past - win_buf + jnp.arange(win_buf + tn, dtype=jnp.int32)
    o_win = _window_attend(q, kw_ext, vw_ext, q_pos, k_pos, rel_bias)
    keep = min(WINDOW, past + tn)
    out = _gate_branches(gates, o_cmp, o_sel, o_win).reshape(n, tn, D_B)
    return out, kw_ext[:, -keep:], vw_ext[:, -keep:]

def _mix_out(a_out, b_out, p):
    merged = jnp.concatenate([_rmsnorm(a_out, p['g_a']), _rmsnorm(b_out, p['g_b'])], axis=-1)
    return merged @ p['w_o']

def _mem_kv(mem, p):
    n, m = mem.shape[:2]
    mn = _rmsnorm(mem, p['g_mem'])
    mk = (mn @ p['w_mk']).reshape(n, m, XA_HEADS, XA_HEAD_DIM)
    mv = (mn @ p['w_mv']).reshape(n, m, XA_HEADS, XA_HEAD_DIM)
    return mk, mv

def _cross_attend(h, mk, mv, p):
    n, t = h.shape[:2]
    q = (h @ p['w_xq']).reshape(n, t, XA_HEADS, XA_HEAD_DIM)
    logits = jnp.einsum('nthd,nmhd->nhtm', q, mk).astype(jnp.float32) * XA_HEAD_DIM ** -0.5
    pr = jax.nn.softmax(logits, axis=-1).astype(mv.dtype)
    o = jnp.einsum('nhtm,nmhd->nthd', pr, mv).reshape(n, t, D_MODEL)
    return o @ p['w_xo']

def _conv_ffn(h, prev, p):
    t = h.shape[1]
    a = h @ p['w_up']
    g = h @ p['w_gate']
    ext = jnp.concatenate([prev, a], axis=1)
    c = p['conv_b']
    for i in range(CONV_W):
        c = c + ext[:, i:i + t] * p['conv_w'][i]
    return (jax.nn.gelu(c) * g) @ p['w_down'], ext[:, t:]

def _layer_prompt(x, mem, p, rel_bias):
    b, t = x.shape[:2]
    h = _rmsnorm(x, p['g_mix'])
    u, v, q, kc, vc, ks, vs, kw, vw, gates = _split_in(h @ p['w_in'])
    a_out, _ = _gmlp_mixer(u, v, p)
    b_out = _nsa_prompt(q, kc, vc, ks, vs, kw, vw, gates, p, rel_bias)
    x = x + _mix_out(a_out, b_out, p)
    mk, mv = _mem_kv(mem, p)
    x = x + _cross_attend(_rmsnorm(x, p['g_xa']), mk, mv, p)
    f, conv_new = _conv_ffn(_rmsnorm(x, p['g_ffn']), jnp.zeros((b, CONV_W - 1, D_FF), x.dtype), p)
    x = x + f
    keep = min(WINDOW, t)
    return x, (kc, vc, ks, vs, kw[:, -keep:], vw[:, -keep:], mk, mv, conv_new)

def _layer_sample(x, pool_cmp_k, pool_cmp_v, pool_sel_k, pool_sel_v, win_k, win_v, mem_k, mem_v,
                  conv_prev, page_table, p, rel_bias):
    h = _rmsnorm(x, p['g_mix'])
    u, v, q, kc, vc, ks, vs, kw, vw, gates = _split_in(h @ p['w_in'])
    a_out, v_rows = _gmlp_mixer(u, v, p)
    b_out, win_k_new, win_v_new = _nsa_sample(q, kc, vc, ks, vs, kw, vw, gates, pool_cmp_k, pool_cmp_v,
                                              pool_sel_k, pool_sel_v, win_k, win_v, page_table, p, rel_bias)
    x = x + _mix_out(a_out, b_out, p)
    x = x + _cross_attend(_rmsnorm(x, p['g_xa']), mem_k, mem_v, p)
    f, conv_new = _conv_ffn(_rmsnorm(x, p['g_ffn']), conv_prev, p)
    x = x + f
    return x, (kc, vc, ks, vs, win_k_new, win_v_new, v_rows, conv_new)

def setup_inputs(seed: int = 0) -> dict:
    key = jax.random.key(seed)
    keys = jax.random.split(key, 80)
    counter = [0]

    def nxt():
        counter[0] += 1
        return keys[counter[0] - 1]

    def nrm(shape, scale=1.0):
        return jax.random.normal(nxt(), shape, jnp.float32) * scale

    def gain(shape):
        return 1.0 + nrm(shape, 0.02)

    n_pages = PAST_LEN // PAGE_SIZE
    n_used = DEC_BATCH * n_pages
    n_pool = n_used + n_used // 4
    win_buf = min(WINDOW, PAST_LEN)
    pool_shape = (DEPTH, n_pool, PAGE_SIZE, NSA_KV_HEADS, HEAD_DIM)
    page_table = jax.random.permutation(nxt(), n_pool)[:n_used].reshape(DEC_BATCH, n_pages).astype(jnp.int32)
    return {
        'x_prompt': nrm((BATCH, SEQ, D_MODEL)),
        'x_sample': nrm((DEC_BATCH, DEC_SEQ, D_MODEL)),
        'mem_prompt': nrm((BATCH, MEM_LEN, D_MODEL)),
        'cache_cmp_k': nrm(pool_shape),
        'cache_cmp_v': nrm(pool_shape),
        'cache_sel_k': nrm(pool_shape),
        'cache_sel_v': nrm(pool_shape),
        'cache_win_k': nrm((DEPTH, DEC_BATCH, win_buf, NSA_KV_HEADS, HEAD_DIM)),
        'cache_win_v': nrm((DEPTH, DEC_BATCH, win_buf, NSA_KV_HEADS, HEAD_DIM)),
        'cache_mem_k': nrm((DEPTH, DEC_BATCH, MEM_LEN, XA_HEADS, XA_HEAD_DIM)),
        'cache_mem_v': nrm((DEPTH, DEC_BATCH, MEM_LEN, XA_HEADS, XA_HEAD_DIM)),
        'state_conv': nrm((DEPTH, DEC_BATCH, CONV_W - 1, D_FF)),
        'page_table': page_table,
        'g_mix': gain((DEPTH, D_MODEL)),
        'w_in': nrm((DEPTH, D_MODEL, D_IN), D_MODEL ** -0.5),
        'w_s': nrm((DEPTH, A_GROUPS, CHUNK, CHUNK), CHUNK ** -0.5),
        'b_s': gain((DEPTH, A_GROUPS, CHUNK)),
        'ln_v_g': gain((DEPTH, D_A)),
        'ln_v_b': nrm((DEPTH, D_A), 0.02),
        'w_cmp1_k': nrm((DEPTH, CMP_LEN, HEAD_DIM, CMP_HID), (CMP_LEN * HEAD_DIM) ** -0.5),
        'b_cmp1_k': nrm((DEPTH, CMP_HID), 0.02),
        'w_cmp2_k': nrm((DEPTH, CMP_HID, HEAD_DIM), CMP_HID ** -0.5),
        'b_cmp2_k': nrm((DEPTH, HEAD_DIM), 0.02),
        'pe_cmp_k': nrm((DEPTH, CMP_LEN, HEAD_DIM), 0.1),
        'w_cmp1_v': nrm((DEPTH, CMP_LEN, HEAD_DIM, CMP_HID), (CMP_LEN * HEAD_DIM) ** -0.5),
        'b_cmp1_v': nrm((DEPTH, CMP_HID), 0.02),
        'w_cmp2_v': nrm((DEPTH, CMP_HID, HEAD_DIM), CMP_HID ** -0.5),
        'b_cmp2_v': nrm((DEPTH, HEAD_DIM), 0.02),
        'pe_cmp_v': nrm((DEPTH, CMP_LEN, HEAD_DIM), 0.1),
        'rel_bias': nrm((REL_BUCKETS, NSA_HEADS), 0.5),
        'g_a': gain((DEPTH, D_A)),
        'g_b': gain((DEPTH, D_B)),
        'w_o': nrm((DEPTH, D_MIX, D_MODEL), D_MIX ** -0.5),
        'g_xa': gain((DEPTH, D_MODEL)),
        'g_mem': gain((DEPTH, D_MODEL)),
        'w_xq': nrm((DEPTH, D_MODEL, D_MODEL), D_MODEL ** -0.5),
        'w_mk': nrm((DEPTH, D_MODEL, D_MODEL), D_MODEL ** -0.5),
        'w_mv': nrm((DEPTH, D_MODEL, D_MODEL), D_MODEL ** -0.5),
        'w_xo': nrm((DEPTH, D_MODEL, D_MODEL), D_MODEL ** -0.5),
        'g_ffn': gain((DEPTH, D_MODEL)),
        'w_up': nrm((DEPTH, D_MODEL, D_FF), D_MODEL ** -0.5),
        'w_gate': nrm((DEPTH, D_MODEL, D_FF), D_MODEL ** -0.5),
        'conv_w': nrm((DEPTH, CONV_W, D_FF), CONV_W ** -0.5),
        'conv_b': nrm((DEPTH, D_FF), 0.02),
        'w_down': nrm((DEPTH, D_FF, D_MODEL), D_FF ** -0.5),
        'g_final': gain((D_MODEL,)),
    }

def reference(x_prompt, x_sample, mem_prompt, cache_cmp_k, cache_cmp_v, cache_sel_k, cache_sel_v,
              cache_win_k, cache_win_v, cache_mem_k, cache_mem_v, state_conv, page_table,
              g_mix, w_in, w_s, b_s, ln_v_g, ln_v_b,
              w_cmp1_k, b_cmp1_k, w_cmp2_k, b_cmp2_k, pe_cmp_k,
              w_cmp1_v, b_cmp1_v, w_cmp2_v, b_cmp2_v, pe_cmp_v,
              rel_bias, g_a, g_b, w_o, g_xa, g_mem, w_xq, w_mk, w_mv, w_xo,
              g_ffn, w_up, w_gate, conv_w, conv_b, w_down, g_final):
    yp = x_prompt
    ys = x_sample
    st_p = []
    st_s = []
    for l in range(DEPTH):
        p = dict(g_mix=g_mix[l], w_in=w_in[l], w_s=w_s[l], b_s=b_s[l], ln_v_g=ln_v_g[l], ln_v_b=ln_v_b[l],
                 w_cmp1_k=w_cmp1_k[l], b_cmp1_k=b_cmp1_k[l], w_cmp2_k=w_cmp2_k[l], b_cmp2_k=b_cmp2_k[l],
                 pe_cmp_k=pe_cmp_k[l], w_cmp1_v=w_cmp1_v[l], b_cmp1_v=b_cmp1_v[l], w_cmp2_v=w_cmp2_v[l],
                 b_cmp2_v=b_cmp2_v[l], pe_cmp_v=pe_cmp_v[l], g_a=g_a[l], g_b=g_b[l], w_o=w_o[l],
                 g_xa=g_xa[l], g_mem=g_mem[l], w_xq=w_xq[l], w_mk=w_mk[l], w_mv=w_mv[l], w_xo=w_xo[l],
                 g_ffn=g_ffn[l], w_up=w_up[l], w_gate=w_gate[l], conv_w=conv_w[l], conv_b=conv_b[l],
                 w_down=w_down[l])
        yp, sp = _layer_prompt(yp, mem_prompt, p, rel_bias)
        ys, ss = _layer_sample(ys, cache_cmp_k[l], cache_cmp_v[l], cache_sel_k[l], cache_sel_v[l],
                               cache_win_k[l], cache_win_v[l], cache_mem_k[l], cache_mem_v[l],
                               state_conv[l], page_table, p, rel_bias)
        st_p.append(sp)
        st_s.append(ss)
    y_prompt = _rmsnorm(yp, g_final)
    y_sample = _rmsnorm(ys, g_final)

    def stk(states, i):
        return jnp.stack([s[i] for s in states])

    return (y_prompt, y_sample,
            stk(st_p, 0), stk(st_p, 1), stk(st_p, 2), stk(st_p, 3), stk(st_p, 4), stk(st_p, 5),
            stk(st_p, 6), stk(st_p, 7), stk(st_p, 8),
            stk(st_s, 0), stk(st_s, 1), stk(st_s, 2), stk(st_s, 3), stk(st_s, 4), stk(st_s, 5),
            stk(st_s, 6), stk(st_s, 7))


_drawn_inputs = setup_inputs


def setup_inputs(seed=0):
    import zlib

    import numpy as np

    out = dict(_drawn_inputs(seed))
    spreads = {}
    factors = {'b_s': 5.581,
     'ln_v_g': 8.562,
     'ln_v_b': 8.755,
     'b_cmp1_k': 8.0,
     'b_cmp2_k': 200.0,
     'pe_cmp_k': 5.625,
     'b_cmp1_v': 3.796,
     'g_a': 5.053,
     'g_b': 4.802,
     'g_xa': 8.0,
     'g_mem': 2.836,
     'conv_b': 21.936,
     'g_final': 22.63,
     'g_ffn': 7.182}
    for name, (base, spread) in spreads.items():
        noise = np.random.default_rng([zlib.crc32(name.encode()), seed]).standard_normal(out[name].shape)
        drawn = base * np.exp(spread * noise) if base else spread * noise
        out[name] = jnp.asarray(drawn.astype(out[name].dtype))
    for name, factor in factors.items():
        out[name] = (out[name] * factor).astype(out[name].dtype)
    return out
```

```python
import math
from contextlib import ExitStack

import numpy as np
import concourse.bass as bass
from concourse import mybir

F32 = mybir.dt.float32
F32R = mybir.dt.float32r
I32 = mybir.dt.int32
ALU = mybir.AluOpType
ACT = mybir.ActivationFunctionType
AX = mybir.AxisListType

P = 128
D = 1024
KD = D // P
SEQ = 1024
NS, TS = 8, 4
T = SEQ + NS * TS
TILES = SEQ // P + 1
SROWS = NS * TS
FREE3 = T // 3
DA = 512
AG, AGD = 8, 64
H, HKV, HPG, HD = 8, 2, 4, 64
KV = HKV * HD
PAST, PAGE, NPAGE = 1024, 128, 8
CL, CS = 32, 16
NCMP = PAST // CS - 1
SELB = 64
NSEL = 17
WIN = 512
BUCKETS, MAXDIST = 32, 128
MEM = 256
XH, XHD = 4, 256
FF = 2816
FC = FF // P
NEG = -1e30
EPS = 1e-6
TMW = 2 * DA + 2 * KV + 3 * H
VECS, VECW = 2048, 768
STRS, STRW = 1920, 640

O_HT = 0
O_W = O_HT + KD * T
O_M = O_W + KD * TMW
O_FM = O_M + TILES * D
O_VT = O_FM + 8 * T
O_TMP = O_VT + TILES * 2 * KV
O_CP = O_TMP + 2 * D
BIG = O_CP + 63 + 128 + 504 + 1024 + 1


def rows_of(t):
    return P if t < TILES - 1 else SROWS


class Chain:

    def __init__(self, eng, sem):
        self.eng, self.sem, self.n = eng, sem, 0

    def __call__(self, ins):
        self.n += 1
        ins.then_inc(self.sem, 1)
        self.eng.wait_ge(self.sem, self.n)


def norm_phase(nc, K, tag, tiles, width, gain, dst, loads=None, extra=None, split=None):
    parts = D // width
    n = len(tiles)
    S = K.sem
    stat_zero, squares, std_ready = S(f"{tag}_stat_set"), S(f"{tag}_squares"), S(f"{tag}_std")
    rstd_ready, scaled, turned, taken = S(f"{tag}_rstd"), S(f"{tag}_scaled"), S(f"{tag}_turned"), S(f"{tag}_taken")
    arrived = [S(f"{tag}_x{i}") for i in range(n)] if loads else None
    ss, std, rs = K.stat[:, 0, :n * parts], K.stat[:, 1, :n * parts], K.stat[:, 2, :n * parts]
    xn = K.tmp.rearrange("p (b n) -> p b n", b=2)
    if split:
        high, low, whole = split
        high_made, low_made = S(f"{tag}_high"), S(f"{tag}_low")

    with nc.Block() as block:
        @block.sync
        def _(sp):
            if loads:
                for i, (to, of) in enumerate(loads):
                    sp.dma_start(to, of).then_inc(arrived[i], 16)
            if extra and "sync" in extra:
                extra["sync"](sp)

        @block.gpsimd
        def _(pool):
            if extra and "gpsimd" in extra:
                extra["gpsimd"](pool)
            if split:
                for i, (_, rows, col) in enumerate(tiles):
                    for b in range(2):
                        pool.wait_ge(high_made, 2 * i + b + 1)
                        at = (slice(None), slice(4 * b, 4 * b + 4), slice(col, col + rows))
                        nc.gpsimd.tensor_tensor(low[at], whole[:, i % 2, 4 * b:4 * b + 4, 0:rows], high[at],
                                                ALU.subtract).then_inc(low_made, 1)

        @block.scalar
        def _(act):
            act.wait_ge(stat_zero, 1)
            for i, (src, rows, _) in enumerate(tiles):
                if loads:
                    act.wait_ge(arrived[i], 16)
                for q in range(parts):
                    if i + q:
                        act.wait_ge(squares, i * parts + q)
                    nc.scalar.activation(K.junk[:rows, 0:width], src[:, q * width:(q + 1) * width], ACT.Square,
                                         accum_out=ss[:rows, i * parts + q:i * parts + q + 1]).then_inc(squares, 1)
            act.wait_ge(squares, n * parts)
            nc.scalar.activation(std, ss, ACT.Sqrt, bias=K.eps[:, 0:1], scale=1.0 / width).then_inc(std_ready, 1)
            if extra and "scalar" in extra:
                extra["scalar"](act)
            if split:
                for i, (_, rows, col) in enumerate(tiles):
                    for b in range(2):
                        act.wait_ge(taken, 2 * i + b + 1)
                        nc.scalar.activation(high[:, 4 * b:4 * b + 4, col:col + rows], whole[:, i % 2, 4 * b:4 * b + 4, 0:rows],
                                             ACT.Copy).then_inc(high_made, 1)

        @block.vector
        def _(dve):
            nc.vector.memset(ss, 1.0).then_inc(stat_zero, 1)
            dve.wait_ge(std_ready, 1)
            nc.vector.reciprocal(rs, std).then_inc(rstd_ready, 1)
            dve.wait_ge(rstd_ready, 1)

            def scale(i):
                src, rows, _ = tiles[i]
                if i >= 2:
                    dve.wait_ge(turned, 2 * (i - 1))
                for q in range(parts):
                    last = nc.vector.tensor_scalar(xn[:rows, i % 2, q * width:(q + 1) * width],
                                                   src[:, q * width:(q + 1) * width],
                                                   rs[:rows, i * parts + q:i * parts + q + 1], None, ALU.mult)
                last.then_inc(scaled, 1)

            def take(i):
                _, rows, col = tiles[i]
                for b in range(2):
                    dve.wait_ge(turned, 2 * i + b + 1)
                    src = K.bank[2 * (i % 2) + b][:, :].rearrange("p (k n) -> p k n", k=4)[:, :, 0:rows]
                    if split and i >= 2:
                        dve.wait_ge(low_made, 2 * (i - 2) + b + 1)
                    to = whole[:, i % 2, 4 * b:4 * b + 4, 0:rows] if split else dst[:, 4 * b:4 * b + 4, col:col + rows]
                    nc.vector.tensor_tensor(to, src,
                                            gain[:, 4 * b:4 * b + 4].unsqueeze(2).to_broadcast([P, 4, rows]),
                                            ALU.mult).then_inc(taken, 1)

            scale(0)
            for i in range(n):
                if i + 1 < n:
                    scale(i + 1)
                take(i)
            if extra and "vector" in extra:
                extra["vector"](dve)

        @block.tensor
        def _(pe):
            for i, (_, rows, _) in enumerate(tiles):
                pe.wait_ge(scaled, i + 1)
                for b in range(2):
                    if i >= 2:
                        pe.wait_ge(taken, 2 * (i - 2) + b + 1)
                    for k in range(4):
                        last = nc.tensor.transpose(K.bank[2 * (i % 2) + b][:, k * P:k * P + rows],
                                                   xn[:rows, i % 2, (4 * b + k) * P:(4 * b + k + 1) * P],
                                                   K.ident[:rows, :rows])
                    last.then_inc(turned, 1)
            if extra and "tensor" in extra:
                extra["tensor"](pe)


def x_tiles(K):
    return [(K.X[:rows_of(t), t, :], rows_of(t), t * P) for t in range(TILES)]


def x_loads(K, I):
    return [(K.X[:rows_of(t), t, :], I["x_prompt"][t] if t < TILES - 1 else I["x_sample"]) for t in range(TILES)]


def feature_major(nc, K, tag, w_dram, chunks, ring, src, cols, dst, extra=None):
    S = K.sem
    came = [S(f"{tag}_w{u}") for u in range(2)]
    done = [S(f"{tag}_product{u}") for u in range(2)]
    taken = [S(f"{tag}_taken{u}") for u in range(2)]
    K.fm_taken = taken
    pieces = [(a, min(a + FREE3, cols)) for a in range(0, cols, FREE3)]
    with nc.Block() as block:
        @block.sync
        def _(sp):
            for c in range(chunks):
                u = c % 2
                if c >= 2:
                    sp.wait_ge(done[u], c // 2)
                sp.dma_start(ring[:, u], w_dram[c]).then_inc(came[u], 16)
                if extra and ("sync", c) in extra:
                    extra["sync", c](sp)
            if extra and "sync" in extra:
                extra["sync"](sp)

        @block.tensor
        def _(pe):
            with pe.Fori(0, chunks // 2) as i:
                for u in range(2):
                    pe.wait_ge(came[u], i * 16 + 16)
                    pe.wait_ge(taken[u], i + 1)
                    for s, (a, b) in enumerate(pieces):
                        for k in range(KD):
                            last = nc.tensor.matmul(K.bank[3 * u + s][:, 0:b - a], ring[:, u, k, :], src[:, k, a:b],
                                                    start=k == 0, stop=k == KD - 1)
                    last.then_inc(done[u], 1)

        @block.scalar
        def _(act):
            for u in range(2):
                act.sem_inc(taken[u], 1)
            with act.Fori(0, chunks // 2) as i:
                for u in range(2):
                    act.wait_ge(done[u], i + 1)
                    for s, (a, b) in enumerate(pieces):
                        last = nc.scalar.activation(dst[:, bass.ds(i * 2 + u, 1), a:b].rearrange("p c n -> p (c n)"),
                                                    K.bank[3 * u + s][:, 0:b - a], ACT.Copy)
                    last.then_inc(taken[u], 1)


def projection_weights(K, tag, w_dram):
    w = K.big[:, O_W:O_W + KD * D].rearrange("p (h k n) -> p h k n", h=2, k=KD)
    came = [K.sem(f"{tag}_w{h}") for h in range(2)]

    def load(sp):
        for h in range(2):
            sp.dma_start(w[:, h], w_dram[h]).then_inc(came[h], 16)

    return w, came, load


def project_add(nc, K, tag, weights, src, x_came=None):
    S = K.sem
    w, came, _ = weights
    done, taken = S(f"{tag}_product"), S(f"{tag}_taken")
    with nc.Block() as block:
        @block.tensor
        def _(pe):
            for j in range(2 * TILES):
                h, t = j // TILES, j % TILES
                if t == 0:
                    pe.wait_ge(came[h], 16)
                if j >= 4:
                    pe.wait_ge(taken, j - 3)
                for k in range(KD):
                    last = nc.tensor.matmul(K.bank[j % 4][:rows_of(t), :], src[:, k, t * P:t * P + rows_of(t)],
                                            w[:, h, k, :], start=k == 0, stop=k == KD - 1)
                last.then_inc(done, 1)

        @block.vector
        def _(dve):
            if x_came:
                dve.wait_ge(x_came, 16 * TILES)
            for j in range(2 * TILES):
                h, t = j // TILES, j % TILES
                x = K.X[:rows_of(t), t, h * 512:(h + 1) * 512]
                dve.wait_ge(done, j + 1)
                nc.vector.tensor_tensor(x, K.bank[j % 4][:rows_of(t), :], x, ALU.add).then_inc(taken, 1)


def gather(sp, K, half, to, of, came):
    regs = K.page_regs = K.page_regs or [sp.alloc_register(f"page{b}") for b in range(NPAGE)]
    with sp.Fori(0, NS // 2) as n:
        sp.load(regs, K.page_table[0:1, bass.ds(n * NPAGE + half * (NS // 2) * NPAGE, NPAGE)])
        pages = [sp.snap(r, min_val=0, max_val=K.n_pool - 1) for r in regs]
        for b, page in enumerate(pages):
            sp.dma_start(to(n * NPAGE + b), of(page)).then_inc(came, 16)


def gather_cmp(sp, I, K, v, half, slot):
    pages = K.slot[slot].rearrange("p (g t) -> p g t", g=2)
    gather(sp, K, half, lambda pg: pages[:, :, bass.ds(pg * (PAGE // 2), PAGE // 2)],
           lambda page: I["pool_cmp"][v][bass.ds(page, 1)].rearrange("a p g t -> (a p) g t"), K.slot_came[slot])


def gather_sel(sp, I, K, name, half, slot):
    gather(sp, K, half, lambda pg: K.slot[slot][:, bass.ds(pg * P, P)],
           lambda page: I[name][bass.ds(page, 1)].rearrange("a p t -> (a p) t"), K.slot_came[slot])


SLOT_PAGES = 16 * NS * NPAGE // 2


def gating_operands(K, I):
    tmp = K.big[:, O_TMP:O_TMP + 2 * D]
    cp = K.big[:, O_CP:O_CP + 1720]
    ws = tmp[:, 2 * DA:].rearrange("p (g t) -> p g t", g=AG)
    wss = cp[:, 512:768].rearrange("p (g t) -> p g t", g=AG)
    return [(tmp[:, 0:DA], I["ln_v_g"].to_broadcast([P, DA])), (tmp[:, DA:2 * DA], I["ln_v_b"].to_broadcast([P, DA])),
            (ws, I["ws_t"]), (wss[:SROWS], I["ws_s"]), (cp[:, 768:776], I["bs_t"]), (cp[:SROWS, 776:784], I["bs_s"]),
            (cp[:, 784:912], I["causal"]), (cp[:SROWS, 912:944], I["causal_s"]), (cp[:, 990:991], I["cmp_valid"])]


def gating_phase(nc, K, I, O):
    S = K.sem
    p_done, uv_taken, rest_taken = S("in_product"), S("in_uv_taken"), S("in_rest_taken")
    a_chain, sd_ready, v_ready, v_chain = S("in_act"), S("in_sd"), S("in_v_ready"), S("in_dve")
    mixed, mixed_used, masked, a_out = S("in_mixed"), S("in_mixed_used"), S("in_ws_masked"), S("in_out")
    sig, gd = S("in_sigmoid"), K.gating_sem
    w = K.big[:, O_W:O_W + KD * TMW].rearrange("p (k n) -> p k n", k=KD)
    tmp = K.big[:, O_TMP:O_TMP + 2 * D]
    lng, lnb = tmp[:, 0:DA], tmp[:, DA:2 * DA]
    ws = tmp[:, 2 * DA:].rearrange("p (g t) -> p g t", g=AG)
    cp = K.big[:, O_CP:O_CP + 1720]
    junk, wss = cp[:, 0:512], cp[:, 512:768].rearrange("p (g t) -> p g t", g=AG)
    bs, bss = cp[:, 768:776], cp[:, 776:784]
    caus, causs = cp[:, 784:912], cp[:, 912:944]
    nm, sq, sd, rsd, sv = (cp[:, 944 + 9 * i:953 + 9 * i] for i in range(5))
    valid = cp[:, 990:991]
    cuts = [(0, DA), (DA, 2 * DA), (2 * DA, TMW)]

    with nc.Block() as block:
        @block.sync
        def _(sp):
            sp.wait_ge(v_ready, TILES)
            sp.dma_start(O["gmlp_v"], K.M[:SROWS, TILES - 1, DA:D]).then_inc(K.out_sem, 16)
            sp.wait_ge(rest_taken, 2 * TILES)
            sp.dma_start(O["vt"].rearrange("t p n -> p t n"), K.VT[:, 0:8, :]).then_inc(K.out_sem, 16)
            sp.dma_start(O["vt_s"], K.VT[:SROWS, 8, :]).then_inc(K.out_sem, 16)
            sp.wait_ge(sig, 2)
            sp.dma_start(K.gates_dram, K.GT[:SROWS, 8, :]).then_inc(K.gates_sem, 16)
            sp.wait_ge(K.out_sem, 16 * K.outs(3))
            sp.wait_ge(K.gates_sem, 16)

        @block.tensor
        def _(pe):
            pe.wait_ge(K.wtm_sem, 16 * KD)
            pe.wait_ge(masked, 2)

            def gate(t):
                r = rows_of(t)
                pe.wait_ge(v_ready, t + 1)
                if t >= 2:
                    pe.wait_ge(mixed_used, t - 1)
                for g in range(AG):
                    lhs = ws[:, g, :] if r == P else wss[:SROWS, g, :]
                    last = nc.tensor.matmul(K.bank[6 + t % 2][:r, g * AGD:(g + 1) * AGD], lhs,
                                            K.M[:r, t, DA + g * AGD:DA + (g + 1) * AGD], start=True, stop=True)
                last.then_inc(mixed, 1)

            for t in range(TILES):
                r = rows_of(t)
                if t >= 2:
                    pe.wait_ge(uv_taken, 2 * (t - 1))
                    pe.wait_ge(rest_taken, 2 * (t - 1))
                for s, (a, b) in enumerate(cuts):
                    for k in range(KD):
                        last = nc.tensor.matmul(K.bank[3 * (t % 2) + s][:r, 0:b - a],
                                                K.HT[:, k, t * P:t * P + r], w[:, k, a:b],
                                                start=k == 0, stop=k == KD - 1)
                last.then_inc(p_done, 1)
                if t >= 1:
                    gate(t - 1)
            gate(TILES - 1)

        @block.scalar
        def _(act):
            link = Chain(act, a_chain)
            for t in range(TILES):
                r = rows_of(t)
                bank = 3 * (t % 2)
                act.wait_ge(p_done, t + 1)
                nc.scalar.activation(K.M[:r, t, 0:DA], K.bank[bank][:r, :], ACT.Gelu_apprx_tanh).then_inc(uv_taken, 1)
                nc.scalar.activation(K.M[:r, t, DA:D], K.bank[bank + 1][:r, :], ACT.Gelu_apprx_tanh,
                                     accum_out=sv[:r, t:t + 1]).then_inc(uv_taken, 1)
                act.wait_ge(uv_taken, 2 * (t + 1))
                link(nc.scalar.activation(nm[:r, t:t + 1], sv[:r, t:t + 1], ACT.Copy, scale=-1.0 / DA))
                link(nc.scalar.activation(junk[:r, :], K.M[:r, t, DA:D], ACT.Square, bias=nm[:r, t:t + 1],
                                          accum_out=sq[:r, t:t + 1]))
                nc.scalar.activation(sd[:r, t:t + 1], sq[:r, t:t + 1], ACT.Sqrt, bias=K.eps[:r, 0:1],
                                     scale=1.0 / DA).then_inc(sd_ready, 1)
            act.wait_ge(rest_taken, 2 * TILES)
            nc.scalar.activation(K.GT[:, 0:8, :], K.GT[:, 0:8, :], ACT.Sigmoid).then_inc(sig, 1)
            nc.scalar.activation(K.GT[:SROWS, 8, :], K.GT[:SROWS, 8, :], ACT.Sigmoid).then_inc(sig, 1)

        @block.vector
        def _(dve):
            link = Chain(dve, v_chain)
            dve.wait_ge(gd, 16 * len(gating_operands(K, I)))
            nc.vector.tensor_tensor(ws, ws, caus.unsqueeze(1).to_broadcast([P, AG, P]), ALU.mult).then_inc(masked, 1)
            nc.vector.tensor_tensor(wss[:SROWS], wss[:SROWS], causs[:SROWS].unsqueeze(1).to_broadcast([SROWS, AG, SROWS]),
                                    ALU.mult).then_inc(masked, 1)

            def gated(t):
                r = rows_of(t)
                b = bs if r == P else bss
                dve.wait_ge(mixed, t + 1)
                for g in range(AG):
                    u = K.M[:r, t, g * AGD:(g + 1) * AGD]
                    last = nc.vector.scalar_tensor_tensor(u, K.bank[6 + t % 2][:r, g * AGD:(g + 1) * AGD],
                                                          b[:r, g:g + 1], u, ALU.add, ALU.mult)
                last.then_inc(mixed_used, 1)

            for t in range(TILES):
                r = rows_of(t)
                bank = K.bank[3 * (t % 2) + 2]
                v = K.M[:r, t, DA:D]
                dve.wait_ge(p_done, t + 1)
                nc.vector.tensor_copy(K.VT[:r, t, :], bank[:r, 0:2 * KV]).then_inc(rest_taken, 1)
                nc.vector.tensor_copy(K.GT[:r, t, :], bank[:r, 2 * KV:2 * KV + 3 * H]).then_inc(rest_taken, 1)
                dve.wait_ge(sd_ready, t + 1)
                link(nc.vector.reciprocal(rsd[:r, t:t + 1], sd[:r, t:t + 1]))
                link(nc.vector.tensor_scalar(v, v, nm[:r, t:t + 1], rsd[:r, t:t + 1], ALU.add, ALU.mult))
                link(nc.vector.tensor_tensor(v, v, lng[:r, :], ALU.mult))
                nc.vector.tensor_tensor(v, v, lnb[:r, :], ALU.add).then_inc(v_ready, 1)
                if t >= 1:
                    gated(t - 1)
            gated(TILES - 1)
            dve.wait_ge(sig, 1)
            gt = K.GT[:, 0:8, :].rearrange("p t (h b) -> p h t b", b=3)
            for b in range(3):
                last = nc.vector.tensor_copy(K.GS[:, :, :, b], gt[:, :, :, b])
            link(last)
            link(nc.vector.tensor_scalar(K.GS[:, :, 0, 0], K.GS[:, :, 0, 0], valid, None, ALU.mult))


def compress_phase(nc, K, I):
    S = K.sem
    ar = K.big[:, O_HT:O_M]
    pages = [slot.rearrange("p (g t) -> p g t", g=2) for slot in K.slot]
    w1 = [ar[:, 8192 + 2048 * v:8192 + 2048 * (v + 1)].rearrange("p (q h) -> p q h", h=P) for v in range(2)]
    dein = [ar[:, 12288 + 1024 * v:12288 + 1024 * (v + 1)].rearrange("p (r t) -> p r t", r=2) for v in range(2)]
    own = [ar[:, 14336 + 1024 * v:14336 + 1024 * (v + 1)].rearrange("p (g t) -> p g t", g=2) for v in range(2)]
    hid = [ar[:, 16384 + 512 * u:16384 + 512 * (u + 1)] for u in range(2)]
    w2 = [ar[:, 17408 + 64 * v:17408 + 64 * (v + 1)] for v in range(2)]
    pe_t = [ar[:, 17536 + 16 * v:17536 + 16 * (v + 1)] for v in range(2)]
    b1, b2k, hb = ar[:, 17568:17570], ar[:, 17570:17571], ar[:, 17571:17573]
    b2v = ar[:, 17600:17728]
    came_w, came_w2, came_own, dei = S("cmp_w_came"), S("cmp_small_came"), S("cmp_own_came"), S("cmp_split")
    first, hidden, second, out, biased = S("cmp_first"), S("cmp_hidden"), S("cmp_second"), S("cmp_out"), S("cmp_bias")
    pe_w1 = S("cmp_pe_product")
    rounds = [(0, None), (1, None), (0, 0), (0, 1), (1, 0), (1, 1)]
    small = [(w2[v], I["w_cmp2"][v]) for v in range(2)] + [(pe_t[v], I["pe_cmp"][v]) for v in range(2)] + \
            [(b1, I["b_cmp1"]), (b2k, I["b2k"]), (b2v, I["b2v"].to_broadcast([P, P]))]

    with nc.Block() as block:
        @block.sync
        def _(sp):
            for v in range(2):
                sp.dma_start(w1[v], I["w_cmp1"][v]).then_inc(came_w, 16)
            for to, of in small:
                sp.dma_start(to, of).then_inc(came_w2, 16)
            sp.wait_ge(dei, 2)
            for v in range(2):
                for g in range(2):
                    for r in range(2):
                        sp.dma_start(own[v][64 * r:64 * r + 64, g, :], dein[v][64 * g:64 * g + 64, r, :]).then_inc(came_own, 16)
            for half in range(2):
                gather_cmp(sp, I, K, 1, half, 2 + half)
            sample_windows(sp, K, I, 0)
            sp.wait_ge(first, 3)
            gather_sel(sp, I, K, "pool_sel_k", 0, 0)
            sp.wait_ge(first, 4)
            gather_sel(sp, I, K, "pool_sel_v", 0, 1)
            sp.wait_ge(came_own, 128)

        @block.vector
        def _(dve):
            for v in range(2):
                nc.vector.tensor_copy(dein[v][:, :, :], K.FM[:, 4 + v, 0:SEQ].rearrange("p (t r) -> p r t", r=2)).then_inc(dei, 1)
            dve.wait_ge(came_w2, 16 * len(small))
            for v in range(2):
                dve.wait_ge(pe_w1, v + 1)
                nc.vector.tensor_tensor(hb[:, v:v + 1], K.bank[6][:, v:v + 1], b1[:, v:v + 1], ALU.add).then_inc(biased, 1)
            for n, (v, half) in enumerate(rounds):
                dve.wait_ge(second, n + 1)
                bank = K.bank[2 + n % 2]
                if v == 0 and half is None:
                    last = nc.vector.tensor_scalar(K.KCP[:, :], bank[:, 0:NCMP], b2k, None, ALU.add)
                elif v == 0:
                    last = nc.vector.tensor_scalar(K.KCS[:, 4 * half:4 * half + 4, :],
                                                   bank[:, 0:4 * NCMP].rearrange("p (n c) -> p n c", n=4), b2k, None, ALU.add)
                elif half is None:
                    last = nc.vector.tensor_tensor(K.VCP[:NCMP, :], bank[:NCMP, 0:P], b2v[:NCMP, :], ALU.add)
                else:
                    last = nc.vector.tensor_tensor(K.VCS[:NCMP, 4 * half:4 * half + 4, :],
                                                   bank[:NCMP, :].rearrange("p (n c) -> p n c", n=4),
                                                   b2v[:NCMP, :].unsqueeze(1).to_broadcast([NCMP, 4, P]), ALU.add)
                last.then_inc(out, 1)

        @block.scalar
        def _(act):
            act.wait_ge(biased, 2)
            for n, (v, half) in enumerate(rounds):
                m = 2 * NCMP if half is None else 8 * NCMP
                act.wait_ge(first, n + 1)
                if n >= 2:
                    act.wait_ge(second, n - 1)
                nc.scalar.activation(hid[n % 2][:, 0:m], K.bank[n % 2][:, 0:m], ACT.Gelu_apprx_tanh,
                                     bias=hb[:, v:v + 1]).then_inc(hidden, 1)

        @block.tensor
        def _(pe):
            pe.wait_ge(came_w, 32)
            pe.wait_ge(came_w2, 16 * len(small))
            for v in range(2):
                for q in range(16):
                    last = nc.tensor.matmul(K.bank[6][:, v:v + 1], w1[v][:, q, :], pe_t[v][:, q:q + 1],
                                            start=q == 0, stop=q == 15)
                last.then_inc(pe_w1, 1)
                pe.wait_ge(biased, v + 1)

            def hidden_rows(n):
                v, half = rounds[n]
                if half is None:
                    pe.wait_ge(came_own, 128)
                    src, m = own[v], 2 * NCMP
                else:
                    pe.wait_ge(K.slot_came[n - 2], SLOT_PAGES)
                    src, m = pages[n - 2], 8 * NCMP
                if n >= 2:
                    pe.wait_ge(hidden, n - 1)
                for q in range(16):
                    if half is None:
                        rhs = src[:, :, q:q + 8 * NCMP - 7:8]
                    else:
                        rhs = src.rearrange("p g (n t) -> p g n t", n=4)[:, :, :, q:q + 8 * NCMP - 7:8]
                    last = nc.tensor.matmul(K.bank[n % 2][:, 0:m], w1[v][:, q, :], rhs, start=q == 0, stop=q == 15)
                last.then_inc(first, 1)

            def rows(n):
                v, half = rounds[n]
                pe.wait_ge(hidden, n + 1)
                if n >= 2:
                    pe.wait_ge(out, n - 1)
                seqs = 1 if half is None else 4
                bank = K.bank[2 + n % 2]
                for g in range(2):
                    if v == 0:
                        last = nc.tensor.matmul(bank[64 * g:64 * g + 64, 0:seqs * NCMP], w2[0],
                                                hid[n % 2][:, g * seqs * NCMP:(g + 1) * seqs * NCMP], start=True, stop=True)
                    else:
                        for s in range(seqs):
                            at = (g * seqs + s) * NCMP
                            last = nc.tensor.matmul(bank[:NCMP, s * P + 64 * g:s * P + 64 * g + 64],
                                                    hid[n % 2][:, at:at + NCMP], w2[1], start=True, stop=True)
                last.then_inc(second, 1)

            for n in range(len(rounds)):
                hidden_rows(n)
                if n >= 1:
                    rows(n - 1)
            rows(len(rounds) - 1)


def sample_windows(sp, K, I, half):
    kw, vw = K.windows[half]
    sp.dma_start(kw, I["win_kt"][4 * half:4 * half + 4].rearrange("n p t -> p n t")).then_inc(K.windows_came[half], 16)
    for n in range(4):
        sp.dma_start(vw[:, n].rearrange("p (b c) -> p b c", b=4),
                     I["win_v"][4 * half + n].rearrange("(b p) c -> p b c", p=P)).then_inc(K.windows_came[half], 16)


def sample_attention(nc, K, I):
    S = K.sem
    ar = K.big[:, O_HT:O_M]
    SC = ar[:, 12288:12288 + 1664]
    SB = ar[:, 13952:13952 + 1664]
    PT = ar[:, 15616:15616 + 15 * P].rearrange("p (b n) -> p b n", b=15)
    a = 15616 + 15 * P
    tabq, dq, gm = ar[:, a:a + 128], ar[:, a + 128:a + 256], ar[:, a + 256:a + 384]
    mn = ar[:, a + 384:a + 512].rearrange("p (h n) -> p h n", h=2)
    qbd = ar[:, a + 512:a + 768].rearrange("p (n r) -> p n r", n=NS)
    OS = ar[:, a + 768:a + 896]
    ovl, mw, t4 = ar[:, a + 896:a + 913], ar[:, a + 914:a + 918], ar[:, a + 920:a + 928]
    gr = ar[:, a + 928:a + 934].rearrange("p (h b) -> p h b", h=2)
    imp, eq, jj = ar[:, a + 940:a + 957], ar[:, a + 960:a + 974], ar[:, a + 974:a + 988]
    st = ar[:, a + 990:a + 1010]
    PC = ar[:, a + 1020:a + 1020 + 63]
    assert a + 1083 <= O_M - O_HT
    c_sel, c_new, c_win, c_cmp, c_end = 0, 1024, 1088, 1600, 1663
    oh = SC
    came_c, zeroed, prep = S("sa_small_came"), S("sa_zeroed"), S("sa_prep")
    pb, bias_done, scores, taken = S("sa_bias_product"), S("sa_bias"), S("sa_scores"), S("sa_scores_taken")
    vch, ach, impt, impu, nmr, exps = S("sa_dve"), S("sa_act"), S("sa_pe_imp"), S("sa_imp_taken"), S("sa_max"), S("sa_exp")
    pready, turned, ptaken, pv, otaken, oscr = S("sa_probs"), S("sa_turned"), S("sa_pt"), S("sa_pv"), S("sa_o"), S("sa_o_dram")
    back = S("sa_o_back")
    consts = [(oh[:, 0:c_end], I["oh_s"]), (dq, I["dq"]), (gm, I["gmat"]), (mn, I["mask_new"]), (mw, I["mask_win"]),
              (ovl[:NCMP], I["overlap"]), (jj, I["jidx"])] + \
             [(t4[32 * q:32 * q + 32, :], I["rel_bias"]) for q in range(4)]
    blocks = [(i * P, P) for i in range(8)] + [(c_new, 32), (c_new + 32, 32)] + \
             [(c_win + i * P, P) for i in range(4)] + [(c_cmp, NCMP)]

    with nc.Block() as block:
        @block.sync
        def _(sp):
            for to, of in consts:
                sp.dma_start(to, of).then_inc(came_c, 16)
            for half in range(2):
                for n in range(4):
                    of = bass.AP(K.gates_dram.tensor, (half * 4 + n) * TS * 3 * H, [[3, H], [3 * H, TS], [1, 3]])
                    sp.dma_start(gr[32 * n:32 * n + 32, half, :], of).then_inc(came_c, 16)
            sample_windows(sp, K, I, 1)
            gather_sel(sp, I, K, "pool_sel_k", 1, 2)
            gather_sel(sp, I, K, "pool_sel_v", 1, 3)
            for half in range(2):
                sp.wait_ge(otaken, half + 1)
                for n in range(4):
                    for g in range(2):
                        to = bass.AP(K.o_dram.tensor, (half * 4 + n) * TS * DA + g * 256, [[HD, HPG], [DA, TS], [1, HD]])
                        sp.dma_start(to, OS[32 * n + 16 * g:32 * n + 16 * g + 16, 64 * g:64 * g + 64]).then_inc(oscr, 16)
            sp.wait_ge(oscr, 256)
            sp.dma_start(K.M[:SROWS, TILES - 1, DA:D], K.o_dram).then_inc(back, 16)
            sp.wait_ge(back, 16)

        @block.gpsimd
        def _(pool):
            nc.gpsimd.memset(qbd, 0.0).then_inc(zeroed, 1)

        @block.tensor
        def _(pe):
            pe.wait_ge(prep, 1)
            for i, (x, y) in enumerate([(0, 512), (512, 1024), (1024, 1536), (1536, c_end)]):
                last = nc.tensor.matmul(K.bank[i][:, 0:y - x], tabq, oh[:, x:y], start=True, stop=True)
            last.then_inc(pb, 1)
            pe.wait_ge(bias_done, 1)
            pe.wait_ge(prep, 3)
            for half in range(2):
                KS, VS = K.slot[2 * half], K.slot[2 * half + 1]
                KW, VW = K.windows[half]
                pe.wait_ge(K.slot_came[2 * half], 2 * SLOT_PAGES)
                pe.wait_ge(K.windows_came[half], 80)
                if half:
                    pe.wait_ge(otaken, half)
                for n in range(4):
                    s = 4 * half + n
                    rows = slice(32 * n, 32 * n + 32)
                    for i in range(2):
                        nc.tensor.matmul(K.bank[i][rows, :], qbd[:, s, :], KS[:, n * 1024 + 512 * i:n * 1024 + 512 * i + 512], start=True, stop=True)
                    nc.tensor.matmul(K.bank[2][rows, 0:32], qbd[:, s, :], K.FM[:, 6, SEQ:T], start=True, stop=True)
                    nc.tensor.matmul(K.bank[2][rows, 32:64], qbd[:, s, :], K.FM[:, 7, SEQ:T], start=True, stop=True)
                    nc.tensor.matmul(K.bank[3][rows, :], qbd[:, s, :], KW[:, n], start=True, stop=True)
                    last = nc.tensor.matmul(K.bank[2][rows, 64:64 + NCMP], qbd[:, s, :], K.KCS[:, s, :], start=True, stop=True)
                last.then_inc(scores, 1)
                pe.wait_ge(impu, 3 * half + 1)
                nc.tensor.transpose(K.bank[4][:NCMP, 0:P], PC, K.ident[:, :]).then_inc(impt, 1)
                pe.wait_ge(impu, 3 * half + 2)
                nc.tensor.matmul(K.bank[4][:, 128:128 + NSEL], PT[:NCMP, 0, :], ovl[:NCMP, :], start=True, stop=True).then_inc(impt, 1)
                pe.wait_ge(impu, 3 * half + 3)
                nc.tensor.matmul(K.bank[4][:, 160:160 + NSEL], gm, imp, start=True, stop=True).then_inc(impt, 1)
                pe.wait_ge(pready, half + 1)
                for i, (x, w) in enumerate(blocks):
                    b = i // 4
                    last = nc.tensor.transpose(K.bank[4 + b][:w, (i % 4) * P:(i % 4 + 1) * P], SC[:, x:x + w], K.ident[:, :])
                last.then_inc(turned, 1)
                pe.wait_ge(ptaken, half + 1)
                pe.wait_ge(K.slot_came[2 * half + 1], 2 * SLOT_PAGES)
                for n in range(4):
                    s = 4 * half + n
                    rows = slice(32 * n, 32 * n + 32)
                    for i, (x, w) in enumerate(blocks):
                        if i < 8:
                            v = VS[:, (n * 8 + i) * P:(n * 8 + i + 1) * P]
                        elif i < 10:
                            v = K.VT[:SROWS, TILES - 1, (i - 8) * KV:(i - 7) * KV]
                        elif i < 14:
                            v = VW[:, n, (i - 10) * P:(i - 9) * P]
                        else:
                            v = K.VCS[:NCMP, s, :]
                        last = nc.tensor.matmul(K.bank[0][rows, 0:P], PT[:w, i, rows], v, start=i == 0, stop=i == 14)
                last.then_inc(pv, 1)

        @block.vector
        def _(dve):
            link = Chain(dve, vch)
            dve.wait_ge(came_c, 16 * (len(consts) + 8))
            nc.vector.tensor_tensor(tabq.rearrange("p (n h q) -> p n h q", n=4, h=H),
                                    t4.unsqueeze(1).unsqueeze(3).to_broadcast([P, 4, H, 4]),
                                    dq.rearrange("p (n h q) -> p n h q", n=4, h=H), ALU.mult).then_inc(prep, 1)
            dve.wait_ge(zeroed, 1)
            for g in range(2):
                nc.vector.tensor_scalar(qbd[64 * g:64 * g + 64, :, 16 * g:16 * g + 16].rearrange("p n (h q) -> p n h q", h=4),
                                        K.FM[64 * g:64 * g + 64, 0:4, SEQ:T].rearrange("p h (n q) -> p n h q", n=NS),
                                        HD ** -0.5, None, ALU.mult).then_inc(prep, 1)
            dve.wait_ge(pb, 1)
            for i, (x, y) in enumerate([(0, 512), (512, 1024), (1024, 1536), (1536, c_end)]):
                last = nc.vector.tensor_copy(SB[:, x:y], K.bank[i][:, 0:y - x])
            link(last)
            link(nc.vector.tensor_tensor(SB[:, c_win:c_win + 4], SB[:, c_win:c_win + 4], mw, ALU.add))
            dve.sem_inc(bias_done, 1)
            for half in range(2):
                dve.wait_ge(scores, half + 1)
                if half:
                    dve.wait_ge(turned, half)
                nc.vector.tensor_tensor(SC[:, c_cmp:c_end], K.bank[2][:, 64:64 + NCMP], SB[:, c_cmp:c_end], ALU.add)
                nc.vector.tensor_tensor(SC[:, 0:512], K.bank[0][:, :], SB[:, 0:512], ALU.add)
                nc.vector.tensor_tensor(SC[:, 512:1024], K.bank[1][:, :], SB[:, 512:1024], ALU.add)
                nc.vector.tensor_tensor(SC[:, c_win:c_win + 512], K.bank[3][:, :], SB[:, c_win:c_win + 512], ALU.add)
                link(nc.vector.tensor_tensor(SC[:, c_new:c_new + 64], K.bank[2][:, 0:64], SB[:, c_new:c_new + 64], ALU.add))
                link(nc.vector.tensor_tensor(SC[:, c_new:c_new + 64], SC[:, c_new:c_new + 64], mn[:, half, :], ALU.add))
                link(nc.vector.tensor_reduce(st[:, 0:1], SC[:, c_cmp:c_end], AX.X, ALU.max, negate=True))
                dve.sem_inc(nmr, 1)
                dve.wait_ge(exps, 3 * half + 1)
                link(nc.vector.reciprocal(st[:, 4:5], st[:, 3:4]))
                link(nc.vector.tensor_scalar(PC, SC[:, c_cmp:c_end], st[:, 4:5], None, ALU.mult))
                dve.sem_inc(impu, 1)
                dve.wait_ge(impt, 3 * half + 1)
                link(nc.vector.tensor_copy(PT[:NCMP, 0, :], K.bank[4][:NCMP, 0:P]))
                dve.sem_inc(impu, 1)
                dve.wait_ge(impt, 3 * half + 2)
                link(nc.vector.tensor_copy(imp, K.bank[4][:, 128:128 + NSEL]))
                dve.sem_inc(impu, 1)
                dve.wait_ge(impt, 3 * half + 3)
                cand = K.bank[4][:, 161:175]
                link(nc.vector.tensor_reduce(st[:, 5:6], cand, AX.X, ALU.min))
                link(nc.vector.scalar_tensor_tensor(eq, cand, st[:, 5:6], jj, ALU.is_equal, ALU.mult))
                link(nc.vector.tensor_reduce(st[:, 6:7], eq, AX.X, ALU.max))
                link(nc.vector.tensor_scalar(eq, jj, st[:, 6:7], NEG, ALU.is_equal, ALU.mult))
                part = SC[:, SELB:15 * SELB].rearrange("p (b k) -> p b k", b=14)
                link(nc.vector.tensor_tensor(part, part, eq.unsqueeze(2).to_broadcast([P, 14, SELB]), ALU.add))
                nc.vector.tensor_reduce(st[:, 1:2], SC[:, 0:c_new + 32], AX.X, ALU.max, negate=True)
                link(nc.vector.tensor_reduce(st[:, 2:3], SC[:, c_new + 32:c_cmp], AX.X, ALU.max, negate=True))
                dve.sem_inc(nmr, 1)
                dve.wait_ge(exps, 3 * half + 3)
                nc.vector.tensor_copy(st[:, 8:9], st[:, 3:4])
                link(nc.vector.tensor_copy(st[:, 9:11], st[:, 11:13]))
                link(nc.vector.reciprocal(st[:, 14:17], st[:, 8:11]))
                link(nc.vector.tensor_tensor(st[:, 14:17], st[:, 14:17], gr[:, half, :], ALU.mult))
                nc.vector.tensor_scalar(SC[:, 0:c_new + 32], SC[:, 0:c_new + 32], st[:, 15:16], None, ALU.mult)
                nc.vector.tensor_scalar(SC[:, c_new + 32:c_cmp], SC[:, c_new + 32:c_cmp], st[:, 16:17], None, ALU.mult)
                nc.vector.tensor_scalar(SC[:, c_cmp:c_end], SC[:, c_cmp:c_end], st[:, 14:15], None, ALU.mult).then_inc(pready, 1)
                dve.wait_ge(turned, half + 1)
                for b in range(4):
                    if b < 2:
                        last = nc.vector.tensor_copy(PT[:, 4 * b:4 * b + 4, :], K.bank[4 + b][:, :].rearrange("p (b n) -> p b n", b=4))
                    elif b == 2:
                        nc.vector.tensor_copy(PT[:32, 8:10, :], K.bank[6][:32, 0:256].rearrange("p (b n) -> p b n", b=2))
                        last = nc.vector.tensor_copy(PT[:, 10:12, :], K.bank[6][:, 256:512].rearrange("p (b n) -> p b n", b=2))
                    else:
                        nc.vector.tensor_copy(PT[:, 12:14, :], K.bank[7][:, 0:256].rearrange("p (b n) -> p b n", b=2))
                        last = nc.vector.tensor_copy(PT[:NCMP, 14, :], K.bank[7][:NCMP, 256:384])
                last.then_inc(ptaken, 1)
                dve.wait_ge(pv, half + 1)
                if half:
                    dve.wait_ge(oscr, 128)
                nc.vector.tensor_copy(OS, K.bank[0][:, 0:P]).then_inc(otaken, 1)

        @block.scalar
        def _(act):
            for half in range(2):
                act.wait_ge(nmr, 2 * half + 1)
                nc.scalar.activation(SC[:, c_cmp:c_end], SC[:, c_cmp:c_end], ACT.Exp, bias=st[:, 0:1],
                                     accum_out=st[:, 3:4]).then_inc(exps, 1)
                act.wait_ge(nmr, 2 * half + 2)
                nc.scalar.activation(SC[:, 0:c_new + 32], SC[:, 0:c_new + 32], ACT.Exp, bias=st[:, 1:2],
                                     accum_out=st[:, 11:12]).then_inc(exps, 1)
                nc.scalar.activation(SC[:, c_new + 32:c_cmp], SC[:, c_new + 32:c_cmp], ACT.Exp, bias=st[:, 2:3],
                                     accum_out=st[:, 12:13]).then_inc(exps, 1)


def prompt_attention(nc, K, I):
    S = K.sem
    ar = K.big[:, O_HT:O_M]
    strips = [ar[:, 2560 * g:2560 * (g + 1)] for g in range(2)]
    qz = [ar[:, 5120 + 1024 * g:5120 + 1024 * (g + 1)] for g in range(2)]
    sc = [ar[:, 7168 + 1728 * b:7168 + 1728 * (b + 1)] for b in range(2)]
    pt = [ar[:, 10624 + 1792 * b:10624 + 1792 * (b + 1)].rearrange("p (b n) -> p b n", b=14) for b in range(2)]
    gh = [ar[:, 14208 + 24 * g:14208 + 24 * (g + 1)].rearrange("p (t b) -> p t b", b=3) for g in range(2)]
    sta = [ar[:, 14300 + 16 * b:14300 + 16 * (b + 1)] for b in range(2)]
    strip_came = [S(f"pa_strip{g}") for g in range(2)]
    zeroed, steps = S("pa_zeroed"), [S("pa_dve_steps"), S("pa_pe_steps")]
    q_ready = [S(f"pa_q{g}") for g in range(2)]
    scores, s_taken, negmax, exps = S("pa_scores"), S("pa_scores_taken"), S("pa_negmax"), S("pa_exp")
    probs, pv, o_taken, vch = S("pa_probs"), S("pa_pv"), S("pa_o_taken"), S("pa_dve")
    TB = 3
    turned = [S(f"pa_turned{b}") for b in range(TB)]
    t_taken = [S(f"pa_turned_taken{b}") for b in range(TB)]
    U = 16
    CHAIN = 2 * U + 2

    def blocks(i):
        lo = max(0, i - 4)
        return [(b * P, P, 0, b) for b in range(i + 1)] + \
               [(1024 + (b - lo) * P, P, 1, b) for b in range(lo, i + 1)] + [(1664, NCMP, 2, 0)]

    groups, per = [], [0] * TB
    for u in range(U):
        bl = blocks(u % 8)
        mine = []
        for n, x in enumerate(range(0, len(bl), 4)):
            per[n % TB] += 1
            mine.append((n % TB, per[n % TB], bl[x:x + 4], x))
        groups.append(mine)

    with nc.Block() as block:
        @block.sync
        def _(sp):
            for j in range(4):
                for g in range(2):
                    h = j + 4 * g
                    if j:
                        sp.wait_ge(s_taken, (j - 1) * U + 8 * g + 9)
                    base = h * (VECS + VECW)
                    sp.dma_start(strips[g][:, 0:STRS], bass.AP(K.vec_dram.tensor, base, [[1, P], [1, STRS]])).then_inc(strip_came[g], 16)
                    sp.dma_start(strips[g][:, STRS:], bass.AP(K.vec_dram.tensor, base + VECS, [[1, P], [1, STRW]])).then_inc(strip_came[g], 16)
                if j == 0:
                    for to, of in x_loads(K, I):
                        sp.dma_start(to, of).then_inc(K.x_came, 16)

        @block.gpsimd
        def _(pool):
            nc.gpsimd.memset(qz[0][64:128, :], 0.0).then_inc(zeroed, 1)
            nc.gpsimd.memset(qz[1][0:64, :], 0.0).then_inc(zeroed, 1)

        @block.tensor
        def _(pe):
            pe.sem_inc(pv, 2)
            pe.wait_ge(zeroed, 2)

            def score(j, u):
                g, i = u // 8, u % 8
                if i == 0:
                    pe.wait_ge(q_ready[g], j + 1)
                pe.wait_ge(s_taken, j * U + u + 1)
                q = qz[g][:, i * P:(i + 1) * P]
                w = (i + 1) * P
                for x in range(0, w, 512):
                    nc.tensor.matmul(K.ps4[:, x:min(x + 512, w)], q, K.FM[:, 6, x:min(x + 512, w)], start=True, stop=True)
                lo = max(0, i - 4) * P
                ww = w - lo
                for x in range(0, ww, 512):
                    y = min(x + 512, ww)
                    nc.tensor.matmul(K.ps4[:, 1024 + x:1024 + y], q, K.FM[:, 7, lo + x:lo + y], start=True, stop=True)
                nc.tensor.matmul(K.ps4[:, 1664:1664 + NCMP], q, K.KCP[:, :], start=True, stop=True).then_inc(scores, 1)

            def turn(j, u, group):
                b, cnt, bl, _ = group
                pe.wait_ge(t_taken[b], j * per[b] + cnt)
                if bl[0][1] < P:
                    pe.sem_inc(steps[1], 1)
                for x, (col, w, _, _) in enumerate(bl):
                    last = nc.tensor.transpose(K.bank[4 + b][:w, x * P:(x + 1) * P], sc[u % 2][:, col:col + w], K.ident[:, :])
                last.then_inc(turned[b], 1)

            def multiply(j, u, group):
                b, cnt, bl, first = group
                end = groups[u][-1] is group
                pe.wait_ge(t_taken[b], j * per[b] + cnt + 1)
                for x, (_, w, kind, t) in enumerate(bl):
                    v = K.VCP[:NCMP, :] if kind == 2 else K.VT[:, t, kind * KV:(kind + 1) * KV]
                    last = nc.tensor.matmul(K.bank[7][:, 0:P], pt[u % 2][:w, first + x, :], v,
                                            start=first + x == 0, stop=end and x == len(bl) - 1)
                if end:
                    last.then_inc(pv, 1)

            with pe.Fori(0, 4) as j:
                score(j, 0)
                score(j, 1)
                for u in range(U):
                    pe.wait_ge(probs, j * U + u + 1)
                    g = groups[u]
                    for group in g[:TB]:
                        turn(j, u, group)
                    pe.wait_ge(o_taken, j * U + u + 1)
                    for n, group in enumerate(g):
                        multiply(j, u, group)
                        if n + TB < len(g):
                            turn(j, u, g[n + TB])
                    if u + 2 < U:
                        score(j, u + 2)

        @block.vector
        def _(dve):
            dve.sem_inc(s_taken, 1)
            count = [0]

            def link(ins, j):
                count[0] += 1
                ins.then_inc(vch, 1)
                dve.wait_ge(vch, j * CHAIN + count[0])

            def add_bias(j, u):
                g, i = u // 8, u % 8
                s, mx = sc[u % 2], sta[u % 2]
                if i == 0:
                    dve.wait_ge(strip_came[g], j * 32 + 32)
                dve.wait_ge(scores, j * U + u + 1)
                dve.wait_ge(pv, j * U + u + 1)
                dve.sem_inc(steps[0], 1)
                w = (i + 1) * P
                ww = min(i + 1, 5) * P
                at = 992 + P * i
                nc.vector.tensor_tensor_reduce(out=s[:, 0:w], in0=K.ps4[:, 0:w], in1=strips[g][:, 895 + w:895:-1], scale=1.0,
                                               scalar=-3e38, op0=ALU.add, op1=ALU.max, accum_out=mx[:, 1:2])
                nc.vector.tensor_tensor_reduce(out=s[:, 1024:1024 + ww], in0=K.ps4[:, 1024:1024 + ww],
                                               in1=strips[g][:, STRS + ww - 1:STRS - 1:-1], scale=1.0,
                                               scalar=-3e38, op0=ALU.add, op1=ALU.max, accum_out=mx[:, 2:3])
                nc.vector.tensor_tensor_reduce(out=s[:, 1664:1664 + NCMP], in0=K.ps4[:, 1664:1664 + NCMP],
                                               in1=strips[g][:, at:at - 16 * NCMP + 15:-16] if i else strips[g][:, at::-16], scale=1.0,
                                               scalar=-3e38, op0=ALU.add, op1=ALU.max, accum_out=mx[:, 0:1]).then_inc(s_taken, 1)
                dve.wait_ge(s_taken, j * U + u + 2)
                nc.vector.tensor_scalar(mx[:, 4:7], mx[:, 0:3], -1.0, None, ALU.mult).then_inc(negmax, 1)

            def gate(j, u):
                g, i = u // 8, u % 8
                s, m = sc[u % 2], sta[u % 2]
                w = (i + 1) * P
                ww = min(i + 1, 5) * P
                dve.wait_ge(exps, j * 3 * U + 3 * u + 3)
                link(nc.vector.reciprocal(m[:, 12:15], m[:, 8:11]), j)
                link(nc.vector.tensor_tensor(m[:, 12:15], m[:, 12:15], gh[g][:, i, :], ALU.mult), j)
                nc.vector.tensor_scalar(s[:, 0:w], s[:, 0:w], m[:, 13:14], None, ALU.mult)
                nc.vector.tensor_scalar(s[:, 1024:1024 + ww], s[:, 1024:1024 + ww], m[:, 14:15], None, ALU.mult)
                nc.vector.tensor_scalar(s[:, 1664:1664 + NCMP], s[:, 1664:1664 + NCMP], m[:, 12:13], None, ALU.mult).then_inc(probs, 1)

            with dve.Fori(0, 4) as j:
                count[0] = 0
                for g in range(2):
                    src = K.FM[64 * g:64 * g + 64, bass.ds(j, 1), 0:SEQ].rearrange("p a n -> p (a n)")
                    nc.vector.tensor_scalar(qz[g][64 * g:64 * g + 64, :], src, HD ** -0.5, None, ALU.mult).then_inc(q_ready[g], 1)
                    link(nc.vector.tensor_copy(gh[g], K.GS[:, bass.ds(j + 4 * g, 1), :, :].rearrange("p a t b -> p (a t) b")), j)
                add_bias(j, 0)
                for u in range(U):
                    gate(j, u)
                    if u + 1 < U:
                        add_bias(j, u + 1)

        @block.scalar
        def _(act):
            for b in range(TB):
                act.sem_inc(t_taken[b], 1)
            act.sem_inc(o_taken, 1)

            def exp(j, u):
                i = u % 8
                s, m = sc[u % 2], sta[u % 2]
                w = (i + 1) * P
                ww = min(i + 1, 5) * P
                act.wait_ge(negmax, j * U + u + 1)
                for b, x, y in ((1, 0, w), (2, 1024, 1024 + ww), (0, 1664, 1664 + NCMP)):
                    nc.scalar.activation(s[:, x:y], s[:, x:y], ACT.Exp, bias=m[:, 4 + b:5 + b],
                                         accum_out=m[:, 8 + b:9 + b]).then_inc(exps, 1)

            with act.Fori(0, 4) as j:
                exp(j, 0)
                for u in range(U):
                    g, i = u // 8, u % 8
                    act.wait_ge(pv, j * U + u + 1)
                    for b, cnt, bl, x in groups[u]:
                        act.wait_ge(turned[b], j * per[b] + cnt)
                        full = [y for y in bl if y[1] == P]
                        if full:
                            last = nc.scalar.copy(pt[u % 2][:, x:x + len(full), :],
                                                  K.bank[4 + b][:, 0:len(full) * P].rearrange("p (b n) -> p b n", n=P))
                        if len(full) < len(bl):
                            last = nc.scalar.copy(pt[u % 2][:NCMP, x + len(full), :],
                                                  K.bank[4 + b][:NCMP, len(full) * P:(len(full) + 1) * P])
                        last.then_inc(t_taken[b], 1)
                    if u + 1 < U:
                        exp(j, u + 1)
                    act.wait_ge(pv, j * U + u + 3)
                    dst = K.M[:, i, bass.ds(j * HD + (DA + 4 * g * HD), HD)]
                    nc.scalar.activation(dst, K.bank[7][:, 64 * g:64 * g + 64], ACT.Copy).then_inc(o_taken, 1)


def bias_rows(nc, K, I):
    S = K.sem
    came, rows, out, product, set_ = S("bias_came"), S("bias_rows"), S("bias_dram"), S("bias_product"), S("bias_table")
    L = VECS + VECW
    oh = K.big[:BUCKETS + 1, O_M:O_M + L]
    vec = K.big[:H, O_M + L:O_M + 2 * L]
    cuts = [(x, min(x + 512, L)) for x in range(0, L, 512)]

    def sync(sp):
        sp.dma_start(oh, I["oh_v"]).then_inc(came, 16)
        sp.wait_ge(set_, 1)
        sp.dma_start(K.table[:BUCKETS, :], I["rel_bias"]).then_inc(came, 16)
        sp.dma_start(K.page_table[:, :], I["page_table"]).then_inc(came, 16)
        w = K.big[:, O_W:O_W + KD * TMW].rearrange("p (k n) -> p k n", k=KD)
        for k in range(KD):
            sp.dma_start(w[:, k, :], I["w_tm"][k]).then_inc(K.wtm_sem, 16)
        sp.wait_ge(rows, len(cuts))
        sp.dma_start(K.vec_dram, vec).then_inc(out, 16)
        sp.wait_ge(out, 16)
        sp.wait_ge(came, 48)

    def gpsimd(pool):
        nc.gpsimd.memset(K.table[:, :], NEG).then_inc(set_, 1)

    def tensor(pe):
        pe.wait_ge(came, 48)
        for n, (x, y) in enumerate(cuts):
            if n >= 2:
                pe.wait_ge(rows, n - 1)
            nc.tensor.matmul(K.bank[4 + n % 2][:H, 0:y - x], K.table[:, :], oh[:, x:y], start=True, stop=True).then_inc(product, 1)

    def scalar(act):
        for n, (x, y) in enumerate(cuts):
            act.wait_ge(product, n + 1)
            nc.scalar.activation(vec[:, x:y], K.bank[4 + n % 2][:H, 0:y - x], ACT.Copy).then_inc(rows, 1)

    return {"sync": sync, "gpsimd": gpsimd, "tensor": tensor, "scalar": scalar}


def memory_values(nc, K, I, O, memt, mkt, mv):
    S = K.sem
    came = [S(f"mv_w{h}") for h in range(2)]
    done, taken = S("mv_product"), S("mv_taken")
    w = K.big[:, O_W:O_W + KD * D].rearrange("p (h k n) -> p h k n", h=2, k=KD)
    with nc.Block() as block:
        @block.sync
        def _(sp):
            for h in range(2):
                sp.dma_start(w[:, h], I["w_mv"][h]).then_inc(came[h], 16)
            sp.dma_start(O["mem_k"], mkt).then_inc(K.out_sem, 16)
            sp.wait_ge(taken, 4)
            sp.dma_start(O["mem_v"].rearrange("t p n -> p t n"), mv).then_inc(K.out_sem, 16)
            K.outs(2)

        @block.tensor
        def _(pe):
            for j in range(4):
                h, t = j // 2, j % 2
                pe.wait_ge(came[h], 16)
                for k in range(KD):
                    last = nc.tensor.matmul(K.bank[j][:, :], memt[:, k, t * P:(t + 1) * P], w[:, h, k, :],
                                            start=k == 0, stop=k == KD - 1)
                last.then_inc(done, 1)

        @block.scalar
        def _(act):
            for j in range(4):
                h, t = j // 2, j % 2
                act.wait_ge(done, j + 1)
                nc.scalar.activation(mv[:, t, h * 512:(h + 1) * 512], K.bank[j][:, :], ACT.Copy).then_inc(taken, 1)


def cross_prompt(nc, K, qx, mkt, mv):
    S = K.sem
    w = K.big[:, O_W:O_M]
    px = [w[:, 1024 * b:1024 * (b + 1)].rearrange("p (h m) -> p h m", h=XH) for b in range(2)]
    pt = [w[:, 2048 + 1024 * b:2048 + 1024 * (b + 1)].rearrange("p (b n) -> p b n", b=8) for b in range(2)]
    st = [w[:, 4096 + 16 * b:4096 + 16 * (b + 1)] for b in range(2)]
    n = SEQ // P
    scores, neg, exps, probs = S("xp_scores"), S("xp_negmax"), S("xp_exp"), S("xp_probs")
    turned, taken, pv, o_taken, vch = S("xp_turned"), S("xp_turned_taken"), S("xp_pv"), S("xp_o_taken"), S("xp_dve")
    with nc.Block() as block:
        @block.tensor
        def _(pe):
            def score(t):
                if t >= 2:
                    pe.wait_ge(exps, XH * (t - 1))
                for h in range(XH):
                    for k in range(2):
                        last = nc.tensor.matmul(K.bank[2 * (t % 2) + h // 2][:, (h % 2) * MEM:(h % 2 + 1) * MEM],
                                                qx[:, 2 * h + k, t * P:(t + 1) * P], mkt[:, 2 * h + k, :],
                                                start=k == 0, stop=k == 1)
                last.then_inc(scores, 1)

            score(0)
            for t in range(n):
                if t + 1 < n:
                    score(t + 1)
                pe.wait_ge(probs, t + 1)
                for b in range(2):
                    if t:
                        pe.wait_ge(taken, 2 * (t - 1) + b + 1)
                    for x in range(4):
                        h, m = 2 * b + x // 2, x % 2
                        last = nc.tensor.transpose(K.bank[4 + b][:, x * P:(x + 1) * P], px[t % 2][:, h, m * P:(m + 1) * P], K.ident[:, :])
                    last.then_inc(turned, 1)
                for b in range(2):
                    pe.wait_ge(taken, 2 * t + b + 1)
                    if t:
                        pe.wait_ge(o_taken, 2 * (t - 1) + b + 1)
                    for x in range(4):
                        c = 4 * b + x
                        h = c // 2
                        for m in range(2):
                            last = nc.tensor.matmul(K.bank[6 + b][:, x * P:(x + 1) * P], mv[:, m, c * P:(c + 1) * P],
                                                    pt[t % 2][:, 2 * h + m, :], start=m == 0, stop=m == 1)
                    last.then_inc(pv, 1)

        @block.vector
        def _(dve):
            link = Chain(dve, vch)

            def maxima(t):
                m = st[t % 2]
                dve.wait_ge(scores, t + 1)
                b = 2 * (t % 2)
                link(nc.vector.tensor_reduce(m[:, 0:4], K.ps[:, b * 512:(b + 2) * 512].rearrange("p (h m) -> p h m", h=XH),
                                             AX.X, ALU.max))
                nc.vector.tensor_scalar(m[:, 4:8], m[:, 0:4], -(XHD ** -0.5), None, ALU.mult).then_inc(neg, 1)

            maxima(0)
            for t in range(n):
                if t + 1 < n:
                    maxima(t + 1)
                m = st[t % 2]
                dve.wait_ge(exps, XH * (t + 1))
                link(nc.vector.reciprocal(m[:, 12:16], m[:, 8:12]))
                nc.vector.tensor_tensor(px[t % 2], px[t % 2], m[:, 12:16].unsqueeze(2).to_broadcast([P, XH, MEM]),
                                        ALU.mult).then_inc(probs, 1)
                for b in range(2):
                    dve.wait_ge(turned, 2 * t + b + 1)
                    if t >= 2:
                        dve.wait_ge(pv, 2 * (t - 1))
                    nc.vector.tensor_copy(pt[t % 2][:, 4 * b:4 * b + 4, :],
                                          K.bank[4 + b][:, :].rearrange("p (b n) -> p b n", b=4)).then_inc(taken, 1)

        @block.scalar
        def _(act):
            def exp(t):
                m = st[t % 2]
                act.wait_ge(neg, t + 1)
                if t >= 2:
                    act.wait_ge(turned, 2 * (t - 1))
                for h in range(XH):
                    nc.scalar.activation(px[t % 2][:, h, :], K.bank[2 * (t % 2) + h // 2][:, (h % 2) * MEM:(h % 2 + 1) * MEM],
                                         ACT.Exp, bias=m[:, 4 + h:5 + h], scale=XHD ** -0.5,
                                         accum_out=m[:, 8 + h:9 + h]).then_inc(exps, 1)

            exp(0)
            for t in range(n):
                if t + 1 < n:
                    exp(t + 1)
                for b in range(2):
                    act.wait_ge(pv, 2 * t + b + 1)
                    nc.scalar.activation(K.HT[:, 4 * b:4 * b + 4, t * P:(t + 1) * P],
                                         K.bank[6 + b][:, :].rearrange("p (c n) -> p c n", c=4), ACT.Copy).then_inc(o_taken, 1)


def cross_sample(nc, K, I, qx):
    S = K.sem
    w = K.big[:, O_W:O_M]
    kr = [w[:, 2048 * b:2048 * (b + 1)].rearrange("p (c m) -> p c m", c=KD) for b in range(2)]
    vr = [w[:, 4096 + 2048 * b:4096 + 2048 * (b + 1)].rearrange("p (m n) -> p m n", m=2) for b in range(2)]
    qbd = w[:, 8192:10240].rearrange("p (c n r) -> p c n r", c=KD, n=NS)
    tmp = K.big[:, O_TMP:O_TMP + 2 * D]
    px, pt, ox, st = tmp[:, 0:256], tmp[:, 256:512].rearrange("p (m r) -> p m r", m=2), tmp[:, 512:1536], tmp[:, 1536:1544]
    k_came, v_came = [S(f"xs_k{b}") for b in range(2)], [S(f"xs_v{b}") for b in range(2)]
    zeroed, q_ready, scores, k_used = S("xs_zeroed"), S("xs_q"), S("xs_scores"), S("xs_keys_used")
    neg, exps, probs, turned, taken = S("xs_negmax"), S("xs_exp"), S("xs_probs"), S("xs_turned"), S("xs_turned_taken")
    pv, o_taken, o_turned, o_done, vch = S("xs_pv"), S("xs_o_taken"), S("xs_o_turned"), S("xs_o_done"), S("xs_dve")
    with nc.Block() as block:
        @block.sync
        def _(sp):
            for n in range(NS):
                if n >= 2:
                    sp.wait_ge(k_used, n - 1)
                sp.dma_start(kr[n % 2], I["mem_kt"][n]).then_inc(k_came[n % 2], 16)

        @block.gpsimd
        def _(pool):
            nc.gpsimd.memset(qbd, 0.0).then_inc(zeroed, 1)
            for n in range(NS):
                if n >= 2:
                    pool.wait_ge(pv, n - 1)
                pool.dma_start(vr[n % 2], I["mem_v"][n].rearrange("(m p) n -> p m n", p=P)).then_inc(v_came[n % 2], 16)

        @block.tensor
        def _(pe):
            pe.wait_ge(q_ready, KD)
            for half in range(2):
                if half:
                    pe.wait_ge(exps, half)
                for x in range(4):
                    n = 4 * half + x
                    pe.wait_ge(k_came[n % 2], 16 * (n // 2 + 1))
                    for c in range(KD):
                        last = nc.tensor.matmul(K.bank[0][32 * x:32 * x + 32, 0:MEM], qbd[:, c, n, :], kr[n % 2][:, c, :],
                                                start=c == 0, stop=c == KD - 1)
                    last.then_inc(k_used, 1)
                pe.wait_ge(probs, half + 1)
                for m in range(2):
                    last = nc.tensor.transpose(K.bank[1][:, m * P:(m + 1) * P], px[:, m * P:(m + 1) * P], K.ident[:, :])
                last.then_inc(turned, 1)
                pe.wait_ge(taken, half + 1)
                for x in range(4):
                    n = 4 * half + x
                    pe.wait_ge(v_came[n % 2], 16 * (n // 2 + 1))
                    for b in range(2):
                        for m in range(2):
                            last = nc.tensor.matmul(K.bank[2 + b][32 * x:32 * x + 32, :], pt[:, m, 32 * x:32 * x + 32],
                                                    vr[n % 2][:, m, b * 512:(b + 1) * 512], start=m == 0, stop=m == 1)
                    last.then_inc(pv, 1)
                pe.wait_ge(o_taken, half + 1)
                for c in range(KD):
                    last = nc.tensor.transpose(K.bank[4 + c // 4][:, (c % 4) * P:(c % 4 + 1) * P], ox[:, c * P:(c + 1) * P], K.ident[:, :])
                last.then_inc(o_turned, 1)

        @block.vector
        def _(dve):
            link = Chain(dve, vch)
            dve.wait_ge(zeroed, 1)
            for c in range(KD):
                nc.vector.tensor_copy(qbd[:, c, :, 4 * (c // 2):4 * (c // 2) + 4],
                                      qx[:, c, SEQ:T].rearrange("p (n q) -> p n q", n=NS)).then_inc(q_ready, 1)
            for half in range(2):
                dve.wait_ge(k_used, 4 * half + 4)
                link(nc.vector.tensor_reduce(st[:, 0:1], K.bank[0][:, 0:MEM], AX.X, ALU.max))
                nc.vector.tensor_scalar(st[:, 1:2], st[:, 0:1], -(XHD ** -0.5), None, ALU.mult).then_inc(neg, 1)
                dve.wait_ge(exps, half + 1)
                link(nc.vector.reciprocal(st[:, 3:4], st[:, 2:3]))
                nc.vector.tensor_scalar(px, px, st[:, 3:4], None, ALU.mult).then_inc(probs, 1)
                dve.wait_ge(turned, half + 1)
                nc.vector.tensor_copy(pt, K.bank[1][:, 0:2 * P].rearrange("p (m r) -> p m r", m=2)).then_inc(taken, 1)
                dve.wait_ge(pv, 4 * half + 4)
                nc.vector.tensor_copy(ox, K.ps[:, 1024:2048]).then_inc(o_taken, 1)
                dve.wait_ge(o_turned, half + 1)
                for c in range(KD):
                    src = K.bank[4 + c // 4][:, (c % 4) * P:(c % 4 + 1) * P].rearrange("p (n r) -> p n r", n=4)[:, :, 4 * (c // 2):4 * (c // 2) + 4]
                    last = nc.vector.tensor_copy(K.HT[:, c, SEQ + 16 * half:SEQ + 16 * half + 16].rearrange("p (n q) -> p n q", n=4), src)
                link(last)

        @block.scalar
        def _(act):
            for half in range(2):
                act.wait_ge(neg, half + 1)
                if half:
                    act.wait_ge(turned, half)
                nc.scalar.activation(px, K.bank[0][:, 0:MEM], ACT.Exp, bias=st[:, 1:2], scale=XHD ** -0.5,
                                     accum_out=st[:, 2:3]).then_inc(exps, 1)


def ffn_up(nc, K, I, O, mem, actt, high, low):
    S = K.sem
    sb = lambda name, shape, dt=F32: mem.enter_context(nc.sbuf_tensor(name, shape, dt))
    landing = sb("ff_weights", [P, 2, KD, P])
    w_high, w_low = sb("ff_weights_high", [P, 2, KD, P], F32R), sb("ff_weights_low", [P, 2, KD, P], F32R)
    ext = [sb(f"ff_row{u}", [P, 1074])[:, :] for u in range(2)]
    ct = [sb(f"ff_conv{u}", [P, T])[:, :] for u in range(2)]
    cpt = sb("ff_small", [P, 848])
    prev = cpt[:, 0:FC * 16].rearrange("p (c n) -> p c n", c=FC)
    co = cpt[:, 352:352 + FC * 18].rearrange("p (c n) -> p c n", c=FC)
    cwb = cpt[:, 752:752 + FC * 4].rearrange("p (c n) -> p c n", c=FC)
    cw = [cpt[:, 840 + 4 * u:844 + 4 * u] for u in range(2)]
    w_came, w_split, low_done = ([S(f"ff_{s}_{x}") for s in ("up", "gate")] for x in ("came", "high", "low"))
    small, zeroed = S("ff_small_came"), S("ff_zeroed")
    up_done, gate_done, up_taken, gate_taken = S("ff_up"), S("ff_gate"), S("ff_up_taken"), S("ff_gate_taken")
    conv_done, gelu_done, vch = S("ff_conv"), S("ff_gelu"), S("ff_dve")
    pieces = [(0, FREE3), (FREE3, 2 * FREE3), (2 * FREE3, T)]
    LINKS = 7

    with nc.Block() as block:
        @block.sync
        def _(sp):
            sp.dma_start(prev, I["conv_prev"]).then_inc(small, 16)
            sp.dma_start(cwb, I["conv_wb"]).then_inc(small, 16)
            for c in range(FC):
                for x, name in enumerate(("w_up", "w_gate")):
                    if c:
                        sp.wait_ge(low_done[x], c)
                    sp.dma_start(landing[:, x], I[name][c]).then_inc(w_came[x], 16)
            sp.wait_ge(conv_done, FC + 2)
            sp.dma_start(O["conv"], co).then_inc(K.out_sem, 16)
            K.outs(1)

        @block.gpsimd
        def _(pool):
            for u in range(2):
                nc.gpsimd.memset(ext[u][:, 0:2], 0.0).then_inc(zeroed, 1)
            with pool.Fori(0, FC) as c:
                for x in range(2):
                    pool.wait_ge(w_split[x], c + 1)
                    nc.gpsimd.tensor_tensor(w_low[:, x], landing[:, x], w_high[:, x], ALU.subtract).then_inc(low_done[x], 1)

        @block.tensor
        def _(pe):
            with pe.Fori(0, FC // 2) as i:
                for u in range(2):
                    for s, (done, taken) in enumerate(((up_done, up_taken), (gate_done, gate_taken))):
                        pe.wait_ge(low_done[s], i * 2 + u + 1)
                        pe.wait_ge(taken, i * 2 + u + 1)
                        for x, (a, b) in enumerate(pieces):
                            for k in range(KD):
                                for n, (w, h) in enumerate(((w_high, high), (w_high, low), (w_low, high))):
                                    last = nc.tensor.matmul(K.bank[3 * s + x][:, 0:b - a], w[:, s, k, :], h[:, k, a:b],
                                                            start=k + n == 0, stop=k == KD - 1 and n == 2)
                        last.then_inc(done, 1)

        @block.scalar
        def _(act):
            act.sem_inc(up_taken, 1)

            def high_part(s, c):
                act.wait_ge(w_came[s], c * 16 + 16)
                nc.scalar.activation(w_high[:, s], landing[:, s], ACT.Copy).then_inc(w_split[s], 1)

            def chunk(i, u, more):
                act.wait_ge(up_done, i * 2 + u + 1)
                if more:
                    high_part(0, i * 2 + (u + 1))
                act.wait_ge(conv_done, i * 2 + u + 1)
                nc.scalar.activation(ext[u][:, 2:2 + FREE3], K.bank[0][:, 0:FREE3], ACT.Copy)
                nc.scalar.activation(ext[u][:, 2 + FREE3:2 + 2 * FREE3], K.bank[1][:, 0:FREE3], ACT.Copy)
                nc.scalar.activation(ext[u][:, 2 + 2 * FREE3:2 + SEQ], K.bank[2][:, 0:SEQ - 2 * FREE3], ACT.Copy)
                nc.scalar.activation(ext[u][:, 1026:1074].rearrange("p (n q) -> p n q", n=NS)[:, :, 2:6],
                                     K.bank[2][:, SEQ - 2 * FREE3:FREE3].rearrange("p (n q) -> p n q", n=NS),
                                     ACT.Copy).then_inc(up_taken, 1)
                act.wait_ge(conv_done, i * 2 + u + 3)
                nc.scalar.activation(ct[u], ct[u], ACT.Gelu_apprx_tanh).then_inc(gelu_done, 1)
                if more:
                    act.wait_ge(gate_done, i * 2 + u + 1)
                    high_part(1, i * 2 + (u + 1))

            high_part(0, 0)
            high_part(1, 0)
            with act.Fori(0, FC // 2 - 1) as i:
                chunk(i, 0, True)
                chunk(i, 1, True)
            chunk(FC // 2 - 1, 0, True)
            chunk(FC // 2 - 1, 1, False)

        @block.vector
        def _(dve):
            dve.sem_inc(conv_done, 2)
            dve.sem_inc(gate_taken, 1)
            dve.wait_ge(small, 32)
            dve.wait_ge(zeroed, 2)
            with dve.Fori(0, FC // 2) as i:
                n = 0

                def link(ins):
                    nonlocal n
                    n += 1
                    ins.then_inc(vch, 1)
                    dve.wait_ge(vch, i * (2 * LINKS) + n)

                for u in range(2):
                    c = bass.ds(i * 2 + u, 1)
                    es = ext[u][:, 1026:1074].rearrange("p (n q) -> p n q", n=NS)
                    cs = ct[u][:, SEQ:T].rearrange("p (n q) -> p n q", n=NS)
                    w = [cw[u][:, x:x + 1] for x in range(4)]
                    link(nc.vector.tensor_copy(cw[u], cwb[:, c, :].rearrange("p a n -> p (a n)")))
                    link(nc.vector.tensor_copy(es[:, :, 0:2], prev[:, c, :].rearrange("p a (n q) -> p (a n) q", q=2)))
                    dve.wait_ge(up_taken, i * 2 + u + 2)
                    nc.vector.tensor_scalar(ct[u][:, 0:SEQ], ext[u][:, 0:SEQ], w[0], w[3], ALU.mult, ALU.add)
                    link(nc.vector.tensor_scalar(cs, es[:, :, 0:4], w[0], w[3], ALU.mult, ALU.add))
                    nc.vector.scalar_tensor_tensor(ct[u][:, 0:SEQ], ext[u][:, 1:SEQ + 1], w[1], ct[u][:, 0:SEQ], ALU.mult, ALU.add)
                    link(nc.vector.scalar_tensor_tensor(cs, es[:, :, 1:5], w[1], cs, ALU.mult, ALU.add))
                    nc.vector.tensor_copy(co[:, c, 0:2].rearrange("p a n -> p (a n)"), ext[u][:, SEQ:SEQ + 2])
                    link(nc.vector.tensor_copy(co[:, c, 2:18].rearrange("p a (n q) -> p (a n) q", q=2), es[:, :, 4:6]))
                    nc.vector.scalar_tensor_tensor(ct[u][:, 0:SEQ], ext[u][:, 2:SEQ + 2], w[2], ct[u][:, 0:SEQ], ALU.mult, ALU.add)
                    link(nc.vector.scalar_tensor_tensor(cs, es[:, :, 2:6], w[2], cs, ALU.mult, ALU.add))
                    dve.sem_inc(conv_done, 1)
                    dve.wait_ge(gelu_done, i * 2 + u + 1)
                    dve.wait_ge(gate_done, i * 2 + u + 1)
                    for x, (a, b) in enumerate(pieces):
                        last = nc.vector.tensor_tensor(actt[:, c, a:b].rearrange("p a n -> p (a n)"), ct[u][:, a:b],
                                                       K.bank[3 + x][:, 0:b - a], ALU.mult)
                    link(last)
                    dve.sem_inc(gate_taken, 1)


def ffn_down(nc, K, I, mem, actt):
    S = K.sem
    slot = [mem.enter_context(nc.sbuf_tensor(f"dn_weights{u}", [P, FC, 256], F32)) for u in range(2)]
    came, x_came = [S(f"dn_w{u}") for u in range(2)], [S(f"dn_x{t}") for t in range(TILES)]
    done, taken = S("dn_product"), S("dn_taken")
    per = 2 * TILES
    with nc.Block() as block:
        @block.sync
        def _(sp):
            for q in range(4):
                if q >= 2:
                    sp.wait_ge(done, (q - 1) * TILES)
                sp.dma_start(slot[q % 2][:, :, :], I["w_down"][q]).then_inc(came[q % 2], 16)
                if q == 0:
                    for t in range(TILES):
                        sp.dma_start(K.X[:rows_of(t), t, :], K.x_dram[t, :rows_of(t), :]).then_inc(x_came[t], 16)

        @block.tensor
        def _(pe):
            with pe.Fori(0, 2) as i:
                for j in range(per):
                    u, t = j // TILES, j % TILES
                    if t == 0:
                        pe.wait_ge(came[u], i * 16 + 16)
                    pe.wait_ge(taken, i * per + j + 1)
                    for k in range(FC):
                        last = nc.tensor.matmul(K.bank[j % 6][:rows_of(t), 0:256], actt[:, k, t * P:t * P + rows_of(t)],
                                                slot[u][:, k, :], start=k == 0, stop=k == FC - 1)
                    last.then_inc(done, 1)

        @block.vector
        def _(dve):
            dve.sem_inc(taken, 6)
            with dve.Fori(0, 2) as i:
                for j in range(per):
                    u, t = j // TILES, j % TILES
                    x = K.X[:rows_of(t), t, bass.ds(i * 512 + u * 256, 256)]
                    dve.wait_ge(done, i * per + j + 1)
                    if u == 0:
                        dve.wait_ge(x_came[t], 16)
                    nc.vector.tensor_tensor(x, K.bank[j % 6][:rows_of(t), 0:256], x, ALU.add).then_inc(taken, 1)


def final_norm(nc, K, I, O, mem):
    S = K.sem
    came, squares, std_ready, rs_ready, y = S("fin_gain"), S("fin_squares"), S("fin_std"), S("fin_rstd"), S("fin_y")
    zero = S("fin_stat_set")
    g = mem.enter_context(nc.sbuf_tensor("final_gain", [P, D], F32))
    ss, std, rs = K.stat[:, 0, :TILES], K.stat[:, 1, :TILES], K.stat[:, 2, :TILES]
    with nc.Block() as block:
        @block.sync
        def _(sp):
            sp.dma_start(g[:, :], I["g_final"].to_broadcast([P, D])).then_inc(came, 16)
            for t in range(TILES):
                sp.wait_ge(y, t + 1)
                to = O["y_prompt"][t] if t < TILES - 1 else O["y_sample"]
                sp.dma_start(to, K.X[:rows_of(t), t, :]).then_inc(K.out_sem, 16)
            sp.wait_ge(K.out_sem, 16 * K.outs(TILES))

        @block.scalar
        def _(act):
            act.wait_ge(zero, 1)
            for t in range(TILES):
                r = rows_of(t)
                if t:
                    act.wait_ge(squares, t)
                nc.scalar.activation(K.junk[:r, :], K.X[:r, t, :], ACT.Square, accum_out=ss[:r, t:t + 1]).then_inc(squares, 1)
            act.wait_ge(squares, TILES)
            nc.scalar.activation(std, ss, ACT.Sqrt, bias=K.eps[:, 0:1], scale=1.0 / D).then_inc(std_ready, 1)

        @block.vector
        def _(dve):
            nc.vector.memset(ss, 1.0).then_inc(zero, 1)
            dve.wait_ge(std_ready, 1)
            nc.vector.reciprocal(rs, std).then_inc(rs_ready, 1)
            dve.wait_ge(rs_ready, 1)
            dve.wait_ge(came, 16)
            for t in range(TILES):
                r = rows_of(t)
                nc.vector.scalar_tensor_tensor(K.X[:r, t, :], K.X[:r, t, :], rs[:r, t:t + 1], g[:r, :], ALU.mult, ALU.mult).then_inc(y, 1)


class Places:

    def outs(self, n):
        self.n_out += n
        return self.n_out


def program(nc, I, O):
    ctx = ExitStack()
    with ctx:
        K = Places()
        K.n_out, K.page_regs = 0, None
        first_part, K.sems = ExitStack(), []

        def phase_sem(name):
            K.sems.append(first_part.enter_context(nc.semaphore(name)))
            return K.sems[-1]

        K.sem = phase_sem
        sb = lambda name, shape, dt=F32: ctx.enter_context(nc.sbuf_tensor(name, shape, dt))
        K.ident = sb("ident", [P, P])
        K.gains = sb("gains", [P, 5, KD])
        K.GT = sb("gates_by_token", [P, TILES, 3 * H])
        K.GS = sb("gates_by_head", [P, H, TILES - 1, 3])
        K.stat = sb("stat", [P, 3, 2 * TILES])
        K.eps = sb("eps", [P, 1])
        K.table = sb("table", [BUCKETS + 1, H])
        K.page_table = sb("pages", [1, NS * NPAGE], I32)
        K.n_pool = I["pool_sel_k"].shape[0]
        x_place, shared = ExitStack(), ExitStack()
        x = x_place.enter_context(nc.sbuf_tensor("x", [P, TILES * D], F32, side="right"))
        K.big = shared.enter_context(nc.sbuf_tensor("big", [P, BIG], F32))
        K.tmp = K.big[:, O_TMP:O_TMP + 2 * D]
        K.ps = ctx.enter_context(nc.psum_tensor("ps", [P, 8 * 512], F32))
        K.bank = [K.ps[:, 512 * b:512 * (b + 1)] for b in range(8)]
        K.ps4 = K.ps[:, 0:2048]
        K.junk = K.ps[:, 3072:4096]
        K.X = x[:, :].rearrange("p (t n) -> p t n", t=TILES)
        K.HT = K.big[:, O_HT:O_W].rearrange("p (k n) -> p k n", k=KD)
        K.M = K.big[:, O_M:O_FM].rearrange("p (t n) -> p t n", t=TILES)
        K.FM = K.big[:, O_FM:O_VT].rearrange("p (c n) -> p c n", c=8)
        K.VT = K.big[:, O_VT:O_TMP].rearrange("p (t n) -> p t n", t=TILES)
        cp = K.big[:, O_CP:BIG]
        K.KCP, K.VCP = cp[:, 0:63], cp[:, 64:192]
        K.KCS = cp[:, 192:696].rearrange("p (n c) -> p n c", n=NS)
        K.VCS = cp[:, 696:1720].rearrange("p (n c) -> p n c", n=NS)
        K.vec_dram = nc.dram_tensor("bias_rows", [H, VECS + VECW], F32).ap()
        K.gates_dram = nc.dram_tensor("sample_gates", [SROWS, 3 * H], F32).ap()
        K.x_dram = nc.dram_tensor("residual_stream", [TILES, P, D], F32).ap()
        K.o_dram = nc.dram_tensor("sample_out", [SROWS, DA], F32).ap()
        K.out_sem, K.gates_sem, K.wtm_sem, K.gating_sem, K.x_came = (
            ctx.enter_context(nc.semaphore(name)) for name in
            ("outputs_written", "gates_in_dram", "token_major_weights", "gating_operands", "x_came_again"))
        K.slot = [x[:, 0:4096], x[:, 4096:8192], K.big[:, O_HT:O_HT + 4096], K.big[:, O_HT + 4096:O_HT + 8192]]
        K.slot_came = [K.sem(f"pages_slot{i}") for i in range(4)]
        K.windows = [(K.M[:, 0:4, DA:D], K.M[:, 4:8, DA:D]),
                     tuple(K.big[:, O_HT + 8192 + 2048 * i:O_HT + 10240 + 2048 * i].rearrange("p (n t) -> p n t", n=4) for i in range(2))]
        K.windows_came = [K.sem(f"windows{i}") for i in range(2)]

        const_came, eps_set = K.sem("const_came"), K.sem("eps_set")
        with nc.Block() as block:
            @block.sync
            def _(sp):
                sp.dma_start(K.ident[:, :], I["ident"]).then_inc(const_came, 16)
                sp.dma_start(K.gains[:, :, :], I["gains"]).then_inc(const_came, 16)
                sp.wait_ge(const_came, 32)

            @block.gpsimd
            def _(pool):
                nc.gpsimd.memset(K.eps[:, :], EPS).then_inc(eps_set, 1)
                pool.wait_ge(eps_set, 1)

        norm_phase(nc, K, "mix", x_tiles(K), D, K.gains[:, 0, :], K.HT, x_loads(K, I), bias_rows(nc, K, I))

        def states(sp):
            for u in range(2):
                sp.wait_ge(K.fm_taken[u], 5)
            sp.dma_start(O["fm"].rearrange("c p n -> p c n"), K.FM[:, 4:8, :]).then_inc(K.out_sem, 16)
            for v in range(2):
                sp.dma_start(O["win_old"][v], I["win_old"][v][:, TS:WIN, :]).then_inc(K.out_sem, 16)
            K.outs(3)

        ring = K.big[:, O_M:O_M + 2048].rearrange("p (u k n) -> p u k n", u=2, k=KD)

        def small(sp):
            for to, of in gating_operands(K, I):
                sp.dma_start(to, of).then_inc(K.gating_sem, 16)

        feature_major(nc, K, "fm", I["w_fm"], 8, ring, K.HT, T, K.FM,
                      {"sync": states, ("sync", 1): lambda sp: gather_cmp(sp, I, K, 0, 0, 0),
                       ("sync", 3): lambda sp: gather_cmp(sp, I, K, 0, 1, 1), ("sync", 5): small})
        gating_phase(nc, K, I, O)
        compress_phase(nc, K, I)
        sample_attention(nc, K, I)
        prompt_attention(nc, K, I)
        with nc.Block() as block:
            @block.gpsimd
            def _(pool):
                for s in K.sems:
                    pool.sem_clear(s)
        first_part.close()
        wo = projection_weights(K, "wo", I["w_o"])
        norm_phase(nc, K, "merge", [(K.M[:rows_of(t), t, :], rows_of(t), t * P) for t in range(TILES)], DA, K.gains[:, 1, :], K.HT,
                   extra={"sync": wo[2]})
        project_add(nc, K, "wo", wo, K.HT, K.x_came)
        norm_phase(nc, K, "xa", x_tiles(K), D, K.gains[:, 2, :], K.HT)
        m = K.big[:, O_M:O_FM]
        memx = m[:, 0:2048].rearrange("p (t n) -> p t n", t=2)
        memt = m[:, 2048:4096].rearrange("p (k n) -> p k n", k=KD)
        mkt = m[:, 4096:6144].rearrange("p (k n) -> p k n", k=KD)
        mv = m[:, 6144:8192].rearrange("p (t n) -> p t n", t=2)
        norm_phase(nc, K, "mem", [(memx[:, t, :], P, t * P) for t in range(2)], D, K.gains[:, 3, :], memt,
                   [(memx[:, t, :], I["mem_prompt"][t]) for t in range(2)])
        ring = K.big[:, O_TMP:O_TMP + 2048].rearrange("p (u k n) -> p u k n", u=2, k=KD)
        feature_major(nc, K, "mk", I["w_mk"], 8, ring, memt, MEM, mkt)
        memory_values(nc, K, I, O, memt, mkt, mv)
        feature_major(nc, K, "xq", I["w_xq"], 8, ring, K.HT, T, K.FM)
        cross_prompt(nc, K, K.FM, mkt, mv)
        cross_sample(nc, K, I, K.FM)
        xo = projection_weights(K, "xo", I["w_xo"])
        with nc.Block() as block:
            @block.sync
            def _(sp):
                xo[2](sp)
        project_add(nc, K, "xo", xo, K.HT)
        shared.close()
        norm_mem, acts_mem, split_mem, down_mem = (ExitStack() for _ in range(4))
        high, low = (split_mem.enter_context(nc.sbuf_tensor(f"ff_in_{n}", [P, KD, T], F32R)) for n in ("high", "low"))
        K.tmp = norm_mem.enter_context(nc.sbuf_tensor("ff_scaled", [P, 2 * D], F32))[:, :]
        whole = norm_mem.enter_context(nc.sbuf_tensor("ff_normed", [P, 2, KD, P], F32))
        spilled = K.sem("x_in_dram")

        def spill(sp):
            for t in range(TILES):
                sp.dma_start(K.x_dram[t, :rows_of(t), :], K.X[:rows_of(t), t, :]).then_inc(spilled, 16)
            sp.wait_ge(spilled, 16 * TILES)

        norm_phase(nc, K, "ffn", x_tiles(K), D, K.gains[:, 4, :], None, extra={"sync": spill}, split=(high, low, whole))
        norm_mem.close()
        x_place.close()
        actt = acts_mem.enter_context(nc.sbuf_tensor("ff_activations", [P, FC, T], F32, side="right"))
        with ExitStack() as mem:
            ffn_up(nc, K, I, O, mem, actt, high, low)
        split_mem.close()
        K.X = down_mem.enter_context(nc.sbuf_tensor("x_again", [P, TILES, D], F32))
        ffn_down(nc, K, I, down_mem, actt)
        acts_mem.close()
        final_norm(nc, K, I, O, down_mem)
        down_mem.close()


def bucket(dist):
    n = np.maximum(dist, 0)
    exact = BUCKETS // 2
    large = exact + (np.log(np.maximum(n, 1) / exact) / math.log(MAXDIST / exact) * (BUCKETS - exact)).astype(np.int64)
    return np.where(n < exact, n, np.minimum(large, BUCKETS - 1))


def constants():
    c = {"ident": np.eye(P)}
    oh = np.zeros((BUCKETS + 1, VECS + VECW))
    d = np.concatenate([np.arange(VECS) - 1023, np.arange(VECW) - 127])
    dead = (d < 0) | ((np.arange(len(d)) >= VECS) & (d >= WIN))
    oh[np.where(dead, BUCKETS, bucket(d)), np.arange(len(d))] = 1
    c["oh_v"] = oh
    new = np.arange(SROWS) % TS
    cmp_end = np.arange(NCMP) * CS + CL - 1
    pos = np.concatenate([np.arange(PAST), PAST + new, PAST + new, PAST - WIN + np.arange(WIN), cmp_end])
    oh = np.zeros((TS, BUCKETS, len(pos)))
    for q in range(TS):
        oh[q, bucket(PAST + q - pos), np.arange(len(pos))] = 1
    c["oh_s"] = oh.reshape(P, -1)
    r = np.arange(P)
    seq, grp, qry = r // 32, r // 16 % 2, r % 4
    c["dq"] = (r[:, None] // 32 == qry[None, :]) * 1.0
    c["gmat"] = ((seq[:, None] == seq) & (grp[:, None] == grp) & (qry[:, None] == qry)) * 1.0
    k = np.arange(SROWS)
    mask = np.zeros((P, 2, 2, SROWS))
    for half in range(2):
        ok = (seq[:, None] + 4 * half == k[None, :] // TS) & (k[None, :] % TS <= qry[:, None])
        mask[:, half, :, :] = np.where(ok, 0, NEG)[:, None, :]
    c["mask_new"] = mask.reshape(P, 2, 2 * SROWS)
    c["mask_win"] = np.where(np.arange(4)[None, :] > qry[:, None], 0, NEG)
    c0, s0 = np.arange(NCMP)[:, None] * CS, np.arange(NSEL)[None, :] * SELB
    c["overlap"] = ((c0 < s0 + SELB) & (c0 + CL > s0)) * 1.0
    c["jidx"] = np.broadcast_to(np.arange(1, 15), (P, 14))
    c["causal"] = (r[:, None] <= r[None, :]) * 1.0
    c["causal_s"] = ((k[:, None] // TS == k[None, :] // TS) & (k[:, None] <= k[None, :])) * 1.0
    c["cmp_valid"] = (r[:, None] >= CL - 1) * 1.0
    return {n: np.ascontiguousarray(a, np.float32) for n, a in c.items()}


def stationary(w):
    r, n = w.shape
    return w.reshape(r // P, P, n // P, P).transpose(2, 1, 0, 3)


def moving(w, width):
    r, n = w.shape
    return w.reshape(r // P, P, n // width, width).transpose(2, 1, 0, 3)


def kernel(**inputs):
    import concourse.bacc as bacc
    from concourse.bass_utils import run_bass_kernel_spmd

    x = {n: np.asarray(a) for n, a in inputs.items()}
    w = x["w_in"][0]
    q0, kv0, g0 = 2 * DA, 2 * DA + DA, 2 * DA + DA + 6 * KV
    q = w[:, q0:kv0].reshape(D, 2, HPG, HD).transpose(0, 2, 1, 3).reshape(D, DA)
    kv = [w[:, kv0 + i * KV:kv0 + (i + 1) * KV] for i in range(6)]
    L = {
        "x_prompt": x["x_prompt"].reshape(SEQ // P, P, D),
        "x_sample": x["x_sample"].reshape(SROWS, D),
        "mem_prompt": x["mem_prompt"].reshape(MEM // P, P, D),
        "page_table": x["page_table"].reshape(1, -1).astype(np.int32),
        "w_fm": stationary(np.concatenate([q, kv[0], kv[1], kv[2], kv[4]], 1)),
        "w_tm": np.concatenate([w[:, :q0], kv[3], kv[5], w[:, g0:]], 1).reshape(KD, P, TMW),
        "gains": np.stack([x["g_mix"][0], np.concatenate([x["g_a"][0], x["g_b"][0]]), x["g_xa"][0], x["g_mem"][0],
                           x["g_ffn"][0]]).reshape(5, KD, P).transpose(2, 0, 1),
        "ln_v_g": x["ln_v_g"], "ln_v_b": x["ln_v_b"], "g_final": x["g_final"][None],
        "ws_t": x["w_s"][0].transpose(2, 0, 1),
        "ws_s": np.tile(x["w_s"][0][:, :TS, :TS].transpose(2, 0, 1), (NS, 1, NS)),
        "bs_t": x["b_s"][0].T,
        "bs_s": np.tile(x["b_s"][0][:, :TS].T, (NS, 1)),
        "w_cmp1": np.stack([x[f"w_cmp1_{c}"][0].reshape(16, P, P).transpose(1, 0, 2) for c in "kv"]),
        "w_cmp2": np.stack([x[f"w_cmp2_{c}"][0] for c in "kv"]),
        "pe_cmp": np.stack([x[f"pe_cmp_{c}"][0].reshape(16, P).T for c in "kv"]),
        "b_cmp1": np.stack([x[f"b_cmp1_{c}"][0] for c in "kv"], 1),
        "b2k": np.tile(x["b_cmp2_k"][0], 2)[:, None],
        "b2v": np.tile(x["b_cmp2_v"][0], 2)[None],
        "pool_cmp": np.stack([x[f"cache_cmp_{c}"][0].reshape(-1, PAGE // 2, 2, HKV, HD).transpose(0, 2, 4, 3, 1).reshape(-1, P, HKV, PAGE // 2)
                              for c in "kv"]),
        "pool_sel_k": x["cache_sel_k"][0].reshape(-1, PAGE, KV).transpose(0, 2, 1),
        "pool_sel_v": x["cache_sel_v"][0].reshape(-1, PAGE, KV),
        "win_kt": x["cache_win_k"][0].reshape(NS, WIN, KV).transpose(0, 2, 1),
        "win_v": x["cache_win_v"][0].reshape(NS, WIN, KV),
        "win_old": np.stack([x[f"cache_win_{c}"][0].reshape(NS, WIN, KV) for c in "kv"]),
        "rel_bias": x["rel_bias"],
        "w_o": moving(x["w_o"][0], 512), "w_mv": moving(x["w_mv"][0], 512), "w_xo": moving(x["w_xo"][0], 512),
        "w_mk": stationary(x["w_mk"][0]), "w_xq": stationary(x["w_xq"][0]),
        "w_up": stationary(x["w_up"][0]), "w_gate": stationary(x["w_gate"][0]),
        "w_down": moving(x["w_down"][0], 256),
        "mem_kt": x["cache_mem_k"][0].reshape(NS, MEM, KD, P).transpose(0, 3, 2, 1),
        "mem_v": x["cache_mem_v"][0].reshape(NS, MEM, D),
        "conv_prev": x["state_conv"][0].transpose(2, 0, 1).reshape(FC, P, NS * 2).transpose(1, 0, 2),
        "conv_wb": np.concatenate([x["conv_w"][0], x["conv_b"]]).reshape(4, FC, P).transpose(2, 1, 0),
    }
    L.update(constants())
    shapes = {
        "y_prompt": (SEQ // P, P, D), "y_sample": (SROWS, D), "fm": (4, P, T), "vt": (SEQ // P, P, 2 * KV),
        "vt_s": (SROWS, 2 * KV), "win_old": (2, NS, WIN - TS, KV), "gmlp_v": (SROWS, DA),
        "mem_k": (P, KD, MEM), "mem_v": (MEM // P, P, D), "conv": (P, FC, 18),
    }
    nc = bacc.Bacc("TRN2", target_bir_lowering=False, num_devices=1)
    arrays, I, O = {}, {}, {}
    for n, a in L.items():
        a = np.ascontiguousarray(a)
        arrays[f"in_{n}"] = a
        I[n] = nc.dram_tensor(f"in_{n}", a.shape, mybir.dt.from_np(a.dtype), kind="ExternalInput").ap()
    for n, s in shapes.items():
        O[n] = nc.dram_tensor(f"out_{n}", s, F32, kind="ExternalOutput").ap()
    program(nc, I, O)
    r = run_bass_kernel_spmd(nc, [arrays], core_ids=[0]).results[0]
    o = {n: np.asarray(r[f"out_{n}"]) for n in shapes}

    fm = o["fm"].transpose(0, 2, 1)
    vt = o["vt"].reshape(SEQ, 2 * KV)
    rows = lambda a: a.reshape(1, 1, -1, HKV, HD)
    srows = lambda a: a.reshape(1, NS, TS, HKV, HD)
    vs, vw = o["vt_s"][:, :KV], o["vt_s"][:, KV:]
    win = [np.concatenate([o["win_old"][i], a.reshape(NS, TS, KV)], 1).reshape(1, NS, WIN, HKV, HD)
           for i, a in enumerate((fm[3][SEQ:], vw))]
    conv = o["conv"].transpose(1, 0, 2).reshape(FF, 18)
    return (o["y_prompt"].reshape(1, SEQ, D), o["y_sample"].reshape(NS, TS, D),
            rows(fm[0][:SEQ]), rows(fm[1][:SEQ]), rows(fm[2][:SEQ]), rows(vt[:, :KV]),
            rows(fm[3][SEQ - WIN:SEQ]), rows(vt[SEQ - WIN:, KV:]),
            o["mem_k"].transpose(2, 1, 0).reshape(1, 1, MEM, XH, XHD), o["mem_v"].reshape(1, 1, MEM, XH, XHD),
            conv[:, :2].T.reshape(1, 1, 2, FF),
            srows(fm[0][SEQ:]), srows(fm[1][SEQ:]), srows(fm[2][SEQ:]), srows(vs),
            win[0], win[1], o["gmlp_v"].reshape(1, NS, TS, DA),
            conv[:, 2:].reshape(FF, NS, 2).transpose(1, 2, 0).reshape(1, NS, 2, FF))
```

```python
import math
from contextlib import ExitStack

import numpy as np
import concourse.bass as bass
from concourse import mybir

F32 = mybir.dt.float32
F32R = mybir.dt.float32r
I32 = mybir.dt.int32
ALU = mybir.AluOpType
ACT = mybir.ActivationFunctionType
AX = mybir.AxisListType

P = 128
D = 1024
KD = D // P
SEQ = 1024
NS, TS = 8, 4
T = SEQ + NS * TS
TILES = SEQ // P + 1
SROWS = NS * TS
FREE3 = T // 3
DA = 512
AG, AGD = 8, 64
H, HKV, HPG, HD = 8, 2, 4, 64
KV = HKV * HD
PAST, PAGE, NPAGE = 1024, 128, 8
CL, CS = 32, 16
NCMP = PAST // CS - 1
SELB = 64
NSEL = 17
WIN = 512
BUCKETS, MAXDIST = 32, 128
MEM = 256
XH, XHD = 4, 256
FF = 2816
FC = FF // P
NEG = -1e30
EPS = 1e-6
TMW = 2 * DA + 2 * KV + 3 * H
VECS, VECW = 2048, 768
STRS, STRW = 1920, 640

O_HT = 0
O_W = O_HT + KD * T
BIG = O_W + KD * TMW
O_M = 0
O_FM = O_M + TILES * D
O_VT = O_FM + 8 * T
O_TMP = O_VT + TILES * 2 * KV
O_CP = O_TMP + 2 * D
TOP = O_CP + 63 + 128 + 504 + 1024 + 1


def rows_of(t):
    return P if t < TILES - 1 else SROWS


class Chain:

    def __init__(self, eng, sem):
        self.eng, self.sem, self.n = eng, sem, 0

    def __call__(self, ins):
        self.n += 1
        ins.then_inc(self.sem, 1)
        self.eng.wait_ge(self.sem, self.n)


def norm_phase(nc, K, tag, tiles, width, gain, dst, loads=None, extra=None):
    parts = D // width
    n = len(tiles)
    S = K.sem
    stat_zero, squares, std_ready = S(f"{tag}_stat_set"), S(f"{tag}_squares"), S(f"{tag}_std")
    rstd_ready, scaled, turned, taken = S(f"{tag}_rstd"), S(f"{tag}_scaled"), S(f"{tag}_turned"), S(f"{tag}_taken")
    arrived = [S(f"{tag}_x{i}") for i in range(n)] if loads else None
    ss, std, rs = K.stat[:, 0, :n * parts], K.stat[:, 1, :n * parts], K.stat[:, 2, :n * parts]
    xn = K.tmp.rearrange("p (b n) -> p b n", b=2)

    with nc.Block() as block:
        @block.sync
        def _(sp):
            if loads:
                for i, (to, of) in enumerate(loads):
                    sp.dma_start(to, of).then_inc(arrived[i], 16)
            if extra and "sync" in extra:
                extra["sync"](sp)

        @block.gpsimd
        def _(pool):
            if extra and "gpsimd" in extra:
                extra["gpsimd"](pool)

        @block.scalar
        def _(act):
            act.wait_ge(stat_zero, 1)
            for i, (src, rows, _) in enumerate(tiles):
                if loads:
                    act.wait_ge(arrived[i], 16)
                for q in range(parts):
                    if i + q:
                        act.wait_ge(squares, i * parts + q)
                    nc.scalar.activation(K.junk[:rows, 0:width], src[:, q * width:(q + 1) * width], ACT.Square,
                                         accum_out=ss[:rows, i * parts + q:i * parts + q + 1]).then_inc(squares, 1)
            act.wait_ge(squares, n * parts)
            nc.scalar.activation(std, ss, ACT.Sqrt, bias=K.eps[:, 0:1], scale=1.0 / width).then_inc(std_ready, 1)
            if extra and "scalar" in extra:
                extra["scalar"](act)

        @block.vector
        def _(dve):
            nc.vector.memset(ss, 1.0).then_inc(stat_zero, 1)
            dve.wait_ge(std_ready, 1)
            nc.vector.reciprocal(rs, std).then_inc(rstd_ready, 1)
            dve.wait_ge(rstd_ready, 1)

            def scale(i):
                src, rows, _ = tiles[i]
                if i >= 2:
                    dve.wait_ge(turned, 2 * (i - 1))
                for q in range(parts):
                    last = nc.vector.tensor_scalar(xn[:rows, i % 2, q * width:(q + 1) * width],
                                                   src[:, q * width:(q + 1) * width],
                                                   rs[:rows, i * parts + q:i * parts + q + 1], None, ALU.mult)
                last.then_inc(scaled, 1)

            def take(i):
                _, rows, col = tiles[i]
                for b in range(2):
                    dve.wait_ge(turned, 2 * i + b + 1)
                    src = K.bank[2 * (i % 2) + b][:, :].rearrange("p (k n) -> p k n", k=4)[:, :, 0:rows]
                    nc.vector.tensor_tensor(dst[:, 4 * b:4 * b + 4, col:col + rows], src,
                                            gain[:, 4 * b:4 * b + 4].unsqueeze(2).to_broadcast([P, 4, rows]),
                                            ALU.mult).then_inc(taken, 1)

            scale(0)
            for i in range(n):
                if i + 1 < n:
                    scale(i + 1)
                take(i)
            if extra and "vector" in extra:
                extra["vector"](dve)

        @block.tensor
        def _(pe):
            for i, (_, rows, _) in enumerate(tiles):
                pe.wait_ge(scaled, i + 1)
                for b in range(2):
                    if i >= 2:
                        pe.wait_ge(taken, 2 * (i - 2) + b + 1)
                    for k in range(4):
                        last = nc.tensor.transpose(K.bank[2 * (i % 2) + b][:, k * P:k * P + rows],
                                                   xn[:rows, i % 2, (4 * b + k) * P:(4 * b + k + 1) * P],
                                                   K.ident[:rows, :rows])
                    last.then_inc(turned, 1)
            if extra and "tensor" in extra:
                extra["tensor"](pe)


def x_tiles(K):
    return [(K.X[:rows_of(t), t, :], rows_of(t), t * P) for t in range(TILES)]


def x_loads(K, I):
    return [(K.X[:rows_of(t), t, :], I["x_prompt"][t] if t < TILES - 1 else I["x_sample"]) for t in range(TILES)]


def feature_major(nc, K, tag, w_dram, chunks, ring, src, cols, dst, extra=None):
    S = K.sem
    came = [S(f"{tag}_w{u}") for u in range(2)]
    done = [S(f"{tag}_product{u}") for u in range(2)]
    taken = [S(f"{tag}_taken{u}") for u in range(2)]
    K.fm_taken = taken
    pieces = [(a, min(a + FREE3, cols)) for a in range(0, cols, FREE3)]
    with nc.Block() as block:
        @block.sync
        def _(sp):
            for c in range(chunks):
                u = c % 2
                if c >= 2:
                    sp.wait_ge(done[u], c // 2)
                sp.dma_start(ring[:, u], w_dram[c]).then_inc(came[u], 16)
                if extra and ("sync", c) in extra:
                    extra["sync", c](sp)
            if extra and "sync" in extra:
                extra["sync"](sp)

        @block.tensor
        def _(pe):
            with pe.Fori(0, chunks // 2) as i:
                for u in range(2):
                    pe.wait_ge(came[u], i * 16 + 16)
                    pe.wait_ge(taken[u], i + 1)
                    for s, (a, b) in enumerate(pieces):
                        for k in range(KD):
                            last = nc.tensor.matmul(K.bank[3 * u + s][:, 0:b - a], ring[:, u, k, :], src[:, k, a:b],
                                                    start=k == 0, stop=k == KD - 1)
                    last.then_inc(done[u], 1)

        @block.scalar
        def _(act):
            for u in range(2):
                act.sem_inc(taken[u], 1)
            with act.Fori(0, chunks // 2) as i:
                for u in range(2):
                    act.wait_ge(done[u], i + 1)
                    for s, (a, b) in enumerate(pieces):
                        last = nc.scalar.activation(dst[:, bass.ds(i * 2 + u, 1), a:b].rearrange("p c n -> p (c n)"),
                                                    K.bank[3 * u + s][:, 0:b - a], ACT.Copy)
                    last.then_inc(taken[u], 1)


def projection_weights(K, tag, w_dram):
    w = K.big[:, O_W:O_W + KD * D].rearrange("p (h k n) -> p h k n", h=2, k=KD)
    came = [K.sem(f"{tag}_w{h}") for h in range(2)]

    def load(sp):
        for h in range(2):
            sp.dma_start(w[:, h], w_dram[h]).then_inc(came[h], 16)

    return w, came, load


def project_norm(nc, K, tag, weights, src, gain, dst, scratch, before=None, sync=None, split=None, x_came=None):
    S = K.sem
    w, came, _ = weights
    n = TILES
    done, added, squares, link_sem = S(f"{tag}_product"), S(f"{tag}_added"), S(f"{tag}_squares"), S(f"{tag}_dve")
    std2, scaled2, turned2, taken2 = S(f"{tag}_std"), S(f"{tag}_scaled"), S(f"{tag}_turned"), S(f"{tag}_taken")
    std1, scaled1, turned1, taken1 = S(f"{tag}_pre_std"), S(f"{tag}_pre_scaled"), S(f"{tag}_pre_turned"), S(f"{tag}_pre_taken")
    square = scratch[:, 0:D]
    xn2 = scratch[:, D:2 * D]
    xn1 = scratch[:, 2 * D:4 * D].rearrange("p (b n) -> p b n", b=2) if before else None
    ss, std, rs = (K.stat[:, i, :] for i in range(3))
    if split:
        high, low, whole = split
        high_made, low_made = S(f"{tag}_high"), S(f"{tag}_low")

    with nc.Block() as block:
        @block.sync
        def _(sp):
            if sync:
                sync(sp, added)

        @block.tensor
        def _(pe):
            def turn(x, r, bank, ready, taken, turned, t):
                pe.wait_ge(ready, t + 1)
                for b in range(2):
                    if t:
                        pe.wait_ge(taken, 2 * (t - 1) + b + 1)
                    for k in range(4):
                        last = nc.tensor.transpose(K.bank[bank + b][:, k * P:k * P + r], x[:r, (4 * b + k) * P:(4 * b + k + 1) * P],
                                                   K.ident[:r, :r])
                    last.then_inc(turned, 1)

            turn1 = lambda t: turn(xn1[:, t % 2], rows_of(t), 4, scaled1, taken1, turned1, t)
            turn2 = lambda t: turn(xn2, rows_of(t), 6, scaled2, taken2, turned2, t)
            if before:
                turn1(0)
                turn1(1)
            for t in range(n):
                r = rows_of(t)
                if before:
                    pe.wait_ge(taken1, 2 * t + 2)
                for h in range(2):
                    if t == 0:
                        pe.wait_ge(came[h], 16)
                    if t >= 2:
                        pe.wait_ge(added, 2 * (t - 2) + h + 1)
                    for k in range(KD):
                        last = nc.tensor.matmul(K.bank[2 * (t % 2) + h][:r, :], src[:, k, t * P:t * P + r], w[:, h, k, :],
                                                start=k == 0, stop=k == KD - 1)
                    last.then_inc(done, 1)
                if t >= 1:
                    turn2(t - 1)
                if before and t + 2 < n:
                    turn1(t + 2)
            turn2(n - 1)

        @block.scalar
        def _(act):
            count = [0]

            def square_sum(x, r, at):
                if count[0]:
                    act.wait_ge(squares, count[0])
                nc.scalar.activation(square[:r, 0:x.shape[1]], x, ACT.Square, accum_out=ss[:r, at:at + 1]).then_inc(squares, 1)
                count[0] += 1

            def halves(t):
                x, r, _ = before[0][t]
                for q in range(2):
                    square_sum(x[:, q * DA:(q + 1) * DA], r, 2 * t + q)

            def root(r, a, b, width, ready):
                act.wait_ge(squares, count[0])
                nc.scalar.activation(std[:r, a:b], ss[:r, a:b], ACT.Sqrt, bias=K.eps[:r, 0:1], scale=1.0 / width).then_inc(ready, 1)

            def high_part(t):
                r = rows_of(t)
                for b in range(2):
                    act.wait_ge(taken2, 2 * t + b + 1)
                    nc.scalar.activation(high[:, 4 * b:4 * b + 4, t * P:t * P + r], whole[:, t % 2, 4 * b:4 * b + 4, 0:r],
                                         ACT.Copy).then_inc(high_made, 1)

            if before:
                for t in range(3):
                    halves(t)
                root(P, 0, 6, DA, std1)
            for t in range(n):
                r = rows_of(t)
                if before and t + 3 < n:
                    halves(t + 3)
                act.wait_ge(added, 2 * t + 2)
                square_sum(K.X[:r, t, :], r, 2 * n + t)
                root(r, 2 * n + t, 2 * n + t + 1, D, std2)
                if before and t + 3 < n:
                    root(rows_of(t + 3), 2 * t + 6, 2 * t + 8, DA, std1)
                if split and t >= 1:
                    high_part(t - 1)
            if split:
                high_part(n - 1)

        @block.gpsimd
        def _(pool):
            if split:
                for t in range(n):
                    r = rows_of(t)
                    for b in range(2):
                        pool.wait_ge(high_made, 2 * t + b + 1)
                        at = (slice(None), slice(4 * b, 4 * b + 4), slice(t * P, t * P + r))
                        nc.gpsimd.tensor_tensor(low[at], whole[:, t % 2, 4 * b:4 * b + 4, 0:r], high[at],
                                                ALU.subtract).then_inc(low_made, 1)

        @block.vector
        def _(dve):
            link = Chain(dve, link_sem)

            def scale1(t):
                x, r, _ = before[0][t]
                if t >= 2:
                    dve.wait_ge(turned1, 2 * (t - 1))
                for q in range(2):
                    last = nc.vector.tensor_scalar(xn1[:r, t % 2, q * DA:(q + 1) * DA], x[:, q * DA:(q + 1) * DA],
                                                   rs[:r, 2 * t + q:2 * t + q + 1], None, ALU.mult)
                last.then_inc(scaled1, 1)

            def take(t, bank, g, turned, taken, to):
                r = rows_of(t)
                for b in range(2):
                    dve.wait_ge(turned, 2 * t + b + 1)
                    nc.vector.tensor_tensor(to[:, 4 * b:4 * b + 4, :], K.bank[bank + b][:, :].rearrange("p (k n) -> p k n", k=4)[:, :, 0:r],
                                            g[:, 4 * b:4 * b + 4].unsqueeze(2).to_broadcast([P, 4, r]), ALU.mult).then_inc(taken, 1)

            def take1(t):
                take(t, 4, before[1], turned1, taken1, src[:, :, t * P:t * P + rows_of(t)])

            def take2(t):
                r = rows_of(t)
                if split and t >= 2:
                    dve.wait_ge(low_made, 2 * (t - 1))
                take(t, 6, gain, turned2, taken2, whole[:, t % 2, :, 0:r] if split else dst[:, :, t * P:t * P + r])

            if before:
                dve.wait_ge(std1, 1)
                link(nc.vector.reciprocal(rs[:, 0:6], std[:, 0:6]))
                scale1(0)
                scale1(1)
                take1(0)
                scale1(2)
                take1(1)
            if x_came:
                dve.wait_ge(x_came, 16 * n)
            for t in range(n):
                r = rows_of(t)
                for h in range(2):
                    x = K.X[:r, t, h * 512:(h + 1) * 512]
                    dve.wait_ge(done, 2 * t + h + 1)
                    nc.vector.tensor_tensor(x, K.bank[2 * (t % 2) + h][:r, :], x, ALU.add).then_inc(added, 1)
                if t >= 1:
                    take2(t - 1)
                if before and t + 2 < n:
                    take1(t + 2)
                dve.wait_ge(std2, t + 1)
                link(nc.vector.reciprocal(rs[:r, 2 * n + t:2 * n + t + 1], std[:r, 2 * n + t:2 * n + t + 1]))
                dve.wait_ge(added, 2 * t + 2)
                nc.vector.tensor_scalar(xn2[:r, :], K.X[:r, t, :], rs[:r, 2 * n + t:2 * n + t + 1], None, ALU.mult).then_inc(scaled2, 1)
                if before and t + 3 < n:
                    dve.wait_ge(std1, t + 2)
                    q = rows_of(t + 3)
                    link(nc.vector.reciprocal(rs[:q, 2 * t + 6:2 * t + 8], std[:q, 2 * t + 6:2 * t + 8]))
                    scale1(t + 3)
            take2(n - 1)


def gather(sp, K, half, to, of, came):
    regs = K.page_regs = K.page_regs or [sp.alloc_register(f"page{b}") for b in range(NPAGE)]
    with sp.Fori(0, NS // 2) as n:
        sp.load(regs, K.page_table[0:1, bass.ds(n * NPAGE + half * (NS // 2) * NPAGE, NPAGE)])
        pages = [sp.snap(r, min_val=0, max_val=K.n_pool - 1) for r in regs]
        for b, page in enumerate(pages):
            sp.dma_start(to(n * NPAGE + b), of(page)).then_inc(came, 16)


def gather_cmp(sp, I, K, v, half, slot):
    pages = K.slot[slot].rearrange("p (g t) -> p g t", g=2)
    gather(sp, K, half, lambda pg: pages[:, :, bass.ds(pg * (PAGE // 2), PAGE // 2)],
           lambda page: I["pool_cmp"][v][bass.ds(page, 1)].rearrange("a p g t -> (a p) g t"), K.slot_came[slot])


def gather_sel(sp, I, K, name, half, slot):
    gather(sp, K, half, lambda pg: K.slot[slot][:, bass.ds(pg * P, P)],
           lambda page: I[name][bass.ds(page, 1)].rearrange("a p t -> (a p) t"), K.slot_came[slot])


SLOT_PAGES = 16 * NS * NPAGE // 2


def gating_operands(K, I):
    tmp = K.top[:, O_TMP:O_TMP + 2 * D]
    cp = K.top[:, O_CP:O_CP + 1720]
    ws = tmp[:, 2 * DA:].rearrange("p (g t) -> p g t", g=AG)
    wss = cp[:, 512:768].rearrange("p (g t) -> p g t", g=AG)
    return [(tmp[:, 0:DA], I["ln_v_g"].to_broadcast([P, DA])), (tmp[:, DA:2 * DA], I["ln_v_b"].to_broadcast([P, DA])),
            (ws, I["ws_t"]), (wss[:SROWS], I["ws_s"]), (cp[:, 768:776], I["bs_t"]), (cp[:SROWS, 776:784], I["bs_s"]),
            (cp[:, 784:912], I["causal"]), (cp[:SROWS, 912:944], I["causal_s"]), (cp[:, 990:991], I["cmp_valid"])]


def gating_phase(nc, K, I, O):
    S = K.sem
    p_done, uv_taken, rest_taken = S("in_product"), S("in_uv_taken"), S("in_rest_taken")
    a_chain, sd_ready, v_ready, v_chain = S("in_act"), S("in_sd"), S("in_v_ready"), S("in_dve")
    mixed, mixed_used, masked, a_out = S("in_mixed"), S("in_mixed_used"), S("in_ws_masked"), S("in_out")
    sig, gd = S("in_sigmoid"), K.gating_sem
    w = K.big[:, O_W:O_W + KD * TMW].rearrange("p (k n) -> p k n", k=KD)
    tmp = K.top[:, O_TMP:O_TMP + 2 * D]
    lng, lnb = tmp[:, 0:DA], tmp[:, DA:2 * DA]
    ws = tmp[:, 2 * DA:].rearrange("p (g t) -> p g t", g=AG)
    cp = K.top[:, O_CP:O_CP + 1720]
    junk, wss = cp[:, 0:512], cp[:, 512:768].rearrange("p (g t) -> p g t", g=AG)
    bs, bss = cp[:, 768:776], cp[:, 776:784]
    caus, causs = cp[:, 784:912], cp[:, 912:944]
    nm, sq, sd, rsd, sv = (cp[:, 944 + 9 * i:953 + 9 * i] for i in range(5))
    valid = cp[:, 990:991]
    cuts = [(0, DA), (DA, 2 * DA), (2 * DA, TMW)]

    with nc.Block() as block:
        @block.sync
        def _(sp):
            sp.wait_ge(v_ready, TILES)
            sp.dma_start(O["gmlp_v"], K.M[:SROWS, TILES - 1, DA:D]).then_inc(K.out_sem, 16)
            sp.wait_ge(rest_taken, 2 * TILES)
            sp.dma_start(O["vt"].rearrange("t p n -> p t n"), K.VT[:, 0:8, :]).then_inc(K.out_sem, 16)
            sp.dma_start(O["vt_s"], K.VT[:SROWS, 8, :]).then_inc(K.out_sem, 16)
            sp.wait_ge(sig, 2)
            sp.dma_start(K.gates_dram, K.GT[:SROWS, 8, :]).then_inc(K.gates_sem, 16)
            sp.wait_ge(K.out_sem, 16 * K.outs(3))
            sp.wait_ge(K.gates_sem, 16)

        @block.tensor
        def _(pe):
            pe.wait_ge(K.wtm_sem, 16 * KD)
            pe.wait_ge(masked, 2)

            def gate(t):
                r = rows_of(t)
                pe.wait_ge(v_ready, t + 1)
                if t >= 2:
                    pe.wait_ge(mixed_used, t - 1)
                for g in range(AG):
                    lhs = ws[:, g, :] if r == P else wss[:SROWS, g, :]
                    last = nc.tensor.matmul(K.bank[6 + t % 2][:r, g * AGD:(g + 1) * AGD], lhs,
                                            K.M[:r, t, DA + g * AGD:DA + (g + 1) * AGD], start=True, stop=True)
                last.then_inc(mixed, 1)

            for t in range(TILES):
                r = rows_of(t)
                if t >= 2:
                    pe.wait_ge(uv_taken, 2 * (t - 1))
                    pe.wait_ge(rest_taken, 2 * (t - 1))
                for s, (a, b) in enumerate(cuts):
                    for k in range(KD):
                        last = nc.tensor.matmul(K.bank[3 * (t % 2) + s][:r, 0:b - a],
                                                K.HT[:, k, t * P:t * P + r], w[:, k, a:b],
                                                start=k == 0, stop=k == KD - 1)
                last.then_inc(p_done, 1)
                if t >= 1:
                    gate(t - 1)
            gate(TILES - 1)

        @block.scalar
        def _(act):
            link = Chain(act, a_chain)
            for t in range(TILES):
                r = rows_of(t)
                bank = 3 * (t % 2)
                act.wait_ge(p_done, t + 1)
                nc.scalar.activation(K.M[:r, t, 0:DA], K.bank[bank][:r, :], ACT.Gelu_apprx_tanh).then_inc(uv_taken, 1)
                nc.scalar.activation(K.M[:r, t, DA:D], K.bank[bank + 1][:r, :], ACT.Gelu_apprx_tanh,
                                     accum_out=sv[:r, t:t + 1]).then_inc(uv_taken, 1)
                act.wait_ge(uv_taken, 2 * (t + 1))
                link(nc.scalar.activation(nm[:r, t:t + 1], sv[:r, t:t + 1], ACT.Copy, scale=-1.0 / DA))
                link(nc.scalar.activation(junk[:r, :], K.M[:r, t, DA:D], ACT.Square, bias=nm[:r, t:t + 1],
                                          accum_out=sq[:r, t:t + 1]))
                nc.scalar.activation(sd[:r, t:t + 1], sq[:r, t:t + 1], ACT.Sqrt, bias=K.eps[:r, 0:1],
                                     scale=1.0 / DA).then_inc(sd_ready, 1)
            act.wait_ge(rest_taken, 2 * TILES)
            nc.scalar.activation(K.GT[:, 0:8, :], K.GT[:, 0:8, :], ACT.Sigmoid).then_inc(sig, 1)
            nc.scalar.activation(K.GT[:SROWS, 8, :], K.GT[:SROWS, 8, :], ACT.Sigmoid).then_inc(sig, 1)

        @block.vector
        def _(dve):
            link = Chain(dve, v_chain)
            dve.wait_ge(gd, 16 * len(gating_operands(K, I)))
            nc.vector.tensor_tensor(ws, ws, caus.unsqueeze(1).to_broadcast([P, AG, P]), ALU.mult).then_inc(masked, 1)
            nc.vector.tensor_tensor(wss[:SROWS], wss[:SROWS], causs[:SROWS].unsqueeze(1).to_broadcast([SROWS, AG, SROWS]),
                                    ALU.mult).then_inc(masked, 1)

            def gated(t):
                r = rows_of(t)
                b = bs if r == P else bss
                dve.wait_ge(mixed, t + 1)
                for g in range(AG):
                    u = K.M[:r, t, g * AGD:(g + 1) * AGD]
                    last = nc.vector.scalar_tensor_tensor(u, K.bank[6 + t % 2][:r, g * AGD:(g + 1) * AGD],
                                                          b[:r, g:g + 1], u, ALU.add, ALU.mult)
                last.then_inc(mixed_used, 1)

            for t in range(TILES):
                r = rows_of(t)
                bank = K.bank[3 * (t % 2) + 2]
                v = K.M[:r, t, DA:D]
                dve.wait_ge(p_done, t + 1)
                nc.vector.tensor_copy(K.VT[:r, t, :], bank[:r, 0:2 * KV]).then_inc(rest_taken, 1)
                nc.vector.tensor_copy(K.GT[:r, t, :], bank[:r, 2 * KV:2 * KV + 3 * H]).then_inc(rest_taken, 1)
                dve.wait_ge(sd_ready, t + 1)
                link(nc.vector.reciprocal(rsd[:r, t:t + 1], sd[:r, t:t + 1]))
                link(nc.vector.tensor_scalar(v, v, nm[:r, t:t + 1], rsd[:r, t:t + 1], ALU.add, ALU.mult))
                link(nc.vector.tensor_tensor(v, v, lng[:r, :], ALU.mult))
                nc.vector.tensor_tensor(v, v, lnb[:r, :], ALU.add).then_inc(v_ready, 1)
                if t >= 1:
                    gated(t - 1)
            gated(TILES - 1)
            dve.wait_ge(sig, 1)
            gt = K.GT[:, 0:8, :].rearrange("p t (h b) -> p h t b", b=3)
            for b in range(3):
                last = nc.vector.tensor_copy(K.GS[:, :, :, b], gt[:, :, :, b])
            link(last)
            link(nc.vector.tensor_scalar(K.GS[:, :, 0, 0], K.GS[:, :, 0, 0], valid, None, ALU.mult))


def compress_phase(nc, K, I):
    S = K.sem
    ar = K.big[:, O_HT:BIG]
    pages = [slot.rearrange("p (g t) -> p g t", g=2) for slot in K.slot]
    w1 = [ar[:, 8192 + 2048 * v:8192 + 2048 * (v + 1)].rearrange("p (q h) -> p q h", h=P) for v in range(2)]
    dein = [ar[:, 12288 + 1024 * v:12288 + 1024 * (v + 1)].rearrange("p (r t) -> p r t", r=2) for v in range(2)]
    own = [ar[:, 14336 + 1024 * v:14336 + 1024 * (v + 1)].rearrange("p (g t) -> p g t", g=2) for v in range(2)]
    hid = [ar[:, 16384 + 512 * u:16384 + 512 * (u + 1)] for u in range(2)]
    w2 = [ar[:, 17408 + 64 * v:17408 + 64 * (v + 1)] for v in range(2)]
    pe_t = [ar[:, 17536 + 16 * v:17536 + 16 * (v + 1)] for v in range(2)]
    b1, b2k, hb = ar[:, 17568:17570], ar[:, 17570:17571], ar[:, 17571:17573]
    b2v = ar[:, 17600:17728]
    came_w, came_w2, came_own, dei = S("cmp_w_came"), S("cmp_small_came"), S("cmp_own_came"), S("cmp_split")
    first, hidden, second, out, biased = S("cmp_first"), S("cmp_hidden"), S("cmp_second"), S("cmp_out"), S("cmp_bias")
    pe_w1 = S("cmp_pe_product")
    rounds = [(0, None), (1, None), (0, 0), (0, 1), (1, 0), (1, 1)]
    small = [(w2[v], I["w_cmp2"][v]) for v in range(2)] + [(pe_t[v], I["pe_cmp"][v]) for v in range(2)] + \
            [(b1, I["b_cmp1"]), (b2k, I["b2k"]), (b2v, I["b2v"].to_broadcast([P, P]))]

    with nc.Block() as block:
        @block.sync
        def _(sp):
            for v in range(2):
                sp.dma_start(w1[v], I["w_cmp1"][v]).then_inc(came_w, 16)
            for to, of in small:
                sp.dma_start(to, of).then_inc(came_w2, 16)
            sp.wait_ge(dei, 2)
            for v in range(2):
                for g in range(2):
                    for r in range(2):
                        sp.dma_start(own[v][64 * r:64 * r + 64, g, :], dein[v][64 * g:64 * g + 64, r, :]).then_inc(came_own, 16)
            for half in range(2):
                gather_cmp(sp, I, K, 1, half, 2 + half)
            sample_windows(sp, K, I, 0)
            sp.wait_ge(first, 3)
            gather_sel(sp, I, K, "pool_sel_k", 0, 0)
            sp.wait_ge(first, 4)
            gather_sel(sp, I, K, "pool_sel_v", 0, 1)
            sp.wait_ge(came_own, 128)

        @block.vector
        def _(dve):
            for v in range(2):
                nc.vector.tensor_copy(dein[v][:, :, :], K.FM[:, 4 + v, 0:SEQ].rearrange("p (t r) -> p r t", r=2)).then_inc(dei, 1)
            dve.wait_ge(came_w2, 16 * len(small))
            for v in range(2):
                dve.wait_ge(pe_w1, v + 1)
                nc.vector.tensor_tensor(hb[:, v:v + 1], K.bank[6][:, v:v + 1], b1[:, v:v + 1], ALU.add).then_inc(biased, 1)
            for n, (v, half) in enumerate(rounds):
                dve.wait_ge(second, n + 1)
                bank = K.bank[2 + n % 2]
                if v == 0 and half is None:
                    last = nc.vector.tensor_scalar(K.KCP[:, :], bank[:, 0:NCMP], b2k, None, ALU.add)
                elif v == 0:
                    last = nc.vector.tensor_scalar(K.KCS[:, 4 * half:4 * half + 4, :],
                                                   bank[:, 0:4 * NCMP].rearrange("p (n c) -> p n c", n=4), b2k, None, ALU.add)
                elif half is None:
                    last = nc.vector.tensor_tensor(K.VCP[:NCMP, :], bank[:NCMP, 0:P], b2v[:NCMP, :], ALU.add)
                else:
                    last = nc.vector.tensor_tensor(K.VCS[:NCMP, 4 * half:4 * half + 4, :],
                                                   bank[:NCMP, :].rearrange("p (n c) -> p n c", n=4),
                                                   b2v[:NCMP, :].unsqueeze(1).to_broadcast([NCMP, 4, P]), ALU.add)
                last.then_inc(out, 1)

        @block.scalar
        def _(act):
            act.wait_ge(biased, 2)
            for n, (v, half) in enumerate(rounds):
                m = 2 * NCMP if half is None else 8 * NCMP
                act.wait_ge(first, n + 1)
                if n >= 2:
                    act.wait_ge(second, n - 1)
                nc.scalar.activation(hid[n % 2][:, 0:m], K.bank[n % 2][:, 0:m], ACT.Gelu_apprx_tanh,
                                     bias=hb[:, v:v + 1]).then_inc(hidden, 1)

        @block.tensor
        def _(pe):
            pe.wait_ge(came_w, 32)
            pe.wait_ge(came_w2, 16 * len(small))
            for v in range(2):
                for q in range(16):
                    last = nc.tensor.matmul(K.bank[6][:, v:v + 1], w1[v][:, q, :], pe_t[v][:, q:q + 1],
                                            start=q == 0, stop=q == 15)
                last.then_inc(pe_w1, 1)
                pe.wait_ge(biased, v + 1)

            def hidden_rows(n):
                v, half = rounds[n]
                if half is None:
                    pe.wait_ge(came_own, 128)
                    src, m = own[v], 2 * NCMP
                else:
                    pe.wait_ge(K.slot_came[n - 2], SLOT_PAGES)
                    src, m = pages[n - 2], 8 * NCMP
                if n >= 2:
                    pe.wait_ge(hidden, n - 1)
                for q in range(16):
                    if half is None:
                        rhs = src[:, :, q:q + 8 * NCMP - 7:8]
                    else:
                        rhs = src.rearrange("p g (n t) -> p g n t", n=4)[:, :, :, q:q + 8 * NCMP - 7:8]
                    last = nc.tensor.matmul(K.bank[n % 2][:, 0:m], w1[v][:, q, :], rhs, start=q == 0, stop=q == 15)
                last.then_inc(first, 1)

            def rows(n):
                v, half = rounds[n]
                pe.wait_ge(hidden, n + 1)
                if n >= 2:
                    pe.wait_ge(out, n - 1)
                seqs = 1 if half is None else 4
                bank = K.bank[2 + n % 2]
                for g in range(2):
                    if v == 0:
                        last = nc.tensor.matmul(bank[64 * g:64 * g + 64, 0:seqs * NCMP], w2[0],
                                                hid[n % 2][:, g * seqs * NCMP:(g + 1) * seqs * NCMP], start=True, stop=True)
                    else:
                        for s in range(seqs):
                            at = (g * seqs + s) * NCMP
                            last = nc.tensor.matmul(bank[:NCMP, s * P + 64 * g:s * P + 64 * g + 64],
                                                    hid[n % 2][:, at:at + NCMP], w2[1], start=True, stop=True)
                last.then_inc(second, 1)

            for n in range(len(rounds)):
                hidden_rows(n)
                if n >= 1:
                    rows(n - 1)
            rows(len(rounds) - 1)


def sample_windows(sp, K, I, half):
    kw, vw = K.windows[half]
    sp.dma_start(kw, I["win_kt"][4 * half:4 * half + 4].rearrange("n p t -> p n t")).then_inc(K.windows_came[half], 16)
    for n in range(4):
        sp.dma_start(vw[:, n].rearrange("p (b c) -> p b c", b=4),
                     I["win_v"][4 * half + n].rearrange("(b p) c -> p b c", p=P)).then_inc(K.windows_came[half], 16)


def sample_attention(nc, K, I):
    S = K.sem
    ar = K.big[:, O_HT:BIG]
    SC = ar[:, 12288:12288 + 1664]
    SB = ar[:, 13952:13952 + 1664]
    PT = ar[:, 15616:15616 + 15 * P].rearrange("p (b n) -> p b n", b=15)
    a = 15616 + 15 * P
    tabq, dq, gm = ar[:, a:a + 128], ar[:, a + 128:a + 256], ar[:, a + 256:a + 384]
    mn = ar[:, a + 384:a + 512].rearrange("p (h n) -> p h n", h=2)
    qbd = ar[:, a + 512:a + 768].rearrange("p (n r) -> p n r", n=NS)
    OS = ar[:, a + 768:a + 896]
    ovl, mw, t4 = ar[:, a + 896:a + 913], ar[:, a + 914:a + 918], ar[:, a + 920:a + 928]
    gr = ar[:, a + 928:a + 934].rearrange("p (h b) -> p h b", h=2)
    imp, eq, jj = ar[:, a + 940:a + 957], ar[:, a + 960:a + 974], ar[:, a + 974:a + 988]
    st = ar[:, a + 990:a + 1010]
    PC = ar[:, a + 1020:a + 1020 + 63]
    assert a + 1083 <= BIG - O_HT
    c_sel, c_new, c_win, c_cmp, c_end = 0, 1024, 1088, 1600, 1663
    oh = SC
    came_c, zeroed, prep = S("sa_small_came"), S("sa_zeroed"), S("sa_prep")
    pb, bias_done, scores, taken = S("sa_bias_product"), S("sa_bias"), S("sa_scores"), S("sa_scores_taken")
    vch, ach, impt, impu, nmr, exps = S("sa_dve"), S("sa_act"), S("sa_pe_imp"), S("sa_imp_taken"), S("sa_max"), S("sa_exp")
    pready, turned, ptaken, pv, otaken, oscr = S("sa_probs"), S("sa_turned"), S("sa_pt"), S("sa_pv"), S("sa_o"), S("sa_o_dram")
    back = S("sa_o_back")
    consts = [(oh[:, 0:c_end], I["oh_s"]), (dq, I["dq"]), (gm, I["gmat"]), (mn, I["mask_new"]), (mw, I["mask_win"]),
              (ovl[:NCMP], I["overlap"]), (jj, I["jidx"])] + \
             [(t4[32 * q:32 * q + 32, :], I["rel_bias"]) for q in range(4)]
    blocks = [(i * P, P) for i in range(8)] + [(c_new, 32), (c_new + 32, 32)] + \
             [(c_win + i * P, P) for i in range(4)] + [(c_cmp, NCMP)]

    with nc.Block() as block:
        @block.sync
        def _(sp):
            for to, of in consts:
                sp.dma_start(to, of).then_inc(came_c, 16)
            for half in range(2):
                for n in range(4):
                    of = bass.AP(K.gates_dram.tensor, (half * 4 + n) * TS * 3 * H, [[3, H], [3 * H, TS], [1, 3]])
                    sp.dma_start(gr[32 * n:32 * n + 32, half, :], of).then_inc(came_c, 16)
            sample_windows(sp, K, I, 1)
            gather_sel(sp, I, K, "pool_sel_k", 1, 2)
            gather_sel(sp, I, K, "pool_sel_v", 1, 3)
            for half in range(2):
                sp.wait_ge(otaken, half + 1)
                for n in range(4):
                    for g in range(2):
                        to = bass.AP(K.o_dram.tensor, (half * 4 + n) * TS * DA + g * 256, [[HD, HPG], [DA, TS], [1, HD]])
                        sp.dma_start(to, OS[32 * n + 16 * g:32 * n + 16 * g + 16, 64 * g:64 * g + 64]).then_inc(oscr, 16)
            sp.wait_ge(oscr, 256)
            sp.dma_start(K.M[:SROWS, TILES - 1, DA:D], K.o_dram).then_inc(back, 16)
            sp.wait_ge(back, 16)

        @block.gpsimd
        def _(pool):
            nc.gpsimd.memset(qbd, 0.0).then_inc(zeroed, 1)

        @block.tensor
        def _(pe):
            pe.wait_ge(prep, 1)
            for i, (x, y) in enumerate([(0, 512), (512, 1024), (1024, 1536), (1536, c_end)]):
                last = nc.tensor.matmul(K.bank[i][:, 0:y - x], tabq, oh[:, x:y], start=True, stop=True)
            last.then_inc(pb, 1)
            pe.wait_ge(bias_done, 1)
            pe.wait_ge(prep, 3)
            for half in range(2):
                KS, VS = K.slot[2 * half], K.slot[2 * half + 1]
                KW, VW = K.windows[half]
                pe.wait_ge(K.slot_came[2 * half], 2 * SLOT_PAGES)
                pe.wait_ge(K.windows_came[half], 80)
                if half:
                    pe.wait_ge(otaken, half)
                for n in range(4):
                    s = 4 * half + n
                    rows = slice(32 * n, 32 * n + 32)
                    for i in range(2):
                        nc.tensor.matmul(K.bank[i][rows, :], qbd[:, s, :], KS[:, n * 1024 + 512 * i:n * 1024 + 512 * i + 512], start=True, stop=True)
                    nc.tensor.matmul(K.bank[2][rows, 0:32], qbd[:, s, :], K.FM[:, 6, SEQ:T], start=True, stop=True)
                    nc.tensor.matmul(K.bank[2][rows, 32:64], qbd[:, s, :], K.FM[:, 7, SEQ:T], start=True, stop=True)
                    nc.tensor.matmul(K.bank[3][rows, :], qbd[:, s, :], KW[:, n], start=True, stop=True)
                    last = nc.tensor.matmul(K.bank[2][rows, 64:64 + NCMP], qbd[:, s, :], K.KCS[:, s, :], start=True, stop=True)
                last.then_inc(scores, 1)
                pe.wait_ge(impu, 3 * half + 1)
                nc.tensor.transpose(K.bank[4][:NCMP, 0:P], PC, K.ident[:, :]).then_inc(impt, 1)
                pe.wait_ge(impu, 3 * half + 2)
                nc.tensor.matmul(K.bank[4][:, 128:128 + NSEL], PT[:NCMP, 0, :], ovl[:NCMP, :], start=True, stop=True).then_inc(impt, 1)
                pe.wait_ge(impu, 3 * half + 3)
                nc.tensor.matmul(K.bank[4][:, 160:160 + NSEL], gm, imp, start=True, stop=True).then_inc(impt, 1)
                pe.wait_ge(pready, half + 1)
                for i, (x, w) in enumerate(blocks):
                    b = i // 4
                    last = nc.tensor.transpose(K.bank[4 + b][:w, (i % 4) * P:(i % 4 + 1) * P], SC[:, x:x + w], K.ident[:, :])
                last.then_inc(turned, 1)
                pe.wait_ge(ptaken, half + 1)
                pe.wait_ge(K.slot_came[2 * half + 1], 2 * SLOT_PAGES)
                for n in range(4):
                    s = 4 * half + n
                    rows = slice(32 * n, 32 * n + 32)
                    for i, (x, w) in enumerate(blocks):
                        if i < 8:
                            v = VS[:, (n * 8 + i) * P:(n * 8 + i + 1) * P]
                        elif i < 10:
                            v = K.VT[:SROWS, TILES - 1, (i - 8) * KV:(i - 7) * KV]
                        elif i < 14:
                            v = VW[:, n, (i - 10) * P:(i - 9) * P]
                        else:
                            v = K.VCS[:NCMP, s, :]
                        last = nc.tensor.matmul(K.bank[0][rows, 0:P], PT[:w, i, rows], v, start=i == 0, stop=i == 14)
                last.then_inc(pv, 1)

        @block.vector
        def _(dve):
            link = Chain(dve, vch)
            dve.wait_ge(came_c, 16 * (len(consts) + 8))
            nc.vector.tensor_tensor(tabq.rearrange("p (n h q) -> p n h q", n=4, h=H),
                                    t4.unsqueeze(1).unsqueeze(3).to_broadcast([P, 4, H, 4]),
                                    dq.rearrange("p (n h q) -> p n h q", n=4, h=H), ALU.mult).then_inc(prep, 1)
            dve.wait_ge(zeroed, 1)
            for g in range(2):
                nc.vector.tensor_scalar(qbd[64 * g:64 * g + 64, :, 16 * g:16 * g + 16].rearrange("p n (h q) -> p n h q", h=4),
                                        K.FM[64 * g:64 * g + 64, 0:4, SEQ:T].rearrange("p h (n q) -> p n h q", n=NS),
                                        HD ** -0.5, None, ALU.mult).then_inc(prep, 1)
            dve.wait_ge(pb, 1)
            for i, (x, y) in enumerate([(0, 512), (512, 1024), (1024, 1536), (1536, c_end)]):
                last = nc.vector.tensor_copy(SB[:, x:y], K.bank[i][:, 0:y - x])
            link(last)
            link(nc.vector.tensor_tensor(SB[:, c_win:c_win + 4], SB[:, c_win:c_win + 4], mw, ALU.add))
            dve.sem_inc(bias_done, 1)
            for half in range(2):
                dve.wait_ge(scores, half + 1)
                if half:
                    dve.wait_ge(turned, half)
                nc.vector.tensor_tensor(SC[:, c_cmp:c_end], K.bank[2][:, 64:64 + NCMP], SB[:, c_cmp:c_end], ALU.add)
                nc.vector.tensor_tensor(SC[:, 0:512], K.bank[0][:, :], SB[:, 0:512], ALU.add)
                nc.vector.tensor_tensor(SC[:, 512:1024], K.bank[1][:, :], SB[:, 512:1024], ALU.add)
                nc.vector.tensor_tensor(SC[:, c_win:c_win + 512], K.bank[3][:, :], SB[:, c_win:c_win + 512], ALU.add)
                link(nc.vector.tensor_tensor(SC[:, c_new:c_new + 64], K.bank[2][:, 0:64], SB[:, c_new:c_new + 64], ALU.add))
                link(nc.vector.tensor_tensor(SC[:, c_new:c_new + 64], SC[:, c_new:c_new + 64], mn[:, half, :], ALU.add))
                link(nc.vector.tensor_reduce(st[:, 0:1], SC[:, c_cmp:c_end], AX.X, ALU.max, negate=True))
                dve.sem_inc(nmr, 1)
                dve.wait_ge(exps, 3 * half + 1)
                link(nc.vector.reciprocal(st[:, 4:5], st[:, 3:4]))
                link(nc.vector.tensor_scalar(PC, SC[:, c_cmp:c_end], st[:, 4:5], None, ALU.mult))
                dve.sem_inc(impu, 1)
                dve.wait_ge(impt, 3 * half + 1)
                link(nc.vector.tensor_copy(PT[:NCMP, 0, :], K.bank[4][:NCMP, 0:P]))
                dve.sem_inc(impu, 1)
                dve.wait_ge(impt, 3 * half + 2)
                link(nc.vector.tensor_copy(imp, K.bank[4][:, 128:128 + NSEL]))
                dve.sem_inc(impu, 1)
                dve.wait_ge(impt, 3 * half + 3)
                cand = K.bank[4][:, 161:175]
                link(nc.vector.tensor_reduce(st[:, 5:6], cand, AX.X, ALU.min))
                link(nc.vector.scalar_tensor_tensor(eq, cand, st[:, 5:6], jj, ALU.is_equal, ALU.mult))
                link(nc.vector.tensor_reduce(st[:, 6:7], eq, AX.X, ALU.max))
                link(nc.vector.tensor_scalar(eq, jj, st[:, 6:7], NEG, ALU.is_equal, ALU.mult))
                part = SC[:, SELB:15 * SELB].rearrange("p (b k) -> p b k", b=14)
                link(nc.vector.tensor_tensor(part, part, eq.unsqueeze(2).to_broadcast([P, 14, SELB]), ALU.add))
                nc.vector.tensor_reduce(st[:, 1:2], SC[:, 0:c_new + 32], AX.X, ALU.max, negate=True)
                link(nc.vector.tensor_reduce(st[:, 2:3], SC[:, c_new + 32:c_cmp], AX.X, ALU.max, negate=True))
                dve.sem_inc(nmr, 1)
                dve.wait_ge(exps, 3 * half + 3)
                nc.vector.tensor_copy(st[:, 8:9], st[:, 3:4])
                link(nc.vector.tensor_copy(st[:, 9:11], st[:, 11:13]))
                link(nc.vector.reciprocal(st[:, 14:17], st[:, 8:11]))
                link(nc.vector.tensor_tensor(st[:, 14:17], st[:, 14:17], gr[:, half, :], ALU.mult))
                nc.vector.tensor_scalar(SC[:, 0:c_new + 32], SC[:, 0:c_new + 32], st[:, 15:16], None, ALU.mult)
                nc.vector.tensor_scalar(SC[:, c_new + 32:c_cmp], SC[:, c_new + 32:c_cmp], st[:, 16:17], None, ALU.mult)
                nc.vector.tensor_scalar(SC[:, c_cmp:c_end], SC[:, c_cmp:c_end], st[:, 14:15], None, ALU.mult).then_inc(pready, 1)
                dve.wait_ge(turned, half + 1)
                for b in range(4):
                    if b < 2:
                        last = nc.vector.tensor_copy(PT[:, 4 * b:4 * b + 4, :], K.bank[4 + b][:, :].rearrange("p (b n) -> p b n", b=4))
                    elif b == 2:
                        nc.vector.tensor_copy(PT[:32, 8:10, :], K.bank[6][:32, 0:256].rearrange("p (b n) -> p b n", b=2))
                        last = nc.vector.tensor_copy(PT[:, 10:12, :], K.bank[6][:, 256:512].rearrange("p (b n) -> p b n", b=2))
                    else:
                        nc.vector.tensor_copy(PT[:, 12:14, :], K.bank[7][:, 0:256].rearrange("p (b n) -> p b n", b=2))
                        last = nc.vector.tensor_copy(PT[:NCMP, 14, :], K.bank[7][:NCMP, 256:384])
                last.then_inc(ptaken, 1)
                dve.wait_ge(pv, half + 1)
                if half:
                    dve.wait_ge(oscr, 128)
                nc.vector.tensor_copy(OS, K.bank[0][:, 0:P]).then_inc(otaken, 1)

        @block.scalar
        def _(act):
            for half in range(2):
                act.wait_ge(nmr, 2 * half + 1)
                nc.scalar.activation(SC[:, c_cmp:c_end], SC[:, c_cmp:c_end], ACT.Exp, bias=st[:, 0:1],
                                     accum_out=st[:, 3:4]).then_inc(exps, 1)
                act.wait_ge(nmr, 2 * half + 2)
                nc.scalar.activation(SC[:, 0:c_new + 32], SC[:, 0:c_new + 32], ACT.Exp, bias=st[:, 1:2],
                                     accum_out=st[:, 11:12]).then_inc(exps, 1)
                nc.scalar.activation(SC[:, c_new + 32:c_cmp], SC[:, c_new + 32:c_cmp], ACT.Exp, bias=st[:, 2:3],
                                     accum_out=st[:, 12:13]).then_inc(exps, 1)


def prompt_attention(nc, K, I):
    S = K.sem
    ar = K.big[:, O_HT:BIG]
    strips = [ar[:, 2560 * g:2560 * (g + 1)] for g in range(2)]
    qz = [ar[:, 5120 + 1024 * g:5120 + 1024 * (g + 1)] for g in range(2)]
    sc = [ar[:, 7168 + 1728 * b:7168 + 1728 * (b + 1)] for b in range(2)]
    pt = [ar[:, 10624 + 1792 * b:10624 + 1792 * (b + 1)].rearrange("p (b n) -> p b n", b=14) for b in range(2)]
    gh = [ar[:, 14208 + 24 * g:14208 + 24 * (g + 1)].rearrange("p (t b) -> p t b", b=3) for g in range(2)]
    sta = [ar[:, 14300 + 16 * b:14300 + 16 * (b + 1)] for b in range(2)]
    strip_came = [S(f"pa_strip{g}") for g in range(2)]
    zeroed, steps = S("pa_zeroed"), [S("pa_dve_steps"), S("pa_pe_steps")]
    q_ready = [S(f"pa_q{g}") for g in range(2)]
    scores, s_taken, negmax, exps = S("pa_scores"), S("pa_scores_taken"), S("pa_negmax"), S("pa_exp")
    probs, pv, o_taken, vch = S("pa_probs"), S("pa_pv"), S("pa_o_taken"), S("pa_dve")
    TB = 3
    turned = [S(f"pa_turned{b}") for b in range(TB)]
    t_taken = [S(f"pa_turned_taken{b}") for b in range(TB)]
    U = 16
    ORDER = [*range(8), *range(7, -1, -1)]
    CHAIN = 2 * U + 2

    def blocks(i):
        lo = max(0, i - 4)
        return [(b * P, P, 0, b) for b in range(i + 1)] + \
               [(1024 + (b - lo) * P, P, 1, b) for b in range(lo, i + 1)] + [(1664, NCMP, 2, 0)]

    groups, per = [], [0] * TB
    for u in range(U):
        bl = blocks(ORDER[u])
        mine = []
        for n, x in enumerate(range(0, len(bl), 4)):
            per[n % TB] += 1
            mine.append((n % TB, per[n % TB], bl[x:x + 4], x))
        groups.append(mine)

    with nc.Block() as block:
        @block.sync
        def _(sp):
            for j in range(4):
                for g in range(2):
                    h = j + 4 * g
                    if j:
                        sp.wait_ge(s_taken, (j - 1) * U + 8 * g + 9)
                    base = h * (VECS + VECW)
                    sp.dma_start(strips[g][:, 0:STRS], bass.AP(K.vec_dram.tensor, base, [[1, P], [1, STRS]])).then_inc(strip_came[g], 16)
                    sp.dma_start(strips[g][:, STRS:], bass.AP(K.vec_dram.tensor, base + VECS, [[1, P], [1, STRW]])).then_inc(strip_came[g], 16)
                if j == 0:
                    for to, of in x_loads(K, I):
                        sp.dma_start(to, of).then_inc(K.x_came, 16)

        @block.gpsimd
        def _(pool):
            nc.gpsimd.memset(qz[0][64:128, :], 0.0).then_inc(zeroed, 1)
            nc.gpsimd.memset(qz[1][0:64, :], 0.0).then_inc(zeroed, 1)

        @block.tensor
        def _(pe):
            pe.sem_inc(pv, 2)
            pe.wait_ge(zeroed, 2)

            def score(j, u):
                g, i = u // 8, ORDER[u]
                if u % 8 == 0:
                    pe.wait_ge(q_ready[g], j + 1)
                pe.wait_ge(s_taken, j * U + u + 1)
                q = qz[g][:, i * P:(i + 1) * P]
                w = (i + 1) * P
                for x in range(0, w, 512):
                    nc.tensor.matmul(K.ps4[:, x:min(x + 512, w)], q, K.FM[:, 6, x:min(x + 512, w)], start=True, stop=True)
                lo = max(0, i - 4) * P
                ww = w - lo
                for x in range(0, ww, 512):
                    y = min(x + 512, ww)
                    nc.tensor.matmul(K.ps4[:, 1024 + x:1024 + y], q, K.FM[:, 7, lo + x:lo + y], start=True, stop=True)
                nc.tensor.matmul(K.ps4[:, 1664:1664 + NCMP], q, K.KCP[:, :], start=True, stop=True).then_inc(scores, 1)

            def turn(j, u, group):
                b, cnt, bl, _ = group
                pe.wait_ge(t_taken[b], j * per[b] + cnt)
                if bl[0][1] < P:
                    pe.sem_inc(steps[1], 1)
                for x, (col, w, _, _) in enumerate(bl):
                    last = nc.tensor.transpose(K.bank[4 + b][:w, x * P:(x + 1) * P], sc[u % 2][:, col:col + w], K.ident[:, :])
                last.then_inc(turned[b], 1)

            def multiply(j, u, group):
                b, cnt, bl, first = group
                end = groups[u][-1] is group
                pe.wait_ge(t_taken[b], j * per[b] + cnt + 1)
                for x, (_, w, kind, t) in enumerate(bl):
                    v = K.VCP[:NCMP, :] if kind == 2 else K.VT[:, t, kind * KV:(kind + 1) * KV]
                    last = nc.tensor.matmul(K.bank[7][:, 0:P], pt[u % 2][:w, first + x, :], v,
                                            start=first + x == 0, stop=end and x == len(bl) - 1)
                if end:
                    last.then_inc(pv, 1)

            with pe.Fori(0, 4) as j:
                score(j, 0)
                score(j, 1)
                for u in range(U):
                    pe.wait_ge(probs, j * U + u + 1)
                    g = groups[u]
                    for group in g[:TB]:
                        turn(j, u, group)
                    pe.wait_ge(o_taken, j * U + u + 1)
                    for n, group in enumerate(g):
                        multiply(j, u, group)
                        if n + TB < len(g):
                            turn(j, u, g[n + TB])
                    if u + 2 < U:
                        score(j, u + 2)

        @block.vector
        def _(dve):
            dve.sem_inc(s_taken, 1)
            count = [0]

            def link(ins, j):
                count[0] += 1
                ins.then_inc(vch, 1)
                dve.wait_ge(vch, j * CHAIN + count[0])

            def add_bias(j, u):
                g, i = u // 8, ORDER[u]
                s, mx = sc[u % 2], sta[u % 2]
                if u % 8 == 0:
                    dve.wait_ge(strip_came[g], j * 32 + 32)
                dve.wait_ge(scores, j * U + u + 1)
                dve.wait_ge(pv, j * U + u + 1)
                dve.sem_inc(steps[0], 1)
                w = (i + 1) * P
                ww = min(i + 1, 5) * P
                at = 992 + P * i
                nc.vector.tensor_tensor_reduce(out=s[:, 0:w], in0=K.ps4[:, 0:w], in1=strips[g][:, 895 + w:895:-1], scale=1.0,
                                               scalar=-3e38, op0=ALU.add, op1=ALU.max, accum_out=mx[:, 1:2])
                nc.vector.tensor_tensor_reduce(out=s[:, 1024:1024 + ww], in0=K.ps4[:, 1024:1024 + ww],
                                               in1=strips[g][:, STRS + ww - 1:STRS - 1:-1], scale=1.0,
                                               scalar=-3e38, op0=ALU.add, op1=ALU.max, accum_out=mx[:, 2:3])
                nc.vector.tensor_tensor_reduce(out=s[:, 1664:1664 + NCMP], in0=K.ps4[:, 1664:1664 + NCMP],
                                               in1=strips[g][:, at:at - 16 * NCMP + 15:-16] if i else strips[g][:, at::-16], scale=1.0,
                                               scalar=-3e38, op0=ALU.add, op1=ALU.max, accum_out=mx[:, 0:1]).then_inc(s_taken, 1)
                dve.wait_ge(s_taken, j * U + u + 2)
                nc.vector.tensor_scalar(mx[:, 4:7], mx[:, 0:3], -1.0, None, ALU.mult).then_inc(negmax, 1)

            def gate(j, u):
                g, i = u // 8, ORDER[u]
                s, m = sc[u % 2], sta[u % 2]
                w = (i + 1) * P
                ww = min(i + 1, 5) * P
                dve.wait_ge(exps, j * 3 * U + 3 * u + 3)
                link(nc.vector.reciprocal(m[:, 12:15], m[:, 8:11]), j)
                link(nc.vector.tensor_tensor(m[:, 12:15], m[:, 12:15], gh[g][:, i, :], ALU.mult), j)
                nc.vector.tensor_scalar(s[:, 0:w], s[:, 0:w], m[:, 13:14], None, ALU.mult)
                nc.vector.tensor_scalar(s[:, 1024:1024 + ww], s[:, 1024:1024 + ww], m[:, 14:15], None, ALU.mult)
                nc.vector.tensor_scalar(s[:, 1664:1664 + NCMP], s[:, 1664:1664 + NCMP], m[:, 12:13], None, ALU.mult).then_inc(probs, 1)

            with dve.Fori(0, 4) as j:
                count[0] = 0
                for g in range(2):
                    src = K.FM[64 * g:64 * g + 64, bass.ds(j, 1), 0:SEQ].rearrange("p a n -> p (a n)")
                    nc.vector.tensor_scalar(qz[g][64 * g:64 * g + 64, :], src, HD ** -0.5, None, ALU.mult).then_inc(q_ready[g], 1)
                    link(nc.vector.tensor_copy(gh[g], K.GS[:, bass.ds(j + 4 * g, 1), :, :].rearrange("p a t b -> p (a t) b")), j)
                add_bias(j, 0)
                for u in range(U):
                    gate(j, u)
                    if u + 1 < U:
                        add_bias(j, u + 1)

        @block.scalar
        def _(act):
            for b in range(TB):
                act.sem_inc(t_taken[b], 1)
            act.sem_inc(o_taken, 1)

            def exp(j, u):
                i = ORDER[u]
                s, m = sc[u % 2], sta[u % 2]
                w = (i + 1) * P
                ww = min(i + 1, 5) * P
                act.wait_ge(negmax, j * U + u + 1)
                for b, x, y in ((1, 0, w), (2, 1024, 1024 + ww), (0, 1664, 1664 + NCMP)):
                    nc.scalar.activation(s[:, x:y], s[:, x:y], ACT.Exp, bias=m[:, 4 + b:5 + b],
                                         accum_out=m[:, 8 + b:9 + b]).then_inc(exps, 1)

            with act.Fori(0, 4) as j:
                exp(j, 0)
                for u in range(U):
                    g, i = u // 8, ORDER[u]
                    act.wait_ge(pv, j * U + u + 1)
                    for b, cnt, bl, x in groups[u]:
                        act.wait_ge(turned[b], j * per[b] + cnt)
                        full = [y for y in bl if y[1] == P]
                        if full:
                            last = nc.scalar.copy(pt[u % 2][:, x:x + len(full), :],
                                                  K.bank[4 + b][:, 0:len(full) * P].rearrange("p (b n) -> p b n", n=P))
                        if len(full) < len(bl):
                            last = nc.scalar.copy(pt[u % 2][:NCMP, x + len(full), :],
                                                  K.bank[4 + b][:NCMP, len(full) * P:(len(full) + 1) * P])
                        last.then_inc(t_taken[b], 1)
                    if u + 1 < U:
                        exp(j, u + 1)
                    act.wait_ge(pv, j * U + u + 3)
                    dst = K.M[:, i, bass.ds(j * HD + (DA + 4 * g * HD), HD)]
                    nc.scalar.activation(dst, K.bank[7][:, 64 * g:64 * g + 64], ACT.Copy).then_inc(o_taken, 1)


def bias_rows(nc, K, I):
    S = K.sem
    came, rows, out, product, set_ = S("bias_came"), S("bias_rows"), S("bias_dram"), S("bias_product"), S("bias_table")
    L = VECS + VECW
    oh = K.top[:BUCKETS + 1, O_M:O_M + L]
    vec = K.top[:H, O_M + L:O_M + 2 * L]
    cuts = [(x, min(x + 512, L)) for x in range(0, L, 512)]

    def sync(sp):
        sp.dma_start(oh, I["oh_v"]).then_inc(came, 16)
        sp.wait_ge(set_, 1)
        sp.dma_start(K.table[:BUCKETS, :], I["rel_bias"]).then_inc(came, 16)
        sp.dma_start(K.page_table[:, :], I["page_table"]).then_inc(came, 16)
        w = K.big[:, O_W:O_W + KD * TMW].rearrange("p (k n) -> p k n", k=KD)
        for k in range(KD):
            sp.dma_start(w[:, k, :], I["w_tm"][k]).then_inc(K.wtm_sem, 16)
        sp.wait_ge(rows, len(cuts))
        sp.dma_start(K.vec_dram, vec).then_inc(out, 16)
        sp.wait_ge(out, 16)
        sp.wait_ge(came, 48)

    def gpsimd(pool):
        nc.gpsimd.memset(K.table[:, :], NEG).then_inc(set_, 1)

    def tensor(pe):
        pe.wait_ge(came, 48)
        for n, (x, y) in enumerate(cuts):
            if n >= 2:
                pe.wait_ge(rows, n - 1)
            nc.tensor.matmul(K.bank[4 + n % 2][:H, 0:y - x], K.table[:, :], oh[:, x:y], start=True, stop=True).then_inc(product, 1)

    def scalar(act):
        for n, (x, y) in enumerate(cuts):
            act.wait_ge(product, n + 1)
            nc.scalar.activation(vec[:, x:y], K.bank[4 + n % 2][:H, 0:y - x], ACT.Copy).then_inc(rows, 1)

    return {"sync": sync, "gpsimd": gpsimd, "tensor": tensor, "scalar": scalar}


def memory_values(nc, K, I, O, memt, mkt, mv):
    S = K.sem
    came = [S(f"mv_w{h}") for h in range(2)]
    done, taken = S("mv_product"), S("mv_taken")
    w = K.big[:, O_W:O_W + KD * D].rearrange("p (h k n) -> p h k n", h=2, k=KD)
    with nc.Block() as block:
        @block.sync
        def _(sp):
            for h in range(2):
                sp.dma_start(w[:, h], I["w_mv"][h]).then_inc(came[h], 16)
            sp.dma_start(O["mem_k"], mkt).then_inc(K.out_sem, 16)
            sp.wait_ge(taken, 4)
            sp.dma_start(O["mem_v"].rearrange("t p n -> p t n"), mv).then_inc(K.out_sem, 16)
            K.outs(2)

        @block.tensor
        def _(pe):
            for j in range(4):
                h, t = j // 2, j % 2
                pe.wait_ge(came[h], 16)
                for k in range(KD):
                    last = nc.tensor.matmul(K.bank[j][:, :], memt[:, k, t * P:(t + 1) * P], w[:, h, k, :],
                                            start=k == 0, stop=k == KD - 1)
                last.then_inc(done, 1)

        @block.scalar
        def _(act):
            for j in range(4):
                h, t = j // 2, j % 2
                act.wait_ge(done, j + 1)
                nc.scalar.activation(mv[:, t, h * 512:(h + 1) * 512], K.bank[j][:, :], ACT.Copy).then_inc(taken, 1)


class CrossSample:

    def __init__(self, K):
        S = K.sem
        m, w = K.top[:, O_M:O_FM], K.big[:, O_W:BIG]
        fm = [K.top[:, O_FM + 2048 * i:O_FM + 2048 * (i + 1)] for i in range(4)]
        vt, tail, low, high = K.top[:, O_VT:O_VT + 2048], w[:, 8192:10240], m[:, 0:2048], m[:, 2048:4096]
        self.kr = [x.rearrange("p (c m) -> p c m", c=KD) for x in (low, high, tail, vt, m[:, 4096:6144], m[:, 6144:8192], low, high)]
        self.vr = [x.rearrange("p (m n) -> p m n", m=2) for x in (*fm, tail, vt, fm[0], fm[1])]
        self.qbd = K.top[:, O_TMP:O_TMP + 2048].rearrange("p (c n r) -> p c n r", c=KD, n=NS)
        self.tmp = K.top[:, O_TMP + 2048:O_TMP + 2048 + 1544]
        assert O_TMP + 2048 + 1544 <= TOP
        self.k_came, self.v_came = ([S(f"xs_{x}{n}") for n in range(NS)] for x in "kv")
        self.zeroed, self.q_ready = S("xs_zeroed"), S("xs_q")

    def load_keys(self, sp, I, n):
        sp.dma_start(self.kr[n], I["mem_kt"][n]).then_inc(self.k_came[n], 16)

    def load_values(self, sp, I, n):
        sp.dma_start(self.vr[n], I["mem_v"][n].rearrange("(m p) n -> p m n", p=P)).then_inc(self.v_came[n], 16)


def cross_prompt(nc, K, I, qx, mkt, mv, sample):
    S = K.sem
    w = K.big[:, O_W:BIG]
    px = [w[:, 1024 * b:1024 * (b + 1)].rearrange("p (h m) -> p h m", h=XH) for b in range(2)]
    pt = [w[:, 2048 + 1024 * b:2048 + 1024 * (b + 1)].rearrange("p (b n) -> p b n", b=8) for b in range(2)]
    st = [w[:, 4096 + 16 * b:4096 + 16 * (b + 1)] for b in range(2)]
    n = SEQ // P
    scores, neg, exps, probs = S("xp_scores"), S("xp_negmax"), S("xp_exp"), S("xp_probs")
    turned, taken, pv, o_taken, vch = S("xp_turned"), S("xp_turned_taken"), S("xp_pv"), S("xp_o_taken"), S("xp_dve")
    with nc.Block() as block:
        @block.sync
        def _(sp):
            for n in range(4):
                sample.load_keys(sp, I, n)

        @block.gpsimd
        def _(pool):
            nc.gpsimd.memset(sample.qbd, 0.0).then_inc(sample.zeroed, 1)

        @block.tensor
        def _(pe):
            def score(t):
                if t >= 2:
                    pe.wait_ge(exps, XH * (t - 1))
                for h in range(XH):
                    for k in range(2):
                        last = nc.tensor.matmul(K.bank[2 * (t % 2) + h // 2][:, (h % 2) * MEM:(h % 2 + 1) * MEM],
                                                qx[:, 2 * h + k, t * P:(t + 1) * P], mkt[:, 2 * h + k, :],
                                                start=k == 0, stop=k == 1)
                last.then_inc(scores, 1)

            score(0)
            for t in range(n):
                if t + 1 < n:
                    score(t + 1)
                pe.wait_ge(probs, t + 1)
                for b in range(2):
                    if t:
                        pe.wait_ge(taken, 2 * (t - 1) + b + 1)
                    for x in range(4):
                        h, m = 2 * b + x // 2, x % 2
                        last = nc.tensor.transpose(K.bank[4 + b][:, x * P:(x + 1) * P], px[t % 2][:, h, m * P:(m + 1) * P], K.ident[:, :])
                    last.then_inc(turned, 1)
                for b in range(2):
                    pe.wait_ge(taken, 2 * t + b + 1)
                    if t:
                        pe.wait_ge(o_taken, 2 * (t - 1) + b + 1)
                    for x in range(4):
                        c = 4 * b + x
                        h = c // 2
                        for m in range(2):
                            last = nc.tensor.matmul(K.bank[6 + b][:, x * P:(x + 1) * P], mv[:, m, c * P:(c + 1) * P],
                                                    pt[t % 2][:, 2 * h + m, :], start=m == 0, stop=m == 1)
                    last.then_inc(pv, 1)

        @block.vector
        def _(dve):
            link = Chain(dve, vch)

            def maxima(t):
                m = st[t % 2]
                dve.wait_ge(scores, t + 1)
                b = 2 * (t % 2)
                link(nc.vector.tensor_reduce(m[:, 0:4], K.ps[:, b * 512:(b + 2) * 512].rearrange("p (h m) -> p h m", h=XH),
                                             AX.X, ALU.max))
                nc.vector.tensor_scalar(m[:, 4:8], m[:, 0:4], -(XHD ** -0.5), None, ALU.mult).then_inc(neg, 1)

            maxima(0)
            dve.wait_ge(sample.zeroed, 1)
            for c in range(KD):
                nc.vector.tensor_copy(sample.qbd[:, c, :, 4 * (c // 2):4 * (c // 2) + 4],
                                      qx[:, c, SEQ:T].rearrange("p (n q) -> p n q", n=NS)).then_inc(sample.q_ready, 1)
            for t in range(n):
                if t + 1 < n:
                    maxima(t + 1)
                m = st[t % 2]
                dve.wait_ge(exps, XH * (t + 1))
                link(nc.vector.reciprocal(m[:, 12:16], m[:, 8:12]))
                nc.vector.tensor_tensor(px[t % 2], px[t % 2], m[:, 12:16].unsqueeze(2).to_broadcast([P, XH, MEM]),
                                        ALU.mult).then_inc(probs, 1)
                for b in range(2):
                    dve.wait_ge(turned, 2 * t + b + 1)
                    if t >= 2:
                        dve.wait_ge(pv, 2 * (t - 1))
                    nc.vector.tensor_copy(pt[t % 2][:, 4 * b:4 * b + 4, :],
                                          K.bank[4 + b][:, :].rearrange("p (b n) -> p b n", b=4)).then_inc(taken, 1)

        @block.scalar
        def _(act):
            def exp(t):
                m = st[t % 2]
                act.wait_ge(neg, t + 1)
                if t >= 2:
                    act.wait_ge(turned, 2 * (t - 1))
                for h in range(XH):
                    nc.scalar.activation(px[t % 2][:, h, :], K.bank[2 * (t % 2) + h // 2][:, (h % 2) * MEM:(h % 2 + 1) * MEM],
                                         ACT.Exp, bias=m[:, 4 + h:5 + h], scale=XHD ** -0.5,
                                         accum_out=m[:, 8 + h:9 + h]).then_inc(exps, 1)

            exp(0)
            for t in range(n):
                if t + 1 < n:
                    exp(t + 1)
                for b in range(2):
                    act.wait_ge(pv, 2 * t + b + 1)
                    nc.scalar.activation(K.HT[:, 4 * b:4 * b + 4, t * P:(t + 1) * P],
                                         K.bank[6 + b][:, :].rearrange("p (c n) -> p c n", c=4), ACT.Copy).then_inc(o_taken, 1)


def cross_sample(nc, K, I, sample, weights):
    S = K.sem
    kr, vr, qbd, tmp, k_came, v_came = sample.kr, sample.vr, sample.qbd, sample.tmp, sample.k_came, sample.v_came
    px, pt, ox, st = tmp[:, 0:256], tmp[:, 256:512].rearrange("p (m r) -> p m r", m=2), tmp[:, 512:1536], tmp[:, 1536:1544]
    scores, k_used = S("xs_scores"), S("xs_keys_used")
    neg, exps, probs, turned, taken = S("xs_negmax"), S("xs_exp"), S("xs_probs"), S("xs_turned"), S("xs_turned_taken")
    pv, o_taken, o_turned, o_done, vch = S("xs_pv"), S("xs_o_taken"), S("xs_o_turned"), S("xs_o_done"), S("xs_dve")
    with nc.Block() as block:
        @block.sync
        def _(sp):
            for n in range(4):
                sample.load_values(sp, I, n)
            sample.load_keys(sp, I, 4)
            sample.load_keys(sp, I, 5)
            for n in range(2):
                sp.wait_ge(k_used, n + 1)
                sample.load_keys(sp, I, 6 + n)
            for n in range(2):
                sp.wait_ge(k_used, n + 3)
                sample.load_values(sp, I, 4 + n)
            for n in range(2):
                sp.wait_ge(pv, n + 1)
                sample.load_values(sp, I, 6 + n)
            weights[2](sp)

        @block.tensor
        def _(pe):
            pe.wait_ge(sample.q_ready, KD)
            for half in range(2):
                if half:
                    pe.wait_ge(exps, half)
                for x in range(4):
                    n = 4 * half + x
                    pe.wait_ge(k_came[n], 16)
                    for c in range(KD):
                        last = nc.tensor.matmul(K.bank[0][32 * x:32 * x + 32, 0:MEM], qbd[:, c, n, :], kr[n][:, c, :],
                                                start=c == 0, stop=c == KD - 1)
                    last.then_inc(k_used, 1)
                pe.wait_ge(probs, half + 1)
                for m in range(2):
                    last = nc.tensor.transpose(K.bank[1][:, m * P:(m + 1) * P], px[:, m * P:(m + 1) * P], K.ident[:, :])
                last.then_inc(turned, 1)
                pe.wait_ge(taken, half + 1)
                for x in range(4):
                    n = 4 * half + x
                    pe.wait_ge(v_came[n], 16)
                    for b in range(2):
                        for m in range(2):
                            last = nc.tensor.matmul(K.bank[2 + b][32 * x:32 * x + 32, :], pt[:, m, 32 * x:32 * x + 32],
                                                    vr[n][:, m, b * 512:(b + 1) * 512], start=m == 0, stop=m == 1)
                    last.then_inc(pv, 1)
                pe.wait_ge(o_taken, half + 1)
                for c in range(KD):
                    last = nc.tensor.transpose(K.bank[4 + c // 4][:, (c % 4) * P:(c % 4 + 1) * P], ox[:, c * P:(c + 1) * P], K.ident[:, :])
                last.then_inc(o_turned, 1)

        @block.vector
        def _(dve):
            link = Chain(dve, vch)
            for half in range(2):
                dve.wait_ge(k_used, 4 * half + 4)
                link(nc.vector.tensor_reduce(st[:, 0:1], K.bank[0][:, 0:MEM], AX.X, ALU.max))
                nc.vector.tensor_scalar(st[:, 1:2], st[:, 0:1], -(XHD ** -0.5), None, ALU.mult).then_inc(neg, 1)
                dve.wait_ge(exps, half + 1)
                link(nc.vector.reciprocal(st[:, 3:4], st[:, 2:3]))
                nc.vector.tensor_scalar(px, px, st[:, 3:4], None, ALU.mult).then_inc(probs, 1)
                dve.wait_ge(turned, half + 1)
                nc.vector.tensor_copy(pt, K.bank[1][:, 0:2 * P].rearrange("p (m r) -> p m r", m=2)).then_inc(taken, 1)
                dve.wait_ge(pv, 4 * half + 4)
                nc.vector.tensor_copy(ox, K.ps[:, 1024:2048]).then_inc(o_taken, 1)
                dve.wait_ge(o_turned, half + 1)
                for c in range(KD):
                    src = K.bank[4 + c // 4][:, (c % 4) * P:(c % 4 + 1) * P].rearrange("p (n r) -> p n r", n=4)[:, :, 4 * (c // 2):4 * (c // 2) + 4]
                    last = nc.vector.tensor_copy(K.HT[:, c, SEQ + 16 * half:SEQ + 16 * half + 16].rearrange("p (n q) -> p n q", n=4), src)
                link(last)

        @block.scalar
        def _(act):
            for half in range(2):
                act.wait_ge(neg, half + 1)
                if half:
                    act.wait_ge(turned, half)
                nc.scalar.activation(px, K.bank[0][:, 0:MEM], ACT.Exp, bias=st[:, 1:2], scale=XHD ** -0.5,
                                     accum_out=st[:, 2:3]).then_inc(exps, 1)


def ffn_up(nc, K, I, O, mem, actt, high, low, landing, w_came):
    S = K.sem
    sb = lambda name, shape, dt=F32: mem.enter_context(nc.sbuf_tensor(name, shape, dt))
    w_high, w_low = sb("ff_weights_high", [P, 2, KD, P], F32R), sb("ff_weights_low", [P, 2, KD, P], F32R)
    ext = [sb(f"ff_row{u}", [P, 1074])[:, :] for u in range(2)]
    ct = [sb(f"ff_conv{u}", [P, T])[:, :] for u in range(2)]
    cpt = sb("ff_small", [P, 848])
    prev = cpt[:, 0:FC * 16].rearrange("p (c n) -> p c n", c=FC)
    co = cpt[:, 352:352 + FC * 18].rearrange("p (c n) -> p c n", c=FC)
    cwb = cpt[:, 752:752 + FC * 4].rearrange("p (c n) -> p c n", c=FC)
    cw = [cpt[:, 840 + 4 * u:844 + 4 * u] for u in range(2)]
    w_split, low_done = ([S(f"ff_{s}_{x}") for s in ("up", "gate")] for x in ("high", "low"))
    small, zeroed = S("ff_small_came"), S("ff_zeroed")
    up_done, gate_done, up_taken, gate_taken = S("ff_up"), S("ff_gate"), S("ff_up_taken"), S("ff_gate_taken")
    conv_done, gelu_done, vch = S("ff_conv"), S("ff_gelu"), S("ff_dve")
    pieces = [(0, FREE3), (FREE3, 2 * FREE3), (2 * FREE3, T)]
    LINKS = 7

    with nc.Block() as block:
        @block.sync
        def _(sp):
            sp.dma_start(prev, I["conv_prev"]).then_inc(small, 16)
            sp.dma_start(cwb, I["conv_wb"]).then_inc(small, 16)
            for c in range(1, FC):
                for x, name in enumerate(("w_up", "w_gate")):
                    sp.wait_ge(low_done[x], c)
                    sp.dma_start(landing[:, x], I[name][c]).then_inc(w_came[x], 16)
            sp.wait_ge(conv_done, FC + 2)
            sp.dma_start(O["conv"], co).then_inc(K.out_sem, 16)
            K.outs(1)

        @block.gpsimd
        def _(pool):
            for u in range(2):
                nc.gpsimd.memset(ext[u][:, 0:2], 0.0).then_inc(zeroed, 1)
            with pool.Fori(0, FC) as c:
                for x in range(2):
                    pool.wait_ge(w_split[x], c + 1)
                    nc.gpsimd.tensor_tensor(w_low[:, x], landing[:, x], w_high[:, x], ALU.subtract).then_inc(low_done[x], 1)

        @block.tensor
        def _(pe):
            with pe.Fori(0, FC // 2) as i:
                for u in range(2):
                    for s, (done, taken) in enumerate(((up_done, up_taken), (gate_done, gate_taken))):
                        pe.wait_ge(low_done[s], i * 2 + u + 1)
                        pe.wait_ge(taken, i * 2 + u + 1)
                        for x, (a, b) in enumerate(pieces):
                            for k in range(KD):
                                for n, (w, h) in enumerate(((w_high, high), (w_high, low), (w_low, high))):
                                    last = nc.tensor.matmul(K.bank[3 * s + x][:, 0:b - a], w[:, s, k, :], h[:, k, a:b],
                                                            start=k + n == 0, stop=k == KD - 1 and n == 2)
                        last.then_inc(done, 1)

        @block.scalar
        def _(act):
            act.sem_inc(up_taken, 1)

            def high_part(s, c):
                act.wait_ge(w_came[s], c * 16 + 16)
                nc.scalar.activation(w_high[:, s], landing[:, s], ACT.Copy).then_inc(w_split[s], 1)

            def chunk(i, u, more):
                act.wait_ge(up_done, i * 2 + u + 1)
                if more:
                    high_part(0, i * 2 + (u + 1))
                act.wait_ge(conv_done, i * 2 + u + 1)
                nc.scalar.activation(ext[u][:, 2:2 + FREE3], K.bank[0][:, 0:FREE3], ACT.Copy)
                nc.scalar.activation(ext[u][:, 2 + FREE3:2 + 2 * FREE3], K.bank[1][:, 0:FREE3], ACT.Copy)
                nc.scalar.activation(ext[u][:, 2 + 2 * FREE3:2 + SEQ], K.bank[2][:, 0:SEQ - 2 * FREE3], ACT.Copy)
                nc.scalar.activation(ext[u][:, 1026:1074].rearrange("p (n q) -> p n q", n=NS)[:, :, 2:6],
                                     K.bank[2][:, SEQ - 2 * FREE3:FREE3].rearrange("p (n q) -> p n q", n=NS),
                                     ACT.Copy).then_inc(up_taken, 1)
                act.wait_ge(conv_done, i * 2 + u + 3)
                nc.scalar.activation(ct[u], ct[u], ACT.Gelu_apprx_tanh).then_inc(gelu_done, 1)
                if more:
                    act.wait_ge(gate_done, i * 2 + u + 1)
                    high_part(1, i * 2 + (u + 1))

            high_part(0, 0)
            high_part(1, 0)
            with act.Fori(0, FC // 2 - 1) as i:
                chunk(i, 0, True)
                chunk(i, 1, True)
            chunk(FC // 2 - 1, 0, True)
            chunk(FC // 2 - 1, 1, False)

        @block.vector
        def _(dve):
            dve.sem_inc(conv_done, 2)
            dve.sem_inc(gate_taken, 1)
            dve.wait_ge(small, 32)
            dve.wait_ge(zeroed, 2)
            with dve.Fori(0, FC // 2) as i:
                n = 0

                def link(ins):
                    nonlocal n
                    n += 1
                    ins.then_inc(vch, 1)
                    dve.wait_ge(vch, i * (2 * LINKS) + n)

                for u in range(2):
                    c = bass.ds(i * 2 + u, 1)
                    es = ext[u][:, 1026:1074].rearrange("p (n q) -> p n q", n=NS)
                    cs = ct[u][:, SEQ:T].rearrange("p (n q) -> p n q", n=NS)
                    w = [cw[u][:, x:x + 1] for x in range(4)]
                    link(nc.vector.tensor_copy(cw[u], cwb[:, c, :].rearrange("p a n -> p (a n)")))
                    link(nc.vector.tensor_copy(es[:, :, 0:2], prev[:, c, :].rearrange("p a (n q) -> p (a n) q", q=2)))
                    dve.wait_ge(up_taken, i * 2 + u + 2)
                    nc.vector.tensor_scalar(ct[u][:, 0:SEQ], ext[u][:, 0:SEQ], w[0], w[3], ALU.mult, ALU.add)
                    link(nc.vector.tensor_scalar(cs, es[:, :, 0:4], w[0], w[3], ALU.mult, ALU.add))
                    nc.vector.scalar_tensor_tensor(ct[u][:, 0:SEQ], ext[u][:, 1:SEQ + 1], w[1], ct[u][:, 0:SEQ], ALU.mult, ALU.add)
                    link(nc.vector.scalar_tensor_tensor(cs, es[:, :, 1:5], w[1], cs, ALU.mult, ALU.add))
                    nc.vector.tensor_copy(co[:, c, 0:2].rearrange("p a n -> p (a n)"), ext[u][:, SEQ:SEQ + 2])
                    link(nc.vector.tensor_copy(co[:, c, 2:18].rearrange("p a (n q) -> p (a n) q", q=2), es[:, :, 4:6]))
                    nc.vector.scalar_tensor_tensor(ct[u][:, 0:SEQ], ext[u][:, 2:SEQ + 2], w[2], ct[u][:, 0:SEQ], ALU.mult, ALU.add)
                    link(nc.vector.scalar_tensor_tensor(cs, es[:, :, 2:6], w[2], cs, ALU.mult, ALU.add))
                    dve.sem_inc(conv_done, 1)
                    dve.wait_ge(gelu_done, i * 2 + u + 1)
                    dve.wait_ge(gate_done, i * 2 + u + 1)
                    for x, (a, b) in enumerate(pieces):
                        last = nc.vector.tensor_tensor(actt[:, c, a:b].rearrange("p a n -> p (a n)"), ct[u][:, a:b],
                                                       K.bank[3 + x][:, 0:b - a], ALU.mult)
                    link(last)
                    dve.sem_inc(gate_taken, 1)


def ffn_down(nc, K, I, O, mem, actt):
    S = K.sem
    slot = [mem.enter_context(nc.sbuf_tensor(f"dn_weights{u}", [P, FC, 256], F32)) for u in range(2)]
    g = mem.enter_context(nc.sbuf_tensor("final_gain", [P, D], F32))
    square = mem.enter_context(nc.sbuf_tensor("final_square", [P, D], F32))
    cuts = [0, 4, 8, 15, FC]
    came = [[S(f"dn_w{u}_{x}") for x in range(4)] for u in range(2)]
    x_came = [S(f"dn_x{t}") for t in range(TILES)]
    done, taken, gain_came = S("dn_product"), S("dn_taken"), S("fin_gain")
    squares, std_ready, rs_ready, y = S("fin_squares"), S("fin_std"), S("fin_rstd"), S("fin_y")
    per = 2 * TILES
    ss, std, rs = (K.stat[:, i, :TILES] for i in range(3))
    with nc.Block() as block:
        @block.sync
        def _(sp):
            for q in range(4):
                if q >= 2:
                    sp.wait_ge(done, (q - 1) * TILES)
                for x in range(4):
                    sp.dma_start(slot[q % 2][:, cuts[x]:cuts[x + 1], :],
                                 I["w_down"][q][:, cuts[x]:cuts[x + 1], :]).then_inc(came[q % 2][x], 16)
                if q == 0:
                    for t in range(TILES):
                        sp.dma_start(K.X[:rows_of(t), t, :], K.x_dram[t, :rows_of(t), :]).then_inc(x_came[t], 16)
            sp.dma_start(g[:, :], I["g_final"].to_broadcast([P, D])).then_inc(gain_came, 16)
            for t in range(TILES):
                sp.wait_ge(y, t + 1)
                to = O["y_prompt"][t] if t < TILES - 1 else O["y_sample"]
                sp.dma_start(to, K.X[:rows_of(t), t, :]).then_inc(K.out_sem, 16)
            sp.wait_ge(K.out_sem, 16 * K.outs(TILES))

        @block.tensor
        def _(pe):
            with pe.Fori(0, 2) as i:
                for j in range(per):
                    u, t = j // TILES, j % TILES
                    pe.wait_ge(taken, i * per + j + 1)
                    for k in range(FC):
                        if t == 0 and k in cuts:
                            pe.wait_ge(came[u][cuts.index(k)], i * 16 + 16)
                        last = nc.tensor.matmul(K.bank[j % 6][:rows_of(t), 0:256], actt[:, k, t * P:t * P + rows_of(t)],
                                                slot[u][:, k, :], start=k == 0, stop=k == FC - 1)
                    last.then_inc(done, 1)

        @block.scalar
        def _(act):
            for t in range(TILES):
                r = rows_of(t)
                act.wait_ge(taken, 6 + 3 * TILES + t + 1)
                if t:
                    act.wait_ge(squares, t)
                nc.scalar.activation(square[:r, :], K.X[:r, t, :], ACT.Square, accum_out=ss[:r, t:t + 1]).then_inc(squares, 1)
                act.wait_ge(squares, t + 1)
                nc.scalar.activation(std[:r, t:t + 1], ss[:r, t:t + 1], ACT.Sqrt, bias=K.eps[:r, 0:1], scale=1.0 / D).then_inc(std_ready, 1)

        @block.vector
        def _(dve):
            dve.sem_inc(taken, 6)

            def add(q, t):
                x = K.X[:rows_of(t), t, q * 256:(q + 1) * 256]
                n = q * TILES + t
                dve.wait_ge(done, n + 1)
                if q == 0:
                    dve.wait_ge(x_came[t], 16)
                nc.vector.tensor_tensor(x, K.bank[n % per % 6][:rows_of(t), 0:256], x, ALU.add).then_inc(taken, 1)

            def norm(t):
                r = rows_of(t)
                dve.wait_ge(std_ready, t + 1)
                nc.vector.reciprocal(rs[:r, t:t + 1], std[:r, t:t + 1]).then_inc(rs_ready, 1)
                dve.wait_ge(rs_ready, t + 1)
                nc.vector.scalar_tensor_tensor(K.X[:r, t, :], K.X[:r, t, :], rs[:r, t:t + 1], g[:r, :], ALU.mult, ALU.mult).then_inc(y, 1)

            for q in range(4):
                for t in range(TILES):
                    if (q, t) == (3, 1):
                        dve.wait_ge(gain_came, 16)
                        dve.wait_ge(taken, 6 + 4 * TILES - TILES + 1)
                    add(q, t)
                    if q == 3 and t >= 1:
                        norm(t - 1)
            dve.wait_ge(taken, 6 + 4 * TILES)
            norm(TILES - 1)


class Places:

    def outs(self, n):
        self.n_out += n
        return self.n_out


def program(nc, I, O):
    ctx = ExitStack()
    with ctx:
        K = Places()
        K.n_out, K.page_regs = 0, None
        first_part, K.sems = ExitStack(), []

        def phase_sem(name):
            K.sems.append(first_part.enter_context(nc.semaphore(name)))
            return K.sems[-1]

        K.sem = phase_sem
        sb = lambda name, shape, dt=F32: ctx.enter_context(nc.sbuf_tensor(name, shape, dt))
        K.ident = sb("ident", [P, P])
        K.gains = sb("gains", [P, 5, KD])
        K.GT = sb("gates_by_token", [P, TILES, 3 * H])
        K.GS = sb("gates_by_head", [P, H, TILES - 1, 3])
        K.stat = sb("stat", [P, 3, 3 * TILES])
        K.eps = sb("eps", [P, 1])
        K.table = sb("table", [BUCKETS + 1, H])
        K.page_table = sb("pages", [1, NS * NPAGE], I32)
        K.n_pool = I["pool_sel_k"].shape[0]
        x_place, top_place = ExitStack(), ExitStack()
        x = x_place.enter_context(nc.sbuf_tensor("x", [P, TILES * D], F32, side="right"))
        K.big = x_place.enter_context(nc.sbuf_tensor("big", [P, BIG], F32, side="right"))
        K.top = top_place.enter_context(nc.sbuf_tensor("top", [P, TOP], F32))
        K.tmp = K.top[:, O_TMP:O_TMP + 2 * D]
        K.ps = ctx.enter_context(nc.psum_tensor("ps", [P, 8 * 512], F32))
        K.bank = [K.ps[:, 512 * b:512 * (b + 1)] for b in range(8)]
        K.ps4 = K.ps[:, 0:2048]
        K.junk = K.ps[:, 3072:4096]
        K.X = x[:, :].rearrange("p (t n) -> p t n", t=TILES)
        K.HT = K.big[:, O_HT:O_W].rearrange("p (k n) -> p k n", k=KD)
        K.M = K.top[:, O_M:O_FM].rearrange("p (t n) -> p t n", t=TILES)
        K.FM = K.top[:, O_FM:O_VT].rearrange("p (c n) -> p c n", c=8)
        K.VT = K.top[:, O_VT:O_TMP].rearrange("p (t n) -> p t n", t=TILES)
        cp = K.top[:, O_CP:TOP]
        K.KCP, K.VCP = cp[:, 0:63], cp[:, 64:192]
        K.KCS = cp[:, 192:696].rearrange("p (n c) -> p n c", n=NS)
        K.VCS = cp[:, 696:1720].rearrange("p (n c) -> p n c", n=NS)
        K.vec_dram = nc.dram_tensor("bias_rows", [H, VECS + VECW], F32).ap()
        K.gates_dram = nc.dram_tensor("sample_gates", [SROWS, 3 * H], F32).ap()
        K.x_dram = nc.dram_tensor("residual_stream", [TILES, P, D], F32).ap()
        K.o_dram = nc.dram_tensor("sample_out", [SROWS, DA], F32).ap()
        K.out_sem, K.gates_sem, K.wtm_sem, K.gating_sem, K.x_came = (
            ctx.enter_context(nc.semaphore(name)) for name in
            ("outputs_written", "gates_in_dram", "token_major_weights", "gating_operands", "x_came_again"))
        K.slot = [x[:, 0:4096], x[:, 4096:8192], K.big[:, O_HT:O_HT + 4096], K.big[:, O_HT + 4096:O_HT + 8192]]
        K.slot_came = [K.sem(f"pages_slot{i}") for i in range(4)]
        K.windows = [(K.M[:, 0:4, DA:D], K.M[:, 4:8, DA:D]),
                     tuple(K.big[:, O_HT + 8192 + 2048 * i:O_HT + 10240 + 2048 * i].rearrange("p (n t) -> p n t", n=4) for i in range(2))]
        K.windows_came = [K.sem(f"windows{i}") for i in range(2)]

        const_came, eps_set = K.sem("const_came"), K.sem("eps_set")
        with nc.Block() as block:
            @block.sync
            def _(sp):
                sp.dma_start(K.ident[:, :], I["ident"]).then_inc(const_came, 16)
                sp.dma_start(K.gains[:, :, :], I["gains"]).then_inc(const_came, 16)
                sp.wait_ge(const_came, 32)

            @block.gpsimd
            def _(pool):
                nc.gpsimd.memset(K.eps[:, :], EPS).then_inc(eps_set, 1)
                pool.wait_ge(eps_set, 1)

        norm_phase(nc, K, "mix", x_tiles(K), D, K.gains[:, 0, :], K.HT, x_loads(K, I), bias_rows(nc, K, I))

        def states(sp):
            for u in range(2):
                sp.wait_ge(K.fm_taken[u], 5)
            sp.dma_start(O["fm"].rearrange("c p n -> p c n"), K.FM[:, 4:8, :]).then_inc(K.out_sem, 16)
            for v in range(2):
                sp.dma_start(O["win_old"][v], I["win_old"][v][:, TS:WIN, :]).then_inc(K.out_sem, 16)
            K.outs(3)

        ring = K.top[:, O_M:O_M + 2048].rearrange("p (u k n) -> p u k n", u=2, k=KD)

        def small(sp):
            for to, of in gating_operands(K, I):
                sp.dma_start(to, of).then_inc(K.gating_sem, 16)

        feature_major(nc, K, "fm", I["w_fm"], 8, ring, K.HT, T, K.FM,
                      {"sync": states, ("sync", 1): lambda sp: gather_cmp(sp, I, K, 0, 0, 0),
                       ("sync", 3): lambda sp: gather_cmp(sp, I, K, 0, 1, 1), ("sync", 5): small})
        gating_phase(nc, K, I, O)
        compress_phase(nc, K, I)
        sample_attention(nc, K, I)
        prompt_attention(nc, K, I)
        with nc.Block() as block:
            @block.gpsimd
            def _(pool):
                for s in K.sems:
                    pool.sem_clear(s)
        first_part.close()
        wo = projection_weights(K, "wo", I["w_o"])
        project_norm(nc, K, "wo", wo, K.HT, K.gains[:, 2, :], K.HT, K.top[:, O_FM:O_FM + 4 * D],
                     before=([(K.M[:rows_of(t), t, :], rows_of(t), t * P) for t in range(TILES)], K.gains[:, 1, :]),
                     sync=lambda sp, added: wo[2](sp), x_came=K.x_came)
        m = K.top[:, O_M:O_FM]
        memx = m[:, 0:2048].rearrange("p (t n) -> p t n", t=2)
        memt = m[:, 2048:4096].rearrange("p (k n) -> p k n", k=KD)
        mkt = m[:, 4096:6144].rearrange("p (k n) -> p k n", k=KD)
        mv = m[:, 6144:8192].rearrange("p (t n) -> p t n", t=2)
        norm_phase(nc, K, "mem", [(memx[:, t, :], P, t * P) for t in range(2)], D, K.gains[:, 3, :], memt,
                   [(memx[:, t, :], I["mem_prompt"][t]) for t in range(2)])
        ring = K.top[:, O_TMP:O_TMP + 2048].rearrange("p (u k n) -> p u k n", u=2, k=KD)
        feature_major(nc, K, "mk", I["w_mk"], 8, ring, memt, MEM, mkt)
        memory_values(nc, K, I, O, memt, mkt, mv)
        feature_major(nc, K, "xq", I["w_xq"], 8, ring, K.HT, T, K.FM)
        sample, xo = CrossSample(K), projection_weights(K, "xo", I["w_xo"])
        cross_prompt(nc, K, I, K.FM, mkt, mv, sample)
        cross_sample(nc, K, I, sample, xo)
        top_place.close()
        norm_mem, acts_mem, split_mem, down_mem = (ExitStack() for _ in range(4))
        high, low = (split_mem.enter_context(nc.sbuf_tensor(f"ff_in_{n}", [P, KD, T], F32R)) for n in ("high", "low"))
        landing = split_mem.enter_context(nc.sbuf_tensor("ff_weights", [P, 2, KD, P], F32))
        scratch = norm_mem.enter_context(nc.sbuf_tensor("ff_scaled", [P, 2 * D], F32))[:, :]
        whole = norm_mem.enter_context(nc.sbuf_tensor("ff_normed", [P, 2, KD, P], F32))
        spilled = K.sem("x_in_dram")

        ff_came = [K.sem(f"ff_{name}_came") for name in ("up", "gate")]

        def spill(sp, added):
            for x, name in enumerate(("w_up", "w_gate")):
                sp.dma_start(landing[:, x], I[name][0]).then_inc(ff_came[x], 16)
            for t in range(TILES):
                sp.wait_ge(added, 2 * t + 2)
                sp.dma_start(K.x_dram[t, :rows_of(t), :], K.X[:rows_of(t), t, :]).then_inc(spilled, 16)
            sp.wait_ge(spilled, 16 * TILES)

        project_norm(nc, K, "xo", xo, K.HT, K.gains[:, 4, :], None, scratch, sync=spill, split=(high, low, whole))
        norm_mem.close()
        x_place.close()
        actt = acts_mem.enter_context(nc.sbuf_tensor("ff_activations", [P, FC, T], F32, side="right"))
        with ExitStack() as mem:
            ffn_up(nc, K, I, O, mem, actt, high, low, landing, ff_came)
        split_mem.close()
        K.X = down_mem.enter_context(nc.sbuf_tensor("x_again", [P, TILES, D], F32))
        ffn_down(nc, K, I, O, down_mem, actt)
        acts_mem.close()
        down_mem.close()


def bucket(dist):
    n = np.maximum(dist, 0)
    exact = BUCKETS // 2
    large = exact + (np.log(np.maximum(n, 1) / exact) / math.log(MAXDIST / exact) * (BUCKETS - exact)).astype(np.int64)
    return np.where(n < exact, n, np.minimum(large, BUCKETS - 1))


def constants():
    c = {"ident": np.eye(P)}
    oh = np.zeros((BUCKETS + 1, VECS + VECW))
    d = np.concatenate([np.arange(VECS) - 1023, np.arange(VECW) - 127])
    dead = (d < 0) | ((np.arange(len(d)) >= VECS) & (d >= WIN))
    oh[np.where(dead, BUCKETS, bucket(d)), np.arange(len(d))] = 1
    c["oh_v"] = oh
    new = np.arange(SROWS) % TS
    cmp_end = np.arange(NCMP) * CS + CL - 1
    pos = np.concatenate([np.arange(PAST), PAST + new, PAST + new, PAST - WIN + np.arange(WIN), cmp_end])
    oh = np.zeros((TS, BUCKETS, len(pos)))
    for q in range(TS):
        oh[q, bucket(PAST + q - pos), np.arange(len(pos))] = 1
    c["oh_s"] = oh.reshape(P, -1)
    r = np.arange(P)
    seq, grp, qry = r // 32, r // 16 % 2, r % 4
    c["dq"] = (r[:, None] // 32 == qry[None, :]) * 1.0
    c["gmat"] = ((seq[:, None] == seq) & (grp[:, None] == grp) & (qry[:, None] == qry)) * 1.0
    k = np.arange(SROWS)
    mask = np.zeros((P, 2, 2, SROWS))
    for half in range(2):
        ok = (seq[:, None] + 4 * half == k[None, :] // TS) & (k[None, :] % TS <= qry[:, None])
        mask[:, half, :, :] = np.where(ok, 0, NEG)[:, None, :]
    c["mask_new"] = mask.reshape(P, 2, 2 * SROWS)
    c["mask_win"] = np.where(np.arange(4)[None, :] > qry[:, None], 0, NEG)
    c0, s0 = np.arange(NCMP)[:, None] * CS, np.arange(NSEL)[None, :] * SELB
    c["overlap"] = ((c0 < s0 + SELB) & (c0 + CL > s0)) * 1.0
    c["jidx"] = np.broadcast_to(np.arange(1, 15), (P, 14))
    c["causal"] = (r[:, None] <= r[None, :]) * 1.0
    c["causal_s"] = ((k[:, None] // TS == k[None, :] // TS) & (k[:, None] <= k[None, :])) * 1.0
    c["cmp_valid"] = (r[:, None] >= CL - 1) * 1.0
    return {n: np.ascontiguousarray(a, np.float32) for n, a in c.items()}


def stationary(w):
    r, n = w.shape
    return w.reshape(r // P, P, n // P, P).transpose(2, 1, 0, 3)


def moving(w, width):
    r, n = w.shape
    return w.reshape(r // P, P, n // width, width).transpose(2, 1, 0, 3)


def kernel(**inputs):
    import concourse.bacc as bacc
    from concourse.bass_utils import run_bass_kernel_spmd

    x = {n: np.asarray(a) for n, a in inputs.items()}
    w = x["w_in"][0]
    q0, kv0, g0 = 2 * DA, 2 * DA + DA, 2 * DA + DA + 6 * KV
    q = w[:, q0:kv0].reshape(D, 2, HPG, HD).transpose(0, 2, 1, 3).reshape(D, DA)
    kv = [w[:, kv0 + i * KV:kv0 + (i + 1) * KV] for i in range(6)]
    L = {
        "x_prompt": x["x_prompt"].reshape(SEQ // P, P, D),
        "x_sample": x["x_sample"].reshape(SROWS, D),
        "mem_prompt": x["mem_prompt"].reshape(MEM // P, P, D),
        "page_table": x["page_table"].reshape(1, -1).astype(np.int32),
        "w_fm": stationary(np.concatenate([q, kv[0], kv[1], kv[2], kv[4]], 1)),
        "w_tm": np.concatenate([w[:, :q0], kv[3], kv[5], w[:, g0:]], 1).reshape(KD, P, TMW),
        "gains": np.stack([x["g_mix"][0], np.concatenate([x["g_a"][0], x["g_b"][0]]), x["g_xa"][0], x["g_mem"][0],
                           x["g_ffn"][0]]).reshape(5, KD, P).transpose(2, 0, 1),
        "ln_v_g": x["ln_v_g"], "ln_v_b": x["ln_v_b"], "g_final": x["g_final"][None],
        "ws_t": x["w_s"][0].transpose(2, 0, 1),
        "ws_s": np.tile(x["w_s"][0][:, :TS, :TS].transpose(2, 0, 1), (NS, 1, NS)),
        "bs_t": x["b_s"][0].T,
        "bs_s": np.tile(x["b_s"][0][:, :TS].T, (NS, 1)),
        "w_cmp1": np.stack([x[f"w_cmp1_{c}"][0].reshape(16, P, P).transpose(1, 0, 2) for c in "kv"]),
        "w_cmp2": np.stack([x[f"w_cmp2_{c}"][0] for c in "kv"]),
        "pe_cmp": np.stack([x[f"pe_cmp_{c}"][0].reshape(16, P).T for c in "kv"]),
        "b_cmp1": np.stack([x[f"b_cmp1_{c}"][0] for c in "kv"], 1),
        "b2k": np.tile(x["b_cmp2_k"][0], 2)[:, None],
        "b2v": np.tile(x["b_cmp2_v"][0], 2)[None],
        "pool_cmp": np.stack([x[f"cache_cmp_{c}"][0].reshape(-1, PAGE // 2, 2, HKV, HD).transpose(0, 2, 4, 3, 1).reshape(-1, P, HKV, PAGE // 2)
                              for c in "kv"]),
        "pool_sel_k": x["cache_sel_k"][0].reshape(-1, PAGE, KV).transpose(0, 2, 1),
        "pool_sel_v": x["cache_sel_v"][0].reshape(-1, PAGE, KV),
        "win_kt": x["cache_win_k"][0].reshape(NS, WIN, KV).transpose(0, 2, 1),
        "win_v": x["cache_win_v"][0].reshape(NS, WIN, KV),
        "win_old": np.stack([x[f"cache_win_{c}"][0].reshape(NS, WIN, KV) for c in "kv"]),
        "rel_bias": x["rel_bias"],
        "w_o": moving(x["w_o"][0], 512), "w_mv": moving(x["w_mv"][0], 512), "w_xo": moving(x["w_xo"][0], 512),
        "w_mk": stationary(x["w_mk"][0]), "w_xq": stationary(x["w_xq"][0]),
        "w_up": stationary(x["w_up"][0]), "w_gate": stationary(x["w_gate"][0]),
        "w_down": moving(x["w_down"][0], 256),
        "mem_kt": x["cache_mem_k"][0].reshape(NS, MEM, KD, P).transpose(0, 3, 2, 1),
        "mem_v": x["cache_mem_v"][0].reshape(NS, MEM, D),
        "conv_prev": x["state_conv"][0].transpose(2, 0, 1).reshape(FC, P, NS * 2).transpose(1, 0, 2),
        "conv_wb": np.concatenate([x["conv_w"][0], x["conv_b"]]).reshape(4, FC, P).transpose(2, 1, 0),
    }
    L.update(constants())
    shapes = {
        "y_prompt": (SEQ // P, P, D), "y_sample": (SROWS, D), "fm": (4, P, T), "vt": (SEQ // P, P, 2 * KV),
        "vt_s": (SROWS, 2 * KV), "win_old": (2, NS, WIN - TS, KV), "gmlp_v": (SROWS, DA),
        "mem_k": (P, KD, MEM), "mem_v": (MEM // P, P, D), "conv": (P, FC, 18),
    }
    nc = bacc.Bacc("TRN2", target_bir_lowering=False, num_devices=1)
    arrays, I, O = {}, {}, {}
    for n, a in L.items():
        a = np.ascontiguousarray(a)
        arrays[f"in_{n}"] = a
        I[n] = nc.dram_tensor(f"in_{n}", a.shape, mybir.dt.from_np(a.dtype), kind="ExternalInput").ap()
    for n, s in shapes.items():
        O[n] = nc.dram_tensor(f"out_{n}", s, F32, kind="ExternalOutput").ap()
    program(nc, I, O)
    r = run_bass_kernel_spmd(nc, [arrays], core_ids=[0]).results[0]
    o = {n: np.asarray(r[f"out_{n}"]) for n in shapes}

    fm = o["fm"].transpose(0, 2, 1)
    vt = o["vt"].reshape(SEQ, 2 * KV)
    rows = lambda a: a.reshape(1, 1, -1, HKV, HD)
    srows = lambda a: a.reshape(1, NS, TS, HKV, HD)
    vs, vw = o["vt_s"][:, :KV], o["vt_s"][:, KV:]
    win = [np.concatenate([o["win_old"][i], a.reshape(NS, TS, KV)], 1).reshape(1, NS, WIN, HKV, HD)
           for i, a in enumerate((fm[3][SEQ:], vw))]
    conv = o["conv"].transpose(1, 0, 2).reshape(FF, 18)
    return (o["y_prompt"].reshape(1, SEQ, D), o["y_sample"].reshape(NS, TS, D),
            rows(fm[0][:SEQ]), rows(fm[1][:SEQ]), rows(fm[2][:SEQ]), rows(vt[:, :KV]),
            rows(fm[3][SEQ - WIN:SEQ]), rows(vt[SEQ - WIN:, KV:]),
            o["mem_k"].transpose(2, 1, 0).reshape(1, 1, MEM, XH, XHD), o["mem_v"].reshape(1, 1, MEM, XH, XHD),
            conv[:, :2].T.reshape(1, 1, 2, FF),
            srows(fm[0][SEQ:]), srows(fm[1][SEQ:]), srows(fm[2][SEQ:]), srows(vs),
            win[0], win[1], o["gmlp_v"].reshape(1, NS, TS, DA),
            conv[:, 2:].reshape(FF, NS, 2).transpose(1, 2, 0).reshape(1, NS, 2, FF))
```

```python
import math
from contextlib import ExitStack

import numpy as np
import concourse.bass as bass
from concourse import mybir

F32 = mybir.dt.float32
F32R = mybir.dt.float32r
I32 = mybir.dt.int32
ALU = mybir.AluOpType
ACT = mybir.ActivationFunctionType
AX = mybir.AxisListType

P = 128
D = 1024
KD = D // P
SEQ = 1024
NS, TS = 8, 4
T = SEQ + NS * TS
TILES = SEQ // P + 1
SROWS = NS * TS
FREE3 = T // 3
DA = 512
AG, AGD = 8, 64
H, HKV, HPG, HD = 8, 2, 4, 64
KV = HKV * HD
PAST, PAGE, NPAGE = 1024, 128, 8
CL, CS = 32, 16
NCMP = PAST // CS - 1
SELB = 64
NSEL = 17
WIN = 512
BUCKETS, MAXDIST = 32, 128
MEM = 256
XH, XHD = 4, 256
FF = 2816
FC = FF // P
NEG = -1e30
EPS = 1e-6
TMW = 2 * DA + 2 * KV + 3 * H
VECS, VECW = 2048, 768
STRS, STRW = 1920, 640

O_HT = 0
O_W = O_HT + KD * T
BIG = O_W + KD * TMW
O_M = 0
O_FM = O_M + TILES * D
O_VT = O_FM + 8 * T
O_TMP = O_VT + TILES * 2 * KV
O_CP = O_TMP + 2 * D
TOP = O_CP + 63 + 128 + 504 + 1024 + 1


def rows_of(t):
    return P if t < TILES - 1 else SROWS


class Chain:

    def __init__(self, eng, sem):
        self.eng, self.sem, self.n = eng, sem, 0

    def __call__(self, ins):
        self.n += 1
        ins.then_inc(self.sem, 1)
        self.eng.wait_ge(self.sem, self.n)


def norm_phase(nc, K, tag, tiles, width, gain, dst, loads=None, extra=None, arrived=None):
    parts = D // width
    n, GROUP = len(tiles), 3
    S = K.sem
    stat_zero, squares, std_ready = S(f"{tag}_stat_set"), S(f"{tag}_squares"), S(f"{tag}_std")
    rstd_ready, scaled, turned, taken = S(f"{tag}_rstd"), S(f"{tag}_scaled"), S(f"{tag}_turned"), S(f"{tag}_taken")
    arrived = [S(f"{tag}_x{i}") for i in range(n)] if loads else arrived
    ss, std, rs = K.stat[:, 0, :n * parts], K.stat[:, 1, :n * parts], K.stat[:, 2, :n * parts]
    xn = K.tmp.rearrange("p (b n) -> p b n", b=2)

    with nc.Block() as block:
        @block.sync
        def _(sp):
            if loads:
                for i, (to, of) in enumerate(loads):
                    sp.dma_start(to, of).then_inc(arrived[i], 16)
            if extra and "sync" in extra:
                extra["sync"](sp)

        @block.gpsimd
        def _(pool):
            if extra and "gpsimd" in extra:
                extra["gpsimd"](pool)

        @block.scalar
        def _(act):
            act.wait_ge(stat_zero, 1)
            for i, (src, rows, _) in enumerate(tiles):
                if arrived:
                    act.wait_ge(arrived[i], 16)
                for q in range(parts):
                    if i + q:
                        act.wait_ge(squares, i * parts + q)
                    nc.scalar.activation(K.junk[:rows, 0:width], src[:, q * width:(q + 1) * width], ACT.Square,
                                         accum_out=ss[:rows, i * parts + q:i * parts + q + 1]).then_inc(squares, 1)
                if i + 1 == n or (i + 1) % GROUP == 0:
                    a, b = i // GROUP * GROUP * parts, (i + 1) * parts
                    act.wait_ge(squares, b)
                    nc.scalar.activation(std[:, a:b], ss[:, a:b], ACT.Sqrt, bias=K.eps[:, 0:1],
                                         scale=1.0 / width).then_inc(std_ready, 1)
            if extra and "scalar" in extra:
                extra["scalar"](act)

        @block.vector
        def _(dve):
            nc.vector.memset(ss, 1.0).then_inc(stat_zero, 1)

            def scale(i):
                src, rows, _ = tiles[i]
                if i % GROUP == 0:
                    a, b = i * parts, min(i + GROUP, n) * parts
                    dve.wait_ge(std_ready, i // GROUP + 1)
                    nc.vector.reciprocal(rs[:, a:b], std[:, a:b]).then_inc(rstd_ready, 1)
                    dve.wait_ge(rstd_ready, i // GROUP + 1)
                if i >= 2:
                    dve.wait_ge(turned, 2 * (i - 1))
                for q in range(parts):
                    last = nc.vector.tensor_scalar(xn[:rows, i % 2, q * width:(q + 1) * width],
                                                   src[:, q * width:(q + 1) * width],
                                                   rs[:rows, i * parts + q:i * parts + q + 1], None, ALU.mult)
                last.then_inc(scaled, 1)

            def take(i):
                _, rows, col = tiles[i]
                for b in range(2):
                    dve.wait_ge(turned, 2 * i + b + 1)
                    src = K.bank[2 * (i % 2) + b][:, :].rearrange("p (k n) -> p k n", k=4)[:, :, 0:rows]
                    nc.vector.tensor_tensor(dst[:, 4 * b:4 * b + 4, col:col + rows], src,
                                            gain[:, 4 * b:4 * b + 4].unsqueeze(2).to_broadcast([P, 4, rows]),
                                            ALU.mult).then_inc(taken, 1)

            scale(0)
            for i in range(n):
                if i + 1 < n:
                    scale(i + 1)
                take(i)
            if extra and "vector" in extra:
                extra["vector"](dve)

        @block.tensor
        def _(pe):
            for i, (_, rows, _) in enumerate(tiles):
                pe.wait_ge(scaled, i + 1)
                for b in range(2):
                    if i >= 2:
                        pe.wait_ge(taken, 2 * (i - 2) + b + 1)
                    for k in range(4):
                        last = nc.tensor.transpose(K.bank[2 * (i % 2) + b][:, k * P:k * P + rows],
                                                   xn[:rows, i % 2, (4 * b + k) * P:(4 * b + k + 1) * P],
                                                   K.ident[:rows, :rows])
                    last.then_inc(turned, 1)
                if extra and ("tensor", i) in extra:
                    extra["tensor", i](pe)


def x_tiles(K):
    return [(K.X[:rows_of(t), t, :], rows_of(t), t * P) for t in range(TILES)]


def x_loads(K, I):
    return [(K.X[:rows_of(t), t, :], I["x_prompt"][t] if t < TILES - 1 else I["x_sample"]) for t in range(TILES)]


class Ring:

    def __init__(self, K, tag, w_dram, place):
        self.slots = place.rearrange("p (u k n) -> p u k n", u=2, k=KD)
        self.tag, self.w = tag, w_dram
        self.came = [K.sem(f"{tag}_w{u}") for u in range(2)]

    def load(self, sp, chunks=(0, 1)):
        for c in chunks:
            sp.dma_start(self.slots[:, c % 2], self.w[c]).then_inc(self.came[c % 2], 16)


def feature_major(nc, K, weights, chunks, src, cols, dst, extra=None):
    S = K.sem
    tag, ring, came = weights.tag, weights.slots, weights.came
    done = [S(f"{tag}_product{u}") for u in range(2)]
    taken = [S(f"{tag}_taken{u}") for u in range(2)]
    K.fm_taken = taken
    pieces = [(a, min(a + FREE3, cols)) for a in range(0, cols, FREE3)]
    with nc.Block() as block:
        @block.sync
        def _(sp):
            for c in range(chunks):
                u = c % 2
                if c >= 2:
                    sp.wait_ge(done[u], c // 2)
                    weights.load(sp, (c,))
                if extra and ("sync", c) in extra:
                    extra["sync", c](sp)
            if extra and "sync" in extra:
                extra["sync"](sp)

        @block.tensor
        def _(pe):
            with pe.Fori(0, chunks // 2) as i:
                for u in range(2):
                    pe.wait_ge(came[u], i * 16 + 16)
                    pe.wait_ge(taken[u], i + 1)
                    for s, (a, b) in enumerate(pieces):
                        for k in range(KD):
                            last = nc.tensor.matmul(K.bank[3 * u + s][:, 0:b - a], ring[:, u, k, :], src[:, k, a:b],
                                                    start=k == 0, stop=k == KD - 1)
                    last.then_inc(done[u], 1)

        @block.scalar
        def _(act):
            for u in range(2):
                act.sem_inc(taken[u], 1)
            with act.Fori(0, chunks // 2) as i:
                for u in range(2):
                    act.wait_ge(done[u], i + 1)
                    for s, (a, b) in enumerate(pieces):
                        last = nc.scalar.activation(dst[:, bass.ds(i * 2 + u, 1), a:b].rearrange("p c n -> p (c n)"),
                                                    K.bank[3 * u + s][:, 0:b - a], ACT.Copy)
                    last.then_inc(taken[u], 1)


def projection_weights(K, tag, w_dram):
    w = K.big[:, O_W:O_W + KD * D].rearrange("p (h k n) -> p h k n", h=2, k=KD)
    came = [K.sem(f"{tag}_w{h}") for h in range(2)]

    def load(sp):
        for h in range(2):
            sp.dma_start(w[:, h], w_dram[h]).then_inc(came[h], 16)

    return w, came, load


def project_norm(nc, K, tag, weights, src, gain, dst, scratch, before=None, sync=None, split=None, x_came=None):
    S = K.sem
    w, came, _ = weights
    n = TILES
    done, added, squares, link_sem = S(f"{tag}_product"), S(f"{tag}_added"), S(f"{tag}_squares"), S(f"{tag}_dve")
    std2, scaled2, turned2, taken2 = S(f"{tag}_std"), S(f"{tag}_scaled"), S(f"{tag}_turned"), S(f"{tag}_taken")
    std1, scaled1, turned1, taken1 = S(f"{tag}_pre_std"), S(f"{tag}_pre_scaled"), S(f"{tag}_pre_turned"), S(f"{tag}_pre_taken")
    square = scratch[:, 0:D]
    xn2 = scratch[:, D:2 * D]
    xn1 = scratch[:, 2 * D:4 * D].rearrange("p (b n) -> p b n", b=2) if before else None
    ss, std, rs = (K.stat[:, i, :] for i in range(3))
    if split:
        high, low, whole = split
        high_made, low_made = S(f"{tag}_high"), S(f"{tag}_low")

    with nc.Block() as block:
        @block.sync
        def _(sp):
            if sync:
                sync(sp, added)

        @block.tensor
        def _(pe):
            def turn(x, r, bank, ready, taken, turned, t):
                pe.wait_ge(ready, t + 1)
                for b in range(2):
                    if t:
                        pe.wait_ge(taken, 2 * (t - 1) + b + 1)
                    for k in range(4):
                        last = nc.tensor.transpose(K.bank[bank + b][:, k * P:k * P + r], x[:r, (4 * b + k) * P:(4 * b + k + 1) * P],
                                                   K.ident[:r, :r])
                    last.then_inc(turned, 1)

            turn1 = lambda t: turn(xn1[:, t % 2], rows_of(t), 4, scaled1, taken1, turned1, t)
            turn2 = lambda t: turn(xn2, rows_of(t), 6, scaled2, taken2, turned2, t)
            if before:
                turn1(0)
                turn1(1)
            for t in range(n):
                r = rows_of(t)
                if before:
                    pe.wait_ge(taken1, 2 * t + 2)
                for h in range(2):
                    if t == 0:
                        pe.wait_ge(came[h], 16)
                    if t >= 2:
                        pe.wait_ge(added, 2 * (t - 2) + h + 1)
                    for k in range(KD):
                        last = nc.tensor.matmul(K.bank[2 * (t % 2) + h][:r, :], src[:, k, t * P:t * P + r], w[:, h, k, :],
                                                start=k == 0, stop=k == KD - 1)
                    last.then_inc(done, 1)
                if t >= 1:
                    turn2(t - 1)
                if before and t + 2 < n:
                    turn1(t + 2)
            turn2(n - 1)

        @block.scalar
        def _(act):
            count = [0]

            def square_sum(x, r, at):
                if count[0]:
                    act.wait_ge(squares, count[0])
                nc.scalar.activation(square[:r, 0:x.shape[1]], x, ACT.Square, accum_out=ss[:r, at:at + 1]).then_inc(squares, 1)
                count[0] += 1

            def halves(t):
                x, r, _ = before[0][t]
                for q in range(2):
                    square_sum(x[:, q * DA:(q + 1) * DA], r, 2 * t + q)

            def root(r, a, b, width, ready):
                act.wait_ge(squares, count[0])
                nc.scalar.activation(std[:r, a:b], ss[:r, a:b], ACT.Sqrt, bias=K.eps[:r, 0:1], scale=1.0 / width).then_inc(ready, 1)

            def high_part(t):
                r = rows_of(t)
                for b in range(2):
                    act.wait_ge(taken2, 2 * t + b + 1)
                    nc.scalar.activation(high[:, 4 * b:4 * b + 4, t * P:t * P + r], whole[:, t % 2, 4 * b:4 * b + 4, 0:r],
                                         ACT.Copy).then_inc(high_made, 1)

            if before:
                for t in range(3):
                    halves(t)
                root(P, 0, 6, DA, std1)
            for t in range(n):
                r = rows_of(t)
                if before and t + 3 < n:
                    halves(t + 3)
                act.wait_ge(added, 2 * t + 2)
                square_sum(K.X[:r, t, :], r, 2 * n + t)
                root(r, 2 * n + t, 2 * n + t + 1, D, std2)
                if before and t + 3 < n:
                    root(rows_of(t + 3), 2 * t + 6, 2 * t + 8, DA, std1)
                if split and t >= 1:
                    high_part(t - 1)
            if split:
                high_part(n - 1)

        @block.gpsimd
        def _(pool):
            if split:
                for t in range(n):
                    r = rows_of(t)
                    for b in range(2):
                        pool.wait_ge(high_made, 2 * t + b + 1)
                        at = (slice(None), slice(4 * b, 4 * b + 4), slice(t * P, t * P + r))
                        nc.gpsimd.tensor_tensor(low[at], whole[:, t % 2, 4 * b:4 * b + 4, 0:r], high[at],
                                                ALU.subtract).then_inc(low_made, 1)

        @block.vector
        def _(dve):
            link = Chain(dve, link_sem)

            def scale1(t):
                x, r, _ = before[0][t]
                if t >= 2:
                    dve.wait_ge(turned1, 2 * (t - 1))
                for q in range(2):
                    last = nc.vector.tensor_scalar(xn1[:r, t % 2, q * DA:(q + 1) * DA], x[:, q * DA:(q + 1) * DA],
                                                   rs[:r, 2 * t + q:2 * t + q + 1], None, ALU.mult)
                last.then_inc(scaled1, 1)

            def take(t, bank, g, turned, taken, to):
                r = rows_of(t)
                for b in range(2):
                    dve.wait_ge(turned, 2 * t + b + 1)
                    nc.vector.tensor_tensor(to[:, 4 * b:4 * b + 4, :], K.bank[bank + b][:, :].rearrange("p (k n) -> p k n", k=4)[:, :, 0:r],
                                            g[:, 4 * b:4 * b + 4].unsqueeze(2).to_broadcast([P, 4, r]), ALU.mult).then_inc(taken, 1)

            def take1(t):
                take(t, 4, before[1], turned1, taken1, src[:, :, t * P:t * P + rows_of(t)])

            def take2(t):
                r = rows_of(t)
                if split and t >= 2:
                    dve.wait_ge(low_made, 2 * (t - 1))
                take(t, 6, gain, turned2, taken2, whole[:, t % 2, :, 0:r] if split else dst[:, :, t * P:t * P + r])

            if before:
                dve.wait_ge(std1, 1)
                link(nc.vector.reciprocal(rs[:, 0:6], std[:, 0:6]))
                scale1(0)
                scale1(1)
                take1(0)
                scale1(2)
                take1(1)
            if x_came:
                dve.wait_ge(x_came, 16 * n)
            for t in range(n):
                r = rows_of(t)
                for h in range(2):
                    x = K.X[:r, t, h * 512:(h + 1) * 512]
                    dve.wait_ge(done, 2 * t + h + 1)
                    nc.vector.tensor_tensor(x, K.bank[2 * (t % 2) + h][:r, :], x, ALU.add).then_inc(added, 1)
                if t >= 1:
                    take2(t - 1)
                if before and t + 2 < n:
                    take1(t + 2)
                dve.wait_ge(std2, t + 1)
                link(nc.vector.reciprocal(rs[:r, 2 * n + t:2 * n + t + 1], std[:r, 2 * n + t:2 * n + t + 1]))
                dve.wait_ge(added, 2 * t + 2)
                nc.vector.tensor_scalar(xn2[:r, :], K.X[:r, t, :], rs[:r, 2 * n + t:2 * n + t + 1], None, ALU.mult).then_inc(scaled2, 1)
                if before and t + 3 < n:
                    dve.wait_ge(std1, t + 2)
                    q = rows_of(t + 3)
                    link(nc.vector.reciprocal(rs[:q, 2 * t + 6:2 * t + 8], std[:q, 2 * t + 6:2 * t + 8]))
                    scale1(t + 3)
            take2(n - 1)


def gather(sp, K, half, name, first=0, count=NS // 2):
    regs = K.page_regs = K.page_regs or [sp.alloc_register(f"page{b}") for b in range(NPAGE)]
    slots = K.slots[half]
    if name == "cmp":
        slots = slots.rearrange("p v (g t) -> p v g t", g=HKV)
    with sp.Fori(first, first + count) as n:
        sp.load(regs, K.page_table[0:1, bass.ds(n * NPAGE + half * (NS // 2) * NPAGE, NPAGE)])
        pages = [sp.snap(r, min_val=0, max_val=K.n_pool - 1) for r in regs]
        for b, page in enumerate(pages):
            of = K.pools[name][bass.ds(page, 1)]
            of = of.rearrange("a p v g t -> (a p) v g t" if name == "cmp" else "a p v t -> (a p) v t")
            to = slots[:, :, :, bass.ds(n * (NPAGE * PAGE // 2) + b * (PAGE // 2), PAGE // 2)] if name == "cmp" else \
                slots[:, :, bass.ds(n * (NPAGE * PAGE) + b * PAGE, PAGE)]
            sp.dma_start(to, of).then_inc(K.slots_came[half], 16)


SLOT_PAGES = 16 * NS * NPAGE // 2


def gating_operands(K, I):
    tmp = K.top[:, O_TMP:O_TMP + 2 * D]
    cp = K.top[:, O_CP:O_CP + 1720]
    ws = tmp[:, 2 * DA:].rearrange("p (g t) -> p g t", g=AG)
    wss = cp[:, 512:768].rearrange("p (g t) -> p g t", g=AG)
    return [(tmp[:, 0:DA], I["ln_v_g"].to_broadcast([P, DA])), (tmp[:, DA:2 * DA], I["ln_v_b"].to_broadcast([P, DA])),
            (ws, I["ws_t"]), (wss[:SROWS], I["ws_s"]), (cp[:, 768:776], I["bs_t"]), (cp[:SROWS, 776:784], I["bs_s"]),
            (cp[:, 784:912], I["causal"]), (cp[:SROWS, 912:944], I["causal_s"]), (cp[:, 990:991], I["cmp_valid"])]


def gating_phase(nc, K, I, O):
    S = K.sem
    p_done, uv_taken, rest_taken = S("in_product"), S("in_uv_taken"), S("in_rest_taken")
    a_chain, sd_ready, v_ready, v_chain = S("in_act"), S("in_sd"), S("in_v_ready"), S("in_dve")
    mixed, mixed_used, masked, a_out = S("in_mixed"), S("in_mixed_used"), S("in_ws_masked"), S("in_out")
    sig, gd = S("in_sigmoid"), K.gating_sem
    w = K.big[:, O_W:O_W + KD * TMW].rearrange("p (k n) -> p k n", k=KD)
    tmp = K.top[:, O_TMP:O_TMP + 2 * D]
    lng, lnb = tmp[:, 0:DA], tmp[:, DA:2 * DA]
    ws = tmp[:, 2 * DA:].rearrange("p (g t) -> p g t", g=AG)
    cp = K.top[:, O_CP:O_CP + 1720]
    junk, wss = cp[:, 0:512], cp[:, 512:768].rearrange("p (g t) -> p g t", g=AG)
    bs, bss = cp[:, 768:776], cp[:, 776:784]
    caus, causs = cp[:, 784:912], cp[:, 912:944]
    nm, sq, sd, rsd, sv = (cp[:, 944 + 9 * i:953 + 9 * i] for i in range(5))
    valid = cp[:, 990:991]
    cuts = [(0, DA), (DA, 2 * DA), (2 * DA, TMW)]

    with nc.Block() as block:
        @block.sync
        def _(sp):
            compress_operands(sp, K, I)
            sp.wait_ge(p_done, TILES)
            for v in range(2):
                sp.dma_start(K.cmp_w1[v], I["w_cmp1"][v]).then_inc(K.cmp_w1_came[v], 16)
            sp.wait_ge(v_ready, TILES)
            sp.dma_start(O["gmlp_v"], K.M[:SROWS, TILES - 1, DA:D]).then_inc(K.out_sem, 16)
            sp.wait_ge(rest_taken, 2 * TILES)
            sp.dma_start(O["vt"].rearrange("t p n -> p t n"), K.VT[:, 0:8, :]).then_inc(K.out_sem, 16)
            sp.dma_start(O["vt_s"], K.VT[:SROWS, 8, :]).then_inc(K.out_sem, 16)
            sp.wait_ge(sig, 2)
            sp.dma_start(K.gates_dram, K.GT[:SROWS, 8, :]).then_inc(K.gates_sem, 16)
            sp.wait_ge(K.out_sem, 16 * K.outs(3))
            sp.wait_ge(K.gates_sem, 16)

        @block.tensor
        def _(pe):
            pe.wait_ge(K.wtm_sem, 16 * KD)
            pe.wait_ge(masked, 2)

            def gate(pair):
                t = 2 * pair
                m = min(2, TILES - t)
                r = rows_of(t)
                pe.wait_ge(v_ready, t + m)
                if pair:
                    pe.wait_ge(mixed_used, pair)
                for g in range(AG):
                    lhs = ws[:, g, :] if r == P else wss[:SROWS, g, :]
                    last = nc.tensor.matmul(K.ps[:r, 3072 + g * 128:3072 + g * 128 + m * AGD], lhs,
                                            K.M[:r, t:t + m, DA + g * AGD:DA + (g + 1) * AGD], start=True, stop=True)
                last.then_inc(mixed, 1)

            for t in range(TILES):
                r = rows_of(t)
                if t >= 2:
                    pe.wait_ge(uv_taken, 2 * (t - 1))
                    pe.wait_ge(rest_taken, 2 * (t - 1))
                for s, (a, b) in enumerate(cuts):
                    for k in range(KD):
                        last = nc.tensor.matmul(K.bank[3 * (t % 2) + s][:r, 0:b - a],
                                                K.HT[:, k, t * P:t * P + r], w[:, k, a:b],
                                                start=k == 0, stop=k == KD - 1)
                last.then_inc(p_done, 1)
                if t >= 2 and t % 2 == 0:
                    gate(t // 2 - 1)
            gate(TILES // 2)

        @block.scalar
        def _(act):
            link = Chain(act, a_chain)
            for t in range(TILES):
                r = rows_of(t)
                bank = 3 * (t % 2)
                act.wait_ge(p_done, t + 1)
                nc.scalar.activation(K.M[:r, t, 0:DA], K.bank[bank][:r, :], ACT.Gelu_apprx_tanh).then_inc(uv_taken, 1)
                nc.scalar.activation(K.M[:r, t, DA:D], K.bank[bank + 1][:r, :], ACT.Gelu_apprx_tanh,
                                     accum_out=sv[:r, t:t + 1]).then_inc(uv_taken, 1)
                act.wait_ge(uv_taken, 2 * (t + 1))
                link(nc.scalar.activation(nm[:r, t:t + 1], sv[:r, t:t + 1], ACT.Copy, scale=-1.0 / DA))
                link(nc.scalar.activation(junk[:r, :], K.M[:r, t, DA:D], ACT.Square, bias=nm[:r, t:t + 1],
                                          accum_out=sq[:r, t:t + 1]))
                nc.scalar.activation(sd[:r, t:t + 1], sq[:r, t:t + 1], ACT.Sqrt, bias=K.eps[:r, 0:1],
                                     scale=1.0 / DA).then_inc(sd_ready, 1)
            act.wait_ge(rest_taken, 2 * TILES)
            nc.scalar.activation(K.GT[:, 0:8, :], K.GT[:, 0:8, :], ACT.Sigmoid).then_inc(sig, 1)
            nc.scalar.activation(K.GT[:SROWS, 8, :], K.GT[:SROWS, 8, :], ACT.Sigmoid).then_inc(sig, 1)

        @block.vector
        def _(dve):
            link = Chain(dve, v_chain)
            dve.wait_ge(gd, 16 * len(gating_operands(K, I)))
            nc.vector.tensor_tensor(ws, ws, caus.unsqueeze(1).to_broadcast([P, AG, P]), ALU.mult).then_inc(masked, 1)
            nc.vector.tensor_tensor(wss[:SROWS], wss[:SROWS], causs[:SROWS].unsqueeze(1).to_broadcast([SROWS, AG, SROWS]),
                                    ALU.mult).then_inc(masked, 1)

            def gated(pair):
                t = 2 * pair
                m = min(2, TILES - t)
                r = rows_of(t)
                b = bs if r == P else bss
                dve.wait_ge(mixed, pair + 1)
                for g in range(AG):
                    u = K.M[:r, t:t + m, g * AGD:(g + 1) * AGD]
                    mix = K.ps[:r, 3072 + g * 128:3072 + g * 128 + m * AGD].rearrange("p (m d) -> p m d", m=m)
                    last = nc.vector.scalar_tensor_tensor(u, mix, b[:r, g:g + 1], u, ALU.add, ALU.mult)
                last.then_inc(mixed_used, 1)

            for t in range(TILES):
                r = rows_of(t)
                bank = K.bank[3 * (t % 2) + 2]
                v = K.M[:r, t, DA:D]
                dve.wait_ge(p_done, t + 1)
                nc.vector.tensor_copy(K.VT[:r, t, :], bank[:r, 0:2 * KV]).then_inc(rest_taken, 1)
                nc.vector.tensor_copy(K.GT[:r, t, :], bank[:r, 2 * KV:2 * KV + 3 * H]).then_inc(rest_taken, 1)
                dve.wait_ge(sd_ready, t + 1)
                link(nc.vector.reciprocal(rsd[:r, t:t + 1], sd[:r, t:t + 1]))
                link(nc.vector.tensor_scalar(v, v, nm[:r, t:t + 1], rsd[:r, t:t + 1], ALU.add, ALU.mult))
                link(nc.vector.tensor_tensor(v, v, lng[:r, :], ALU.mult))
                nc.vector.tensor_tensor(v, v, lnb[:r, :], ALU.add).then_inc(v_ready, 1)
                if t >= 2 and t % 2 == 0:
                    gated(t // 2 - 1)
            gated(TILES // 2)
            dve.wait_ge(sig, 1)
            gt = K.GT[:, 0:8, :].rearrange("p t (h b) -> p h t b", b=3)
            for b in range(3):
                last = nc.vector.tensor_copy(K.GS[:, :, :, b], gt[:, :, :, b])
            link(last)
            link(nc.vector.tensor_scalar(K.GS[:, :, 0, 0], K.GS[:, :, 0, 0], valid, None, ALU.mult))


CMP_OPERANDS = 7


def compress_operands(sp, K, I):
    w2, pe_t, b1, b2k, b2v, _ = K.cmp_small
    for to, of in [(w2[v], I["w_cmp2"][v]) for v in range(2)] + [(pe_t[v], I["pe_cmp"][v]) for v in range(2)] + \
                  [(b1, I["b_cmp1"]), (b2k, I["b2k"]), (b2v, I["b2v"].to_broadcast([P, P]))]:
        sp.dma_start(to, of).then_inc(K.cmp_came, 16)


def compress_phase(nc, K, I):
    S = K.sem
    ar = K.big[:, O_HT:BIG]
    pages = [K.slots[half][:, v].rearrange("p (g t) -> p g t", g=2) for half in range(2) for v in range(2)]
    w1 = K.cmp_w1
    dein = [ar[:, 12288 + 1024 * v:12288 + 1024 * (v + 1)].rearrange("p (r t) -> p r t", r=2) for v in range(2)]
    own = [ar[:, 14336 + 1024 * v:14336 + 1024 * (v + 1)].rearrange("p (g t) -> p g t", g=2) for v in range(2)]
    hid = [ar[:, 16384 + 512 * u:16384 + 512 * (u + 1)] for u in range(2)]
    w2, pe_t, b1, b2k, b2v, hb = K.cmp_small
    came_w, came_w2, came_own, dei = K.cmp_w1_came, K.cmp_came, S("cmp_own_came"), S("cmp_split")
    first, hidden, second, out, biased = S("cmp_first"), S("cmp_hidden"), S("cmp_second"), S("cmp_out"), S("cmp_bias")
    pe_w1, summed, vch = S("cmp_pe_product"), S("cmp_pe_sums"), S("cmp_dve")
    terms = ar[:, 16384:18432].rearrange("p (q h) -> p q h", h=P)
    c = K.x_tail
    ones, sums = c[:, 168:169], [c[:, 320 + P * v:320 + P * (v + 1)] for v in range(2)]
    rounds = [(0, 0), (1, 0), (0, None), (1, None), (0, 1), (1, 1)]

    with nc.Block() as block:
        @block.sync
        def _(sp):
            sp.wait_ge(dei, 2)
            for v in range(2):
                for g in range(2):
                    for r in range(2):
                        sp.dma_start(own[v][64 * r:64 * r + 64, g, :], dein[v][64 * g:64 * g + 64, r, :]).then_inc(came_own, 16)
            gather(sp, K, 1, "cmp")
            sample_windows(sp, K, I, 0)
            sp.wait_ge(first, 2)
            gather(sp, K, 0, "sel")

        @block.vector
        def _(dve):
            for v in range(2):
                nc.vector.tensor_copy(dein[v][:, :, :], K.FM[:, 4 + v, 0:SEQ].rearrange("p (t r) -> p r t", r=2)).then_inc(dei, 1)
            dve.wait_ge(came_w2, 16 * CMP_OPERANDS)
            link = Chain(dve, vch)
            link(nc.vector.memset(ones, 1.0))
            for v in range(2):
                dve.wait_ge(came_w[v], 16)
                link(nc.vector.tensor_tensor(terms, w1[v], pe_t[v].unsqueeze(2).to_broadcast([P, 16, P]), ALU.mult))
                link(nc.vector.tensor_reduce(sums[v], terms.rearrange("p q h -> p h q"), AX.X, ALU.add))
                dve.sem_inc(summed, 1)
            for v in range(2):
                dve.wait_ge(pe_w1, v + 1)
                nc.vector.tensor_tensor(hb[:, v:v + 1], K.bank[6 + v][:, v:v + 1], b1[:, v:v + 1], ALU.add).then_inc(biased, 1)
            for n, (v, half) in enumerate(rounds):
                dve.wait_ge(second, n + 1)
                bank = K.bank[2 + n % 2]
                if v == 0 and half is None:
                    last = nc.vector.tensor_scalar(K.KCP[:, :], bank[:, 0:NCMP], b2k, None, ALU.add)
                elif v == 0:
                    last = nc.vector.tensor_scalar(K.KCS[:, 4 * half:4 * half + 4, :],
                                                   bank[:, 0:4 * NCMP].rearrange("p (n c) -> p n c", n=4), b2k, None, ALU.add)
                elif half is None:
                    last = nc.vector.tensor_tensor(K.VCP[:NCMP, :], bank[:NCMP, 0:P], b2v[:NCMP, :], ALU.add)
                else:
                    last = nc.vector.tensor_tensor(K.VCS[:NCMP, 4 * half:4 * half + 4, :],
                                                   bank[:NCMP, :].rearrange("p (n c) -> p n c", n=4),
                                                   b2v[:NCMP, :].unsqueeze(1).to_broadcast([NCMP, 4, P]), ALU.add)
                last.then_inc(out, 1)

        @block.scalar
        def _(act):
            for n, (v, half) in enumerate(rounds):
                if n == 0:
                    act.wait_ge(biased, 2)
                m = 2 * NCMP if half is None else 8 * NCMP
                act.wait_ge(first, n + 1)
                if n >= 2:
                    act.wait_ge(second, n - 1)
                nc.scalar.activation(hid[n % 2][:, 0:m], K.bank[n % 2][:, 0:m], ACT.Gelu_apprx_tanh,
                                     bias=hb[:, v:v + 1]).then_inc(hidden, 1)
                if n == 3:
                    act.wait_ge(came_own, 128)
                    sample_operands(act, K, I)

        @block.tensor
        def _(pe):
            pe.wait_ge(came_w2, 16 * CMP_OPERANDS)
            def bias():
                for v in range(2):
                    pe.wait_ge(summed, v + 1)
                    nc.tensor.matmul(K.bank[6 + v][:, v:v + 1], sums[v], ones, start=True, stop=True).then_inc(pe_w1, 1)

            def hidden_rows(n):
                v, half = rounds[n]
                if half is None:
                    pe.wait_ge(came_own, 128)
                    src, m = own[v], 2 * NCMP
                else:
                    pe.wait_ge(K.slots_came[half], SLOT_PAGES)
                    src, m = pages[2 * half + v], 8 * NCMP
                if n >= 2:
                    pe.wait_ge(hidden, n - 1)
                for q in range(16):
                    if half is None:
                        rhs = src[:, :, q:q + 8 * NCMP - 7:8]
                    else:
                        rhs = src.rearrange("p g (n t) -> p g n t", n=4)[:, :, :, q:q + 8 * NCMP - 7:8]
                    last = nc.tensor.matmul(K.bank[n % 2][:, 0:m], w1[v][:, q, :], rhs, start=q == 0, stop=q == 15)
                last.then_inc(first, 1)

            def rows(n):
                v, half = rounds[n]
                pe.wait_ge(hidden, n + 1)
                if n >= 2:
                    pe.wait_ge(out, n - 1)
                seqs = 1 if half is None else 4
                bank = K.bank[2 + n % 2]
                for g in range(2):
                    if v == 0:
                        last = nc.tensor.matmul(bank[64 * g:64 * g + 64, 0:seqs * NCMP], w2[0],
                                                hid[n % 2][:, g * seqs * NCMP:(g + 1) * seqs * NCMP], start=True, stop=True)
                    else:
                        for s in range(seqs):
                            at = (g * seqs + s) * NCMP
                            last = nc.tensor.matmul(bank[:NCMP, s * P + 64 * g:s * P + 64 * g + 64],
                                                    hid[n % 2][:, at:at + NCMP], w2[1], start=True, stop=True)
                last.then_inc(second, 1)

            for v in range(2):
                pe.wait_ge(came_w[v], 16)
            for n in range(len(rounds)):
                hidden_rows(n)
                if n == 0:
                    bias()
                if n >= 1:
                    rows(n - 1)
            rows(len(rounds) - 1)


def sample_windows(sp, K, I, half):
    kw, vw = K.windows[half]
    sp.dma_start(kw, I["win_kt"][4 * half:4 * half + 4].rearrange("n p t -> p n t")).then_inc(K.windows_came[half], 16)
    for n in range(4):
        sp.dma_start(vw[:, n].rearrange("p (b c) -> p b c", b=4),
                     I["win_v"][4 * half + n].rearrange("(b p) c -> p b c", p=P)).then_inc(K.windows_came[half], 16)


SAMPLE_OPERANDS = 7 + 4 + NS


def sample_outputs(sp, K, half, of):
    for n in range(4):
        for g in range(2):
            to = bass.AP(K.o_dram.tensor, (half * 4 + n) * TS * DA + g * 256, [[HD, HPG], [DA, TS], [1, HD]])
            sp.dma_start(to, of[32 * n + 16 * g:32 * n + 16 * g + 16, 64 * g:64 * g + 64]).then_inc(K.sample_out, 16)


def sample_operands(sp, K, I):
    dq, gm, mn, ovl, mw, t4, gr, jj = K.sample_small
    for to, of in [(K.big[:, O_HT + 12288:O_HT + 12288 + I["oh_s"].shape[1]], I["oh_s"]), (dq, I["dq"]), (gm, I["gmat"]),
                   (mn, I["mask_new"]), (mw, I["mask_win"]), (ovl[:NCMP], I["overlap"]), (jj, I["jidx"])] + \
                  [(t4[32 * q:32 * q + 32, :], I["rel_bias"]) for q in range(4)]:
        sp.dma_start(to, of).then_inc(K.sample_came, 16)
    for half in range(2):
        for n in range(4):
            of = bass.AP(K.gates_dram.tensor, (half * 4 + n) * TS * 3 * H, [[3, H], [3 * H, TS], [1, 3]])
            sp.dma_start(gr[32 * n:32 * n + 32, half, :], of).then_inc(K.sample_came, 16)


def sample_attention(nc, K, I):
    S = K.sem
    ar = K.big[:, O_HT:BIG]
    SC = ar[:, 12288:12288 + 1664]
    SB = ar[:, 13952:13952 + 1664]
    PT = ar[:, 15616:15616 + 15 * P].rearrange("p (b n) -> p b n", b=15)
    a = 15616 + 15 * P
    tabq, (dq, gm, mn, ovl, mw, t4, gr, jj) = ar[:, a:a + 128], K.sample_small
    qbd = ar[:, a + 512:a + 768].rearrange("p (n r) -> p n r", n=NS)
    OS = K.sample_o
    imp, eq = ar[:, a + 940:a + 957], ar[:, a + 960:a + 974]
    st = ar[:, a + 990:a + 1010]
    PC = ar[:, a + 1020:a + 1020 + 63]
    assert a + 1083 <= BIG - O_HT - P
    c_sel, c_new, c_win, c_cmp, c_end = 0, 1024, 1088, 1600, 1663
    oh = SC
    came_c, zeroed, prep = K.sample_came, S("sa_zeroed"), S("sa_prep")
    pb, bias_done, scores, taken = S("sa_bias_product"), S("sa_bias"), S("sa_scores"), S("sa_scores_taken")
    vch, ach, impt, impu, nmr, exps = S("sa_dve"), S("sa_act"), S("sa_pe_imp"), S("sa_imp_taken"), S("sa_max"), S("sa_exp")
    pready, turned, ptaken, pv, otaken = S("sa_probs"), S("sa_turned"), S("sa_pt"), S("sa_pv"), S("sa_o")
    blocks = [(i * P, P) for i in range(8)] + [(c_new, 32), (c_new + 32, 32)] + \
             [(c_win + i * P, P) for i in range(4)] + [(c_cmp, NCMP)]

    with nc.Block() as block:
        @block.sync
        def _(sp):
            gather(sp, K, 1, "sel")
            sp.wait_ge(otaken, 1)
            sample_outputs(sp, K, 0, OS)

        @block.gpsimd
        def _(pool):
            nc.gpsimd.memset(qbd, 0.0).then_inc(zeroed, 1)

        @block.tensor
        def _(pe):
            pe.wait_ge(prep, 1)
            for i, (x, y) in enumerate([(0, 512), (512, 1024), (1024, 1536), (1536, c_end)]):
                last = nc.tensor.matmul(K.bank[i][:, 0:y - x], tabq, oh[:, x:y], start=True, stop=True)
            last.then_inc(pb, 1)
            pe.wait_ge(bias_done, 1)
            pe.wait_ge(prep, 3)

            def score(half):
                KS, VS = K.slots[half][:, 0], K.slots[half][:, 1]
                KW, VW = K.windows[half]
                pe.wait_ge(K.slots_came[half], 2 * SLOT_PAGES)
                pe.wait_ge(K.windows_came[half], 80)
                for n in range(4):
                    s = 4 * half + n
                    rows = slice(32 * n, 32 * n + 32)
                    for i in range(2):
                        nc.tensor.matmul(K.bank[i][rows, :], qbd[:, s, :], KS[:, n * 1024 + 512 * i:n * 1024 + 512 * i + 512], start=True, stop=True)
                    nc.tensor.matmul(K.bank[2][rows, 0:32], qbd[:, s, :], K.FM[:, 6, SEQ:T], start=True, stop=True)
                    nc.tensor.matmul(K.bank[2][rows, 32:64], qbd[:, s, :], K.FM[:, 7, SEQ:T], start=True, stop=True)
                    nc.tensor.matmul(K.bank[3][rows, :], qbd[:, s, :], KW[:, n], start=True, stop=True)
                    last = nc.tensor.matmul(K.bank[2][rows, 64:64 + NCMP], qbd[:, s, :], K.KCS[:, s, :], start=True, stop=True)
                last.then_inc(scores, 1)

            score(0)
            for half in range(2):
                VS, VW = K.slots[half][:, 1], K.windows[half][1]
                pe.wait_ge(impu, 3 * half + 1)
                nc.tensor.transpose(K.bank[4][:NCMP, 0:P], PC, K.ident[:, :]).then_inc(impt, 1)
                pe.wait_ge(impu, 3 * half + 2)
                nc.tensor.matmul(K.bank[4][:, 128:128 + NSEL], PT[:NCMP, 0, :], ovl[:NCMP, :], start=True, stop=True).then_inc(impt, 1)
                pe.wait_ge(impu, 3 * half + 3)
                nc.tensor.matmul(K.bank[4][:, 160:160 + NSEL], gm, imp, start=True, stop=True).then_inc(impt, 1)
                pe.wait_ge(pready, half + 1)
                if half:
                    pe.wait_ge(otaken, half)
                for i, (x, w) in enumerate(blocks):
                    b = i // 4
                    last = nc.tensor.transpose(K.bank[4 + b][:w, (i % 4) * P:(i % 4 + 1) * P], SC[:, x:x + w], K.ident[:, :])
                last.then_inc(turned, 1)
                if not half:
                    score(1)
                pe.wait_ge(ptaken, half + 1)
                for n in range(4):
                    s = 4 * half + n
                    rows = slice(32 * n, 32 * n + 32)
                    for i, (x, w) in enumerate(blocks):
                        if i < 8:
                            v = VS[:, (n * 8 + i) * P:(n * 8 + i + 1) * P]
                        elif i < 10:
                            v = K.VT[:SROWS, TILES - 1, (i - 8) * KV:(i - 7) * KV]
                        elif i < 14:
                            v = VW[:, n, (i - 10) * P:(i - 9) * P]
                        else:
                            v = K.VCS[:NCMP, s, :]
                        last = nc.tensor.matmul(K.bank[5][rows, 0:P], PT[:w, i, rows], v, start=i == 0, stop=i == 14)
                last.then_inc(pv, 1)

        @block.vector
        def _(dve):
            link = Chain(dve, vch)
            dve.wait_ge(came_c, 16 * SAMPLE_OPERANDS)
            nc.vector.tensor_tensor(tabq.rearrange("p (n h q) -> p n h q", n=4, h=H),
                                    t4.unsqueeze(1).unsqueeze(3).to_broadcast([P, 4, H, 4]),
                                    dq.rearrange("p (n h q) -> p n h q", n=4, h=H), ALU.mult).then_inc(prep, 1)
            dve.wait_ge(zeroed, 1)
            for g in range(2):
                nc.vector.tensor_scalar(qbd[64 * g:64 * g + 64, :, 16 * g:16 * g + 16].rearrange("p n (h q) -> p n h q", h=4),
                                        K.FM[64 * g:64 * g + 64, 0:4, SEQ:T].rearrange("p h (n q) -> p n h q", n=NS),
                                        HD ** -0.5, None, ALU.mult).then_inc(prep, 1)
            dve.wait_ge(pb, 1)
            for i, (x, y) in enumerate([(0, 512), (512, 1024), (1024, 1536), (1536, c_end)]):
                last = nc.vector.tensor_copy(SB[:, x:y], K.bank[i][:, 0:y - x])
            link(last)
            link(nc.vector.tensor_tensor(SB[:, c_win:c_win + 4], SB[:, c_win:c_win + 4], mw, ALU.add))
            dve.sem_inc(bias_done, 1)

            def outputs(half):
                dve.wait_ge(pv, half + 1)
                if half:
                    dve.wait_ge(K.sample_out, 128)
                nc.vector.tensor_copy(OS, K.bank[5][:, 0:P]).then_inc(otaken, 1)

            for half in range(2):
                dve.wait_ge(scores, half + 1)
                if half:
                    dve.wait_ge(turned, half)
                nc.vector.tensor_tensor(SC[:, c_cmp:c_end], K.bank[2][:, 64:64 + NCMP], SB[:, c_cmp:c_end], ALU.add)
                nc.vector.tensor_tensor(SC[:, 0:512], K.bank[0][:, :], SB[:, 0:512], ALU.add)
                nc.vector.tensor_tensor(SC[:, 512:1024], K.bank[1][:, :], SB[:, 512:1024], ALU.add)
                nc.vector.tensor_tensor(SC[:, c_win:c_win + 512], K.bank[3][:, :], SB[:, c_win:c_win + 512], ALU.add)
                link(nc.vector.tensor_tensor(SC[:, c_new:c_new + 64], K.bank[2][:, 0:64], SB[:, c_new:c_new + 64], ALU.add))
                link(nc.vector.tensor_tensor(SC[:, c_new:c_new + 64], SC[:, c_new:c_new + 64], mn[:, half, :], ALU.add))
                link(nc.vector.tensor_reduce(st[:, 0:1], SC[:, c_cmp:c_end], AX.X, ALU.max, negate=True))
                dve.sem_inc(nmr, 1)
                dve.wait_ge(exps, 3 * half + 1)
                link(nc.vector.reciprocal(st[:, 4:5], st[:, 3:4]))
                link(nc.vector.tensor_scalar(PC, SC[:, c_cmp:c_end], st[:, 4:5], None, ALU.mult))
                dve.sem_inc(impu, 1)
                if half:
                    outputs(0)
                dve.wait_ge(impt, 3 * half + 1)
                link(nc.vector.tensor_copy(PT[:NCMP, 0, :], K.bank[4][:NCMP, 0:P]))
                dve.sem_inc(impu, 1)
                dve.wait_ge(impt, 3 * half + 2)
                link(nc.vector.tensor_copy(imp, K.bank[4][:, 128:128 + NSEL]))
                dve.sem_inc(impu, 1)
                dve.wait_ge(impt, 3 * half + 3)
                cand = K.bank[4][:, 161:175]
                link(nc.vector.tensor_reduce(st[:, 5:6], cand, AX.X, ALU.min))
                link(nc.vector.scalar_tensor_tensor(eq, cand, st[:, 5:6], jj, ALU.is_equal, ALU.mult))
                link(nc.vector.tensor_reduce(st[:, 6:7], eq, AX.X, ALU.max))
                link(nc.vector.tensor_scalar(eq, jj, st[:, 6:7], NEG, ALU.is_equal, ALU.mult))
                part = SC[:, SELB:15 * SELB].rearrange("p (b k) -> p b k", b=14)
                link(nc.vector.tensor_tensor(part, part, eq.unsqueeze(2).to_broadcast([P, 14, SELB]), ALU.add))
                nc.vector.tensor_reduce(st[:, 1:2], SC[:, 0:c_new + 32], AX.X, ALU.max, negate=True)
                link(nc.vector.tensor_reduce(st[:, 2:3], SC[:, c_new + 32:c_cmp], AX.X, ALU.max, negate=True))
                dve.sem_inc(nmr, 1)
                dve.wait_ge(exps, 3 * half + 3)
                nc.vector.tensor_copy(st[:, 8:9], st[:, 3:4])
                link(nc.vector.tensor_copy(st[:, 9:11], st[:, 11:13]))
                link(nc.vector.reciprocal(st[:, 14:17], st[:, 8:11]))
                link(nc.vector.tensor_tensor(st[:, 14:17], st[:, 14:17], gr[:, half, :], ALU.mult))
                nc.vector.tensor_scalar(SC[:, 0:c_new + 32], SC[:, 0:c_new + 32], st[:, 15:16], None, ALU.mult)
                nc.vector.tensor_scalar(SC[:, c_new + 32:c_cmp], SC[:, c_new + 32:c_cmp], st[:, 16:17], None, ALU.mult)
                nc.vector.tensor_scalar(SC[:, c_cmp:c_end], SC[:, c_cmp:c_end], st[:, 14:15], None, ALU.mult).then_inc(pready, 1)
                dve.wait_ge(turned, half + 1)
                for b in range(4):
                    if b < 2:
                        last = nc.vector.tensor_copy(PT[:, 4 * b:4 * b + 4, :], K.bank[4 + b][:, :].rearrange("p (b n) -> p b n", b=4))
                    elif b == 2:
                        nc.vector.tensor_copy(PT[:32, 8:10, :], K.bank[6][:32, 0:256].rearrange("p (b n) -> p b n", b=2))
                        last = nc.vector.tensor_copy(PT[:, 10:12, :], K.bank[6][:, 256:512].rearrange("p (b n) -> p b n", b=2))
                    else:
                        nc.vector.tensor_copy(PT[:, 12:14, :], K.bank[7][:, 0:256].rearrange("p (b n) -> p b n", b=2))
                        last = nc.vector.tensor_copy(PT[:NCMP, 14, :], K.bank[7][:NCMP, 256:384])
                last.then_inc(ptaken, 1)
            outputs(1)

        @block.scalar
        def _(act):
            sample_windows(act, K, I, 1)
            for half in range(2):
                act.wait_ge(nmr, 2 * half + 1)
                nc.scalar.activation(SC[:, c_cmp:c_end], SC[:, c_cmp:c_end], ACT.Exp, bias=st[:, 0:1],
                                     accum_out=st[:, 3:4]).then_inc(exps, 1)
                act.wait_ge(nmr, 2 * half + 2)
                nc.scalar.activation(SC[:, 0:c_new + 32], SC[:, 0:c_new + 32], ACT.Exp, bias=st[:, 1:2],
                                     accum_out=st[:, 11:12]).then_inc(exps, 1)
                nc.scalar.activation(SC[:, c_new + 32:c_cmp], SC[:, c_new + 32:c_cmp], ACT.Exp, bias=st[:, 2:3],
                                     accum_out=st[:, 12:13]).then_inc(exps, 1)


def prompt_attention(nc, K, I):
    S = K.sem
    ar = K.big[:, O_HT:BIG]
    strips = [ar[:, 2560 * g:2560 * (g + 1)] for g in range(2)]
    qz = [ar[:, 5120 + 1024 * g:5120 + 1024 * (g + 1)] for g in range(2)]
    sc = [ar[:, 7168 + 1728 * b:7168 + 1728 * (b + 1)] for b in range(2)]
    pt = [ar[:, 10624 + 1792 * b:10624 + 1792 * (b + 1)].rearrange("p (b n) -> p b n", b=14) for b in range(2)]
    gh = [ar[:, 14208 + 24 * g:14208 + 24 * (g + 1)].rearrange("p (t b) -> p t b", b=3) for g in range(2)]
    sta = [ar[:, 14300 + 16 * b:14300 + 16 * (b + 1)] for b in range(2)]
    strip_came = [S(f"pa_strip{g}") for g in range(2)]
    zeroed, steps = S("pa_zeroed"), [S("pa_dve_steps"), S("pa_pe_steps")]
    q_ready = [S(f"pa_q{g}") for g in range(2)]
    scores, s_taken, negmax, exps = S("pa_scores"), S("pa_scores_taken"), S("pa_negmax"), S("pa_exp")
    probs, pv, o_taken, vch = S("pa_probs"), S("pa_pv"), S("pa_o_taken"), S("pa_dve")
    TB = 3
    turned = [S(f"pa_turned{b}") for b in range(TB)]
    t_taken = [S(f"pa_turned_taken{b}") for b in range(TB)]
    U = 16
    ORDER = [*range(8), *range(7, -1, -1)]
    CHAIN = 2 * U + 2

    def blocks(i):
        lo = max(0, i - 4)
        return [(b * P, P, 0, b) for b in range(i + 1)] + \
               [(1024 + (b - lo) * P, P, 1, b) for b in range(lo, i + 1)] + [(1664, NCMP, 2, 0)]

    groups, per = [], [0] * TB
    for u in range(U):
        bl = blocks(ORDER[u])
        mine = []
        for n, x in enumerate(range(0, len(bl), 4)):
            per[n % TB] += 1
            mine.append((n % TB, per[n % TB], bl[x:x + 4], x))
        groups.append(mine)

    with nc.Block() as block:
        @block.sync
        def _(sp):
            for j in range(4):
                for g in range(2):
                    h = j + 4 * g
                    if j:
                        sp.wait_ge(s_taken, (j - 1) * U + 8 * g + 9)
                    base = h * (VECS + VECW)
                    sp.dma_start(strips[g][:, 0:STRS], bass.AP(K.vec_dram.tensor, base, [[1, P], [1, STRS]])).then_inc(strip_came[g], 16)
                    sp.dma_start(strips[g][:, STRS:], bass.AP(K.vec_dram.tensor, base + VECS, [[1, P], [1, STRW]])).then_inc(strip_came[g], 16)
                if j == 0:
                    for to, of in x_loads(K, I):
                        sp.dma_start(to, of).then_inc(K.x_came, 16)
                    sample_outputs(sp, K, 1, K.sample_o)
                    sp.wait_ge(K.sample_out, 256)
                    sp.dma_start(K.M[:SROWS, TILES - 1, DA:D], K.o_dram).then_inc(K.sample_back, 16)

            sp.wait_ge(K.sample_back, 16)

        @block.gpsimd
        def _(pool):
            nc.gpsimd.memset(qz[0][64:128, :], 0.0).then_inc(zeroed, 1)
            nc.gpsimd.memset(qz[1][0:64, :], 0.0).then_inc(zeroed, 1)

        @block.tensor
        def _(pe):
            pe.sem_inc(pv, 2)
            pe.wait_ge(zeroed, 2)

            def score(j, u):
                g, i = u // 8, ORDER[u]
                if u % 8 == 0:
                    pe.wait_ge(q_ready[g], j + 1)
                pe.wait_ge(s_taken, j * U + u + 1)
                q = qz[g][:, i * P:(i + 1) * P]
                w = (i + 1) * P
                for x in range(0, w, 512):
                    nc.tensor.matmul(K.ps4[:, x:min(x + 512, w)], q, K.FM[:, 6, x:min(x + 512, w)], start=True, stop=True)
                lo = max(0, i - 4) * P
                ww = w - lo
                for x in range(0, ww, 512):
                    y = min(x + 512, ww)
                    nc.tensor.matmul(K.ps4[:, 1024 + x:1024 + y], q, K.FM[:, 7, lo + x:lo + y], start=True, stop=True)
                nc.tensor.matmul(K.ps4[:, 1664:1664 + NCMP], q, K.KCP[:, :], start=True, stop=True).then_inc(scores, 1)

            def turn(j, u, group):
                b, cnt, bl, _ = group
                pe.wait_ge(t_taken[b], j * per[b] + cnt)
                if bl[0][1] < P:
                    pe.sem_inc(steps[1], 1)
                for x, (col, w, _, _) in enumerate(bl):
                    last = nc.tensor.transpose(K.bank[4 + b][:w, x * P:(x + 1) * P], sc[u % 2][:, col:col + w], K.ident[:, :])
                last.then_inc(turned[b], 1)

            def multiply(j, u, group):
                b, cnt, bl, first = group
                end = groups[u][-1] is group
                pe.wait_ge(t_taken[b], j * per[b] + cnt + 1)
                for x, (_, w, kind, t) in enumerate(bl):
                    v = K.VCP[:NCMP, :] if kind == 2 else K.VT[:, t, kind * KV:(kind + 1) * KV]
                    last = nc.tensor.matmul(K.bank[7][:, 0:P], pt[u % 2][:w, first + x, :], v,
                                            start=first + x == 0, stop=end and x == len(bl) - 1)
                if end:
                    last.then_inc(pv, 1)

            with pe.Fori(0, 4) as j:
                score(j, 0)
                score(j, 1)
                for u in range(U):
                    pe.wait_ge(probs, j * U + u + 1)
                    g = groups[u]
                    for group in g[:TB]:
                        turn(j, u, group)
                    pe.wait_ge(o_taken, j * U + u + 1)
                    for n, group in enumerate(g):
                        multiply(j, u, group)
                        if n + TB < len(g):
                            turn(j, u, g[n + TB])
                    if u + 2 < U:
                        score(j, u + 2)

        @block.vector
        def _(dve):
            dve.sem_inc(s_taken, 1)
            count = [0]

            def link(ins, j):
                count[0] += 1
                ins.then_inc(vch, 1)
                dve.wait_ge(vch, j * CHAIN + count[0])

            def add_bias(j, u):
                g, i = u // 8, ORDER[u]
                s, mx = sc[u % 2], sta[u % 2]
                if u % 8 == 0:
                    dve.wait_ge(strip_came[g], j * 32 + 32)
                dve.wait_ge(scores, j * U + u + 1)
                dve.wait_ge(pv, j * U + u + 1)
                dve.sem_inc(steps[0], 1)
                w = (i + 1) * P
                ww = min(i + 1, 5) * P
                at = 992 + P * i
                nc.vector.tensor_tensor_reduce(out=s[:, 0:w], in0=K.ps4[:, 0:w], in1=strips[g][:, 895 + w:895:-1], scale=1.0,
                                               scalar=-3e38, op0=ALU.add, op1=ALU.max, accum_out=mx[:, 1:2])
                nc.vector.tensor_tensor_reduce(out=s[:, 1024:1024 + ww], in0=K.ps4[:, 1024:1024 + ww],
                                               in1=strips[g][:, STRS + ww - 1:STRS - 1:-1], scale=1.0,
                                               scalar=-3e38, op0=ALU.add, op1=ALU.max, accum_out=mx[:, 2:3])
                nc.vector.tensor_tensor_reduce(out=s[:, 1664:1664 + NCMP], in0=K.ps4[:, 1664:1664 + NCMP],
                                               in1=strips[g][:, at:at - 16 * NCMP + 15:-16] if i else strips[g][:, at::-16], scale=1.0,
                                               scalar=-3e38, op0=ALU.add, op1=ALU.max, accum_out=mx[:, 0:1]).then_inc(s_taken, 1)
                dve.wait_ge(s_taken, j * U + u + 2)
                nc.vector.tensor_scalar(mx[:, 4:7], mx[:, 0:3], -1.0, None, ALU.mult).then_inc(negmax, 1)

            def gate(j, u):
                g, i = u // 8, ORDER[u]
                s, m = sc[u % 2], sta[u % 2]
                w = (i + 1) * P
                ww = min(i + 1, 5) * P
                dve.wait_ge(exps, j * 3 * U + 3 * u + 3)
                link(nc.vector.reciprocal(m[:, 12:15], m[:, 8:11]), j)
                link(nc.vector.tensor_tensor(m[:, 12:15], m[:, 12:15], gh[g][:, i, :], ALU.mult), j)
                nc.vector.tensor_scalar(s[:, 0:w], s[:, 0:w], m[:, 13:14], None, ALU.mult)
                nc.vector.tensor_scalar(s[:, 1024:1024 + ww], s[:, 1024:1024 + ww], m[:, 14:15], None, ALU.mult)
                nc.vector.tensor_scalar(s[:, 1664:1664 + NCMP], s[:, 1664:1664 + NCMP], m[:, 12:13], None, ALU.mult).then_inc(probs, 1)

            with dve.Fori(0, 4) as j:
                count[0] = 0
                for g in range(2):
                    src = K.FM[64 * g:64 * g + 64, bass.ds(j, 1), 0:SEQ].rearrange("p a n -> p (a n)")
                    nc.vector.tensor_scalar(qz[g][64 * g:64 * g + 64, :], src, HD ** -0.5, None, ALU.mult).then_inc(q_ready[g], 1)
                    link(nc.vector.tensor_copy(gh[g], K.GS[:, bass.ds(j + 4 * g, 1), :, :].rearrange("p a t b -> p (a t) b")), j)
                add_bias(j, 0)
                for u in range(U):
                    gate(j, u)
                    if u + 1 < U:
                        add_bias(j, u + 1)

        @block.scalar
        def _(act):
            for b in range(TB):
                act.sem_inc(t_taken[b], 1)
            act.sem_inc(o_taken, 1)

            def exp(j, u):
                i = ORDER[u]
                s, m = sc[u % 2], sta[u % 2]
                w = (i + 1) * P
                ww = min(i + 1, 5) * P
                act.wait_ge(negmax, j * U + u + 1)
                for b, x, y in ((1, 0, w), (2, 1024, 1024 + ww), (0, 1664, 1664 + NCMP)):
                    nc.scalar.activation(s[:, x:y], s[:, x:y], ACT.Exp, bias=m[:, 4 + b:5 + b],
                                         accum_out=m[:, 8 + b:9 + b]).then_inc(exps, 1)

            with act.Fori(0, 4) as j:
                exp(j, 0)
                for u in range(U):
                    g, i = u // 8, ORDER[u]
                    act.wait_ge(pv, j * U + u + 1)
                    for b, cnt, bl, x in groups[u]:
                        act.wait_ge(turned[b], j * per[b] + cnt)
                        full = [y for y in bl if y[1] == P]
                        if full:
                            last = nc.scalar.copy(pt[u % 2][:, x:x + len(full), :],
                                                  K.bank[4 + b][:, 0:len(full) * P].rearrange("p (b n) -> p b n", n=P))
                        if len(full) < len(bl):
                            last = nc.scalar.copy(pt[u % 2][:NCMP, x + len(full), :],
                                                  K.bank[4 + b][:NCMP, len(full) * P:(len(full) + 1) * P])
                        last.then_inc(t_taken[b], 1)
                    if u + 1 < U:
                        exp(j, u + 1)
                    act.wait_ge(pv, j * U + u + 3)
                    dst = K.M[:, i, bass.ds(j * HD + (DA + 4 * g * HD), HD)]
                    nc.scalar.activation(dst, K.bank[7][:, 64 * g:64 * g + 64], ACT.Copy).then_inc(o_taken, 1)


def bias_rows(nc, K, I, fm):
    S = K.sem
    came, rows, out, product, set_ = S("bias_came"), S("bias_rows"), S("bias_dram"), S("bias_product"), S("bias_table")
    L = VECS + VECW
    oh = K.top[:BUCKETS + 1, O_M:O_M + L]
    vec = K.top[:H, O_M + L:O_M + 2 * L]
    cuts = [(x, min(x + 512, L)) for x in range(0, L, 512)]

    def sync(sp):
        sp.dma_start(oh, I["oh_v"]).then_inc(came, 16)
        sp.wait_ge(set_, 1)
        sp.dma_start(K.table[:BUCKETS, :], I["rel_bias"]).then_inc(came, 16)
        sp.dma_start(K.page_table[:, :], I["page_table"]).then_inc(came, 16)
        fm.load(sp)
        w = K.big[:, O_W:O_W + KD * TMW].rearrange("p (k n) -> p k n", k=KD)
        for k in range(KD):
            sp.dma_start(w[:, k, :], I["w_tm"][k]).then_inc(K.wtm_sem, 16)

    def store(sp):
        sp.wait_ge(rows, len(cuts))
        sp.dma_start(K.vec_dram, vec).then_inc(out, 16)

    def gpsimd(pool):
        nc.gpsimd.memset(K.table[:, :], NEG).then_inc(set_, 1)

    def tensor(pe, n):
        x, y = cuts[n]
        if n == 0:
            pe.wait_ge(came, 48)
        if n >= 2:
            pe.wait_ge(rows, n - 1)
        nc.tensor.matmul(K.bank[4 + n % 2][:H, 0:y - x], K.table[:, :], oh[:, x:y], start=True, stop=True).then_inc(product, 1)

    def scalar(act):
        for n, (x, y) in enumerate(cuts):
            act.wait_ge(product, n + 1)
            nc.scalar.activation(vec[:, x:y], K.bank[4 + n % 2][:H, 0:y - x], ACT.Copy).then_inc(rows, 1)

    beside = {"sync": sync, "gpsimd": gpsimd, "scalar": scalar}
    for n in range(len(cuts)):
        beside["tensor", TILES - len(cuts) + n] = lambda pe, n=n: tensor(pe, n)
    return beside, store, out


def memory_values(nc, K, I, O, memt, mkt, mv, weights, following):
    S = K.sem
    w, came, _ = weights
    done, taken = S("mv_product"), S("mv_taken")
    with nc.Block() as block:
        @block.sync
        def _(sp):
            following.load(sp)
            sp.dma_start(O["mem_k"], mkt).then_inc(K.out_sem, 16)
            sp.wait_ge(taken, 4)
            sp.dma_start(O["mem_v"].rearrange("t p n -> p t n"), mv).then_inc(K.out_sem, 16)
            K.outs(2)

        @block.tensor
        def _(pe):
            for j in range(4):
                h, t = j // 2, j % 2
                pe.wait_ge(came[h], 16)
                for k in range(KD):
                    last = nc.tensor.matmul(K.bank[j][:, :], memt[:, k, t * P:(t + 1) * P], w[:, h, k, :],
                                            start=k == 0, stop=k == KD - 1)
                last.then_inc(done, 1)

        @block.scalar
        def _(act):
            for j in range(4):
                h, t = j // 2, j % 2
                act.wait_ge(done, j + 1)
                nc.scalar.activation(mv[:, t, h * 512:(h + 1) * 512], K.bank[j][:, :], ACT.Copy).then_inc(taken, 1)


class CrossSample:

    def __init__(self, K):
        S = K.sem
        m, w = K.top[:, O_M:O_FM], K.big[:, O_W:BIG]
        fm = [K.top[:, O_FM + 2048 * i:O_FM + 2048 * (i + 1)] for i in range(4)]
        wa, wb, wc = (w[:, o:o + 2048] for o in (4160, 6208, 8384))
        vt, low, high = K.top[:, O_VT:O_VT + 2048], m[:, 0:2048], m[:, 2048:4096]
        keys = (low, high, wc, vt, m[:, 4096:6144], m[:, 6144:8192], fm[2], fm[3])
        values = (wa, wb, fm[0], fm[1], low, high, wc, vt)
        self.kr = [x.rearrange("p (c m) -> p c m", c=KD) for x in keys]
        self.vr = [x.rearrange("p (m n) -> p m n", m=2) for x in values]
        self.qbd = K.top[:, O_TMP:O_TMP + 2048].rearrange("p (c n r) -> p c n r", c=KD, n=NS)
        self.tmp = K.top[:, O_TMP + 2048:O_TMP + 2048 + 1544]
        assert O_TMP + 2048 + 1544 <= TOP
        self.k_came, self.v_came = ([S(f"xs_{x}{n}") for n in range(NS)] for x in "kv")
        self.zeroed, self.q_ready = S("xs_zeroed"), S("xs_q")

    def load_keys(self, sp, I, n):
        sp.dma_start(self.kr[n], I["mem_kt"][n]).then_inc(self.k_came[n], 16)

    def load_values(self, sp, I, n):
        sp.dma_start(self.vr[n], I["mem_v"][n].rearrange("(m p) n -> p m n", p=P)).then_inc(self.v_came[n], 16)


def cross_prompt(nc, K, I, qx, mkt, mv, sample):
    S = K.sem
    w = K.big[:, O_W:BIG]
    px = [w[:, 1024 * b:1024 * (b + 1)].rearrange("p (h m) -> p h m", h=XH) for b in range(2)]
    pt = [w[:, 2048 + 1024 * b:2048 + 1024 * (b + 1)].rearrange("p (b n) -> p b n", b=8) for b in range(2)]
    st = [w[:, 4096 + 16 * b:4096 + 16 * (b + 1)] for b in range(2)]
    n = SEQ // P
    scores, neg, exps, probs = S("xp_scores"), S("xp_negmax"), S("xp_exp"), S("xp_probs")
    turned, taken, pv, o_taken, vch = S("xp_turned"), S("xp_turned_taken"), S("xp_pv"), S("xp_o_taken"), S("xp_dve")
    with nc.Block() as block:
        @block.sync
        def _(sp):
            for n in range(4):
                sample.load_keys(sp, I, n)
            for n in range(2):
                sample.load_values(sp, I, n)

        @block.gpsimd
        def _(pool):
            nc.gpsimd.memset(sample.qbd, 0.0).then_inc(sample.zeroed, 1)

        @block.tensor
        def _(pe):
            def score(t):
                if t >= 2:
                    pe.wait_ge(exps, XH * (t - 1))
                for h in range(XH):
                    for k in range(2):
                        last = nc.tensor.matmul(K.bank[2 * (t % 2) + h // 2][:, (h % 2) * MEM:(h % 2 + 1) * MEM],
                                                qx[:, 2 * h + k, t * P:(t + 1) * P], mkt[:, 2 * h + k, :],
                                                start=k == 0, stop=k == 1)
                last.then_inc(scores, 1)

            score(0)
            for t in range(n):
                pe.wait_ge(probs, t + 1)
                for b in range(2):
                    if t:
                        pe.wait_ge(taken, 2 * (t - 1) + b + 1)
                    for x in range(4):
                        h, m = 2 * b + x // 2, x % 2
                        last = nc.tensor.transpose(K.bank[4 + b][:, x * P:(x + 1) * P], px[t % 2][:, h, m * P:(m + 1) * P], K.ident[:, :])
                    last.then_inc(turned, 1)
                if t + 1 < n:
                    score(t + 1)
                for b in range(2):
                    pe.wait_ge(taken, 2 * t + b + 1)
                    if t:
                        pe.wait_ge(o_taken, 2 * (t - 1) + b + 1)
                    for x in range(4):
                        c = 4 * b + x
                        h = c // 2
                        for m in range(2):
                            last = nc.tensor.matmul(K.bank[6 + b][:, x * P:(x + 1) * P], mv[:, m, c * P:(c + 1) * P],
                                                    pt[t % 2][:, 2 * h + m, :], start=m == 0, stop=m == 1)
                    last.then_inc(pv, 1)

        @block.vector
        def _(dve):
            link = Chain(dve, vch)

            def maxima(t):
                m = st[t % 2]
                dve.wait_ge(scores, t + 1)
                b = 2 * (t % 2)
                link(nc.vector.tensor_reduce(m[:, 0:4], K.ps[:, b * 512:(b + 2) * 512].rearrange("p (h m) -> p h m", h=XH),
                                             AX.X, ALU.max))
                nc.vector.tensor_scalar(m[:, 4:8], m[:, 0:4], -(XHD ** -0.5), None, ALU.mult).then_inc(neg, 1)

            maxima(0)
            dve.wait_ge(sample.zeroed, 1)
            for c in range(KD):
                nc.vector.tensor_copy(sample.qbd[:, c, :, 4 * (c // 2):4 * (c // 2) + 4],
                                      qx[:, c, SEQ:T].rearrange("p (n q) -> p n q", n=NS)).then_inc(sample.q_ready, 1)
            for t in range(n):
                m = st[t % 2]
                dve.wait_ge(exps, XH * (t + 1))
                link(nc.vector.reciprocal(m[:, 12:16], m[:, 8:12]))
                nc.vector.tensor_tensor(px[t % 2], px[t % 2], m[:, 12:16].unsqueeze(2).to_broadcast([P, XH, MEM]),
                                        ALU.mult).then_inc(probs, 1)
                for b in range(2):
                    dve.wait_ge(turned, 2 * t + b + 1)
                    if t >= 2:
                        dve.wait_ge(pv, 2 * (t - 1))
                    nc.vector.tensor_copy(pt[t % 2][:, 4 * b:4 * b + 4, :],
                                          K.bank[4 + b][:, :].rearrange("p (b n) -> p b n", b=4)).then_inc(taken, 1)
                if t + 1 < n:
                    maxima(t + 1)

        @block.scalar
        def _(act):
            def exp(t):
                m = st[t % 2]
                act.wait_ge(neg, t + 1)
                if t >= 2:
                    act.wait_ge(turned, 2 * (t - 1))
                for h in range(XH):
                    nc.scalar.activation(px[t % 2][:, h, :], K.bank[2 * (t % 2) + h // 2][:, (h % 2) * MEM:(h % 2 + 1) * MEM],
                                         ACT.Exp, bias=m[:, 4 + h:5 + h], scale=XHD ** -0.5,
                                         accum_out=m[:, 8 + h:9 + h]).then_inc(exps, 1)

            exp(0)
            for t in range(n):
                if t + 1 < n:
                    exp(t + 1)
                for b in range(2):
                    act.wait_ge(pv, 2 * t + b + 1)
                    nc.scalar.activation(K.HT[:, 4 * b:4 * b + 4, t * P:(t + 1) * P],
                                         K.bank[6 + b][:, :].rearrange("p (c n) -> p c n", c=4), ACT.Copy).then_inc(o_taken, 1)


def cross_sample(nc, K, I, sample, weights):
    S = K.sem
    kr, vr, qbd, tmp, k_came, v_came = sample.kr, sample.vr, sample.qbd, sample.tmp, sample.k_came, sample.v_came
    px, pt, ox, st = tmp[:, 0:256], tmp[:, 256:512].rearrange("p (m r) -> p m r", m=2), tmp[:, 512:1536], tmp[:, 1536:1544]
    k_used = S("xs_keys_used")
    neg, exps, probs, turned, taken = S("xs_negmax"), S("xs_exp"), S("xs_probs"), S("xs_turned"), S("xs_turned_taken")
    pv, o_taken, o_turned, vch = S("xs_pv"), S("xs_o_taken"), S("xs_o_turned"), S("xs_dve")
    with nc.Block() as block:
        @block.sync
        def _(sp):
            for n in range(2, 4):
                sample.load_values(sp, I, n)
            for n in range(4, NS):
                sample.load_keys(sp, I, n)
            for n in range(4, NS):
                sp.wait_ge(k_used, n - 3)
                sample.load_values(sp, I, n)
            sp.wait_ge(pv, 2)
            weights[2](sp)

        @block.tensor
        def _(pe):
            pe.wait_ge(sample.q_ready, KD)
            for half in range(2):
                if half:
                    pe.wait_ge(exps, half)
                for x in range(4):
                    n = 4 * half + x
                    pe.wait_ge(k_came[n], 16)
                    for c in range(KD):
                        last = nc.tensor.matmul(K.bank[0][32 * x:32 * x + 32, 0:MEM], qbd[:, c, n, :], kr[n][:, c, :],
                                                start=c == 0, stop=c == KD - 1)
                    last.then_inc(k_used, 1)
                pe.wait_ge(probs, half + 1)
                for m in range(2):
                    last = nc.tensor.transpose(K.bank[1][:, m * P:(m + 1) * P], px[:, m * P:(m + 1) * P], K.ident[:, :])
                last.then_inc(turned, 1)
                pe.wait_ge(taken, half + 1)
                for x in range(4):
                    n = 4 * half + x
                    pe.wait_ge(v_came[n], 16)
                    for b in range(2):
                        for m in range(2):
                            last = nc.tensor.matmul(K.bank[2 + b][32 * x:32 * x + 32, :], pt[:, m, 32 * x:32 * x + 32],
                                                    vr[n][:, m, b * 512:(b + 1) * 512], start=m == 0, stop=m == 1)
                    last.then_inc(pv, 1)
                pe.wait_ge(o_taken, half + 1)
                for c in range(KD):
                    last = nc.tensor.transpose(K.bank[4 + c // 4][:, (c % 4) * P:(c % 4 + 1) * P], ox[:, c * P:(c + 1) * P], K.ident[:, :])
                last.then_inc(o_turned, 1)

        @block.vector
        def _(dve):
            link = Chain(dve, vch)
            for half in range(2):
                dve.wait_ge(k_used, 4 * half + 4)
                link(nc.vector.tensor_reduce(st[:, 0:1], K.bank[0][:, 0:MEM], AX.X, ALU.max))
                nc.vector.tensor_scalar(st[:, 1:2], st[:, 0:1], -(XHD ** -0.5), None, ALU.mult).then_inc(neg, 1)
                dve.wait_ge(exps, half + 1)
                link(nc.vector.reciprocal(st[:, 3:4], st[:, 2:3]))
                nc.vector.tensor_scalar(px, px, st[:, 3:4], None, ALU.mult).then_inc(probs, 1)
                dve.wait_ge(turned, half + 1)
                nc.vector.tensor_copy(pt, K.bank[1][:, 0:2 * P].rearrange("p (m r) -> p m r", m=2)).then_inc(taken, 1)
                dve.wait_ge(pv, 4 * half + 4)
                nc.vector.tensor_copy(ox, K.ps[:, 1024:2048]).then_inc(o_taken, 1)
                dve.wait_ge(o_turned, half + 1)
                for c in range(KD):
                    src = K.bank[4 + c // 4][:, (c % 4) * P:(c % 4 + 1) * P].rearrange("p (n r) -> p n r", n=4)[:, :, 4 * (c // 2):4 * (c // 2) + 4]
                    last = nc.vector.tensor_copy(K.HT[:, c, SEQ + 16 * half:SEQ + 16 * half + 16].rearrange("p (n q) -> p n q", n=4), src)
                link(last)

        @block.scalar
        def _(act):
            for half in range(2):
                act.wait_ge(neg, half + 1)
                if half:
                    act.wait_ge(turned, half)
                nc.scalar.activation(px, K.bank[0][:, 0:MEM], ACT.Exp, bias=st[:, 1:2], scale=XHD ** -0.5,
                                     accum_out=st[:, 2:3]).then_inc(exps, 1)


GRP = 4
TPAD = TILES * P


def ffn(nc, K, I, O, mem, high, low, landing, w_came):
    S = K.sem
    sb = lambda name, shape, dt=F32: mem.enter_context(nc.sbuf_tensor(name, shape, dt))
    w_high, w_low = sb("ff_weights_high", [P, 2, KD, P], F32R), sb("ff_weights_low", [P, 2, KD, P], F32R)
    a_high, a_low = sb("ff_act_high", [P, GRP, TPAD], F32R), sb("ff_act_low", [P, GRP, TPAD], F32R)
    d_landing = sb("ff_down", [P, GRP, 256])
    d_high, d_low = sb("ff_down_high", [P, 2, GRP, 256], F32R), sb("ff_down_low", [P, 2, GRP, 256], F32R)
    ext, ct = sb("ff_row", [P, 1074])[:, :], sb("ff_conv", [P, T])[:, :]
    cpt = sb("ff_small", [P, 848])
    g, square = sb("final_gain", [P, D]), sb("final_square", [P, D])
    prev = cpt[:, 0:FC * 16].rearrange("p (c n) -> p c n", c=FC)
    co = cpt[:, 352:352 + FC * 18].rearrange("p (c n) -> p c n", c=FC)
    cwb = cpt[:, 752:752 + FC * 4].rearrange("p (c n) -> p c n", c=FC)
    cw = cpt[:, 840:844]
    w_split, low_done = ([S(f"ff_{s}_{x}") for s in ("up", "gate")] for x in ("high", "low"))
    small, zeroed, padded = S("ff_small_came"), S("ff_zeroed"), S("ff_padded")
    up_done, gate_done, up_taken, gate_taken = S("ff_up"), S("ff_gate"), S("ff_up_taken"), S("ff_gate_taken")
    conv_done, gelu_done, vch = S("ff_conv_done"), S("ff_gelu"), S("ff_dve")
    act_made, act_split, act_low = S("ff_act"), S("ff_act_high_made"), S("ff_act_low_made")
    d_came, d_split, d_low_made = S("ff_down_came"), S("ff_down_high_made"), S("ff_down_low_made")
    down_done, down_taken, gain_came = S("ff_down_product"), S("ff_down_taken"), S("fin_gain")
    squares, std_ready, rs_ready, y = S("fin_squares"), S("fin_std"), S("fin_rstd"), S("fin_y")
    pieces = [(0, FREE3), (FREE3, 2 * FREE3), (2 * FREE3, T)]
    ss, std, rs = (K.stat[:, i, :TILES] for i in range(3))
    QUARTERS, PRODUCTS, LINKS = 4, 4 * TILES, 6
    loops = (FC - 1) // GRP
    left = FC - loops * GRP
    assert 1 + loops * GRP == FC - 1

    def at(p, e, each, more):
        return p * (GRP * each) + (e * each + more)

    with nc.Block() as block:
        @block.sync
        def _(sp):
            sp.dma_start(prev, I["conv_prev"]).then_inc(small, 16)
            sp.dma_start(cwb, I["conv_wb"]).then_inc(small, 16)
            sp.dma_start(g[:, :], I["g_final"].to_broadcast([P, D])).then_inc(gain_came, 16)

            def down_weights(p, q):
                n = QUARTERS * p + q
                if n:
                    sp.wait_ge(d_low_made, n)
                k = min(GRP, FC - GRP * p)
                sp.dma_start(d_landing[:, 0:k, :], I["w_down"][q][:, GRP * p:GRP * p + k, :]).then_inc(d_came, 16)

            for c in range(1, FC + 1):
                for x, name in enumerate(("w_up", "w_gate")):
                    if c < FC:
                        sp.wait_ge(low_done[x], c)
                        sp.dma_start(landing[:, x], I[name][c]).then_inc(w_came[x], 16)
                    if c > 1 and c % GRP == 1 or c == FC:
                        p = (c - 1) // GRP - (c < FC)
                        for q in range(2 * x, 2 * x + 2):
                            down_weights(p, q)
            sp.wait_ge(conv_done, FC)
            sp.dma_start(O["conv"], co).then_inc(K.out_sem, 16)
            for t in range(TILES):
                sp.wait_ge(y, t + 1)
                to = O["y_prompt"][t] if t < TILES - 1 else O["y_sample"]
                sp.dma_start(to, K.X[:rows_of(t), t, :]).then_inc(K.out_sem, 16)
            sp.wait_ge(K.out_sem, 16 * K.outs(TILES + 1))

        @block.gpsimd
        def _(pool):
            def weights(s, p, e):
                pool.wait_ge(w_split[s], at(p, e, 1, 1))
                nc.gpsimd.tensor_tensor(w_low[:, s], landing[:, s], w_high[:, s], ALU.subtract).then_inc(low_done[s], 1)

            def down(p, q, k=GRP):
                pool.wait_ge(d_split, p * QUARTERS + (q + 1))
                nc.gpsimd.tensor_tensor(d_low[:, q % 2, 0:k], d_landing[:, 0:k], d_high[:, q % 2, 0:k],
                                        ALU.subtract).then_inc(d_low_made, 1)

            def activation(p, e):
                pool.wait_ge(act_split, at(p, e, 1, 1))
                nc.gpsimd.tensor_tensor(a_low[:, e % GRP, 0:T], ct, a_high[:, e % GRP, 0:T], ALU.subtract).then_inc(act_low, 1)

            weights(0, 0, 0)
            weights(1, 0, 0)
            zeros = square[:, 0:GRP * (TPAD - T)].rearrange("p (k n) -> p k n", k=GRP)
            nc.gpsimd.memset(ext[:, 0:2], 0.0).then_inc(zeroed, 1)
            nc.gpsimd.memset(zeros, 0.0).then_inc(zeroed, 1)
            pool.wait_ge(zeroed, 2)
            for x in (a_high, a_low):
                nc.gpsimd.tensor_tensor(x[:, :, T:TPAD], zeros, zeros, ALU.subtract).then_inc(padded, 1)
            weights(0, 0, 1)
            weights(1, 0, 1)
            activation(0, 0)
            with pool.Fori(0, loops) as p:
                for e in range(1, GRP + 1):
                    weights(0, p, e + 1)
                    if e == GRP:
                        down(p, 0)
                        down(p, 1)
                    weights(1, p, e + 1)
                    if e == GRP:
                        down(p, 2)
                        down(p, 3)
                    activation(p, e)
            down(loops, 0, left)
            down(loops, 1, left)
            activation(loops, 1)
            down(loops, 2, left)
            down(loops, 3, left)

        @block.tensor
        def _(pe):
            def up_and_gate(p, e):
                for s, (done, taken) in enumerate(((up_done, up_taken), (gate_done, gate_taken))):
                    pe.wait_ge(low_done[s], at(p, e, 1, 1))
                    if e:
                        pe.wait_ge(taken, at(p, e, 1, 0))
                    for x, (a, b) in enumerate(pieces):
                        for k in range(KD):
                            for n, (w, h) in enumerate(((w_high, high), (w_high, low), (w_low, high))):
                                last = nc.tensor.matmul(K.bank[3 * s + x][:, 0:b - a], w[:, s, k, :], h[:, k, a:b],
                                                        start=k + n == 0, stop=k == KD - 1 and n == 2)
                    last.then_inc(done, 1)

            def down(p, chunks=GRP):
                pe.wait_ge(act_low, p * GRP + chunks)
                for q in range(QUARTERS):
                    pe.wait_ge(d_low_made, p * QUARTERS + (q + 1))
                    for t in range(TILES):
                        n = q * TILES + t
                        pe.wait_ge(down_taken, p * PRODUCTS + (n + 1))
                        for k in range(chunks):
                            for m, (a, w) in enumerate(((a_high, d_high), (a_high, d_low), (a_low, d_high))):
                                last = nc.tensor.matmul(K.bank[6 + n % 2][:, 0:256], a[:, k, t * P:(t + 1) * P], w[:, q % 2, k, :],
                                                        start=k + m == 0, stop=k == chunks - 1 and m == 2)
                        last.then_inc(down_done, 1)

            up_and_gate(0, 0)
            pe.wait_ge(padded, 2)
            with pe.Fori(0, loops) as p:
                for e in range(1, GRP + 1):
                    up_and_gate(p, e)
                down(p)
            up_and_gate(loops, 1)
            down(loops, left)

        @block.scalar
        def _(act):
            def weights(s, p, e):
                act.wait_ge(w_came[s], at(p, e, 16, 16))
                nc.scalar.activation(w_high[:, s], landing[:, s], ACT.Copy).then_inc(w_split[s], 1)

            def down(p, q, k=GRP):
                if q >= 2:
                    act.wait_ge(down_done, p * PRODUCTS + (q - 1) * TILES)
                act.wait_ge(d_came, p * (QUARTERS * 16) + (q + 1) * 16)
                nc.scalar.activation(d_high[:, q % 2, 0:k], d_landing[:, 0:k], ACT.Copy).then_inc(d_split, 1)

            def chunk(p, e, k=None, more=True):
                act.wait_ge(up_done, at(p, e, 1, 1))
                if more:
                    weights(0, p, e + 1)
                if e:
                    act.wait_ge(conv_done, at(p, e, 1, 0))
                nc.scalar.activation(ext[:, 2:2 + FREE3], K.bank[0][:, 0:FREE3], ACT.Copy)
                nc.scalar.activation(ext[:, 2 + FREE3:2 + 2 * FREE3], K.bank[1][:, 0:FREE3], ACT.Copy)
                nc.scalar.activation(ext[:, 2 + 2 * FREE3:2 + SEQ], K.bank[2][:, 0:SEQ - 2 * FREE3], ACT.Copy)
                nc.scalar.activation(ext[:, 1026:1074].rearrange("p (n q) -> p n q", n=NS)[:, :, 2:6],
                                     K.bank[2][:, SEQ - 2 * FREE3:FREE3].rearrange("p (n q) -> p n q", n=NS),
                                     ACT.Copy).then_inc(up_taken, 1)
                if k:
                    down(p, 0, k)
                    down(p, 1, k)
                act.wait_ge(conv_done, at(p, e, 1, 1))
                nc.scalar.activation(ct, ct, ACT.Gelu_apprx_tanh).then_inc(gelu_done, 1)
                if more:
                    act.wait_ge(gate_done, at(p, e, 1, 1))
                    weights(1, p, e + 1)
                    if k:
                        down(p, 2, k)
                        down(p, 3, k)
                        act.wait_ge(down_done, p * PRODUCTS + PRODUCTS)
                act.wait_ge(act_made, at(p, e, 1, 1))
                nc.scalar.activation(a_high[:, e % GRP, 0:T], ct, ACT.Copy).then_inc(act_split, 1)

            weights(0, 0, 0)
            weights(1, 0, 0)
            chunk(0, 0)
            with act.Fori(0, loops) as p:
                for e in range(1, GRP + 1):
                    chunk(p, e, GRP if e == GRP else None)
            chunk(loops, 1, left, more=False)
            down(loops, 2, left)
            down(loops, 3, left)
            act.wait_ge(padded, 2)
            for t in range(TILES):
                r = rows_of(t)
                act.wait_ge(down_taken, 2 + loops * PRODUCTS + 3 * TILES + t + 1)
                if t:
                    act.wait_ge(squares, t)
                nc.scalar.activation(square[:r, :], K.X[:r, t, :], ACT.Square, accum_out=ss[:r, t:t + 1]).then_inc(squares, 1)
                act.wait_ge(squares, t + 1)
                nc.scalar.activation(std[:r, t:t + 1], ss[:r, t:t + 1], ACT.Sqrt, bias=K.eps[:r, 0:1], scale=1.0 / D).then_inc(std_ready, 1)

        @block.vector
        def _(dve):
            dve.sem_inc(down_taken, 2)
            dve.wait_ge(small, 32)
            dve.wait_ge(zeroed, 2)

            def chunk(p, e):
                n = 0

                def link(ins):
                    nonlocal n
                    n += 1
                    ins.then_inc(vch, 1)
                    dve.wait_ge(vch, at(p, e, LINKS, n))

                c = bass.ds(p * GRP + e, 1)
                es = ext[:, 1026:1074].rearrange("p (n q) -> p n q", n=NS)
                cs = ct[:, SEQ:T].rearrange("p (n q) -> p n q", n=NS)
                w = [cw[:, x:x + 1] for x in range(4)]
                link(nc.vector.tensor_copy(cw, cwb[:, c, :].rearrange("p a n -> p (a n)")))
                link(nc.vector.tensor_copy(es[:, :, 0:2], prev[:, c, :].rearrange("p a (n q) -> p (a n) q", q=2)))
                dve.wait_ge(up_taken, at(p, e, 1, 1))
                if e:
                    dve.wait_ge(act_low, at(p, e, 1, 0))
                nc.vector.tensor_scalar(ct[:, 0:SEQ], ext[:, 0:SEQ], w[0], w[3], ALU.mult, ALU.add)
                link(nc.vector.tensor_scalar(cs, es[:, :, 0:4], w[0], w[3], ALU.mult, ALU.add))
                nc.vector.scalar_tensor_tensor(ct[:, 0:SEQ], ext[:, 1:SEQ + 1], w[1], ct[:, 0:SEQ], ALU.mult, ALU.add)
                link(nc.vector.scalar_tensor_tensor(cs, es[:, :, 1:5], w[1], cs, ALU.mult, ALU.add))
                nc.vector.tensor_copy(co[:, c, 0:2].rearrange("p a n -> p (a n)"), ext[:, SEQ:SEQ + 2])
                link(nc.vector.tensor_copy(co[:, c, 2:18].rearrange("p a (n q) -> p (a n) q", q=2), es[:, :, 4:6]))
                nc.vector.scalar_tensor_tensor(ct[:, 0:SEQ], ext[:, 2:SEQ + 2], w[2], ct[:, 0:SEQ], ALU.mult, ALU.add)
                link(nc.vector.scalar_tensor_tensor(cs, es[:, :, 2:6], w[2], cs, ALU.mult, ALU.add))
                dve.sem_inc(conv_done, 1)
                dve.wait_ge(gelu_done, at(p, e, 1, 1))
                dve.wait_ge(gate_done, at(p, e, 1, 1))
                for x, (a, b) in enumerate(pieces):
                    last = nc.vector.tensor_tensor(ct[:, a:b], ct[:, a:b], K.bank[3 + x][:, 0:b - a], ALU.mult)
                last.then_inc(act_made, 1)
                dve.wait_ge(act_made, at(p, e, 1, 1))
                dve.sem_inc(gate_taken, 1)

            def add(p, q, t):
                x = K.X[:rows_of(t), t, q * 256:(q + 1) * 256]
                n = q * TILES + t
                dve.wait_ge(down_done, p * PRODUCTS + (n + 1))
                if q == 0 and t == 0:
                    dve.wait_ge(down_taken, p * PRODUCTS + 2)
                nc.vector.tensor_tensor(x, K.bank[6 + n % 2][:rows_of(t), 0:256], x, ALU.add).then_inc(down_taken, 1)

            def norm(t):
                r = rows_of(t)
                dve.wait_ge(std_ready, t + 1)
                nc.vector.reciprocal(rs[:r, t:t + 1], std[:r, t:t + 1]).then_inc(rs_ready, 1)
                dve.wait_ge(rs_ready, t + 1)
                nc.vector.scalar_tensor_tensor(K.X[:r, t, :], K.X[:r, t, :], rs[:r, t:t + 1], g[:r, :], ALU.mult, ALU.mult).then_inc(y, 1)

            chunk(0, 0)
            with dve.Fori(0, loops) as p:
                for e in range(1, GRP + 1):
                    chunk(p, e)
                for q in range(QUARTERS):
                    for t in range(TILES):
                        add(p, q, t)
            chunk(loops, 1)
            dve.wait_ge(gain_came, 16)
            for q in range(QUARTERS):
                for t in range(TILES):
                    add(loops, q, t)
                    if q == QUARTERS - 1 and t >= 1:
                        norm(t - 1)
            norm(TILES - 1)


class Places:

    def outs(self, n):
        self.n_out += n
        return self.n_out


def program(nc, I, O):
    ctx = ExitStack()
    with ctx:
        K = Places()
        K.n_out, K.page_regs = 0, None
        first_part, K.sems = ExitStack(), []

        def phase_sem(name):
            K.sems.append(first_part.enter_context(nc.semaphore(name)))
            return K.sems[-1]

        K.sem = phase_sem
        sb = lambda name, shape, dt=F32: ctx.enter_context(nc.sbuf_tensor(name, shape, dt))
        K.ident = sb("ident", [P, P])
        K.gains = sb("gains", [P, 5, KD])
        K.GT = sb("gates_by_token", [P, TILES, 3 * H])
        K.GS = sb("gates_by_head", [P, H, TILES - 1, 3])
        K.stat = sb("stat", [P, 3, 3 * TILES])
        K.eps = sb("eps", [P, 1])
        K.table = sb("table", [BUCKETS + 1, H])
        K.page_table = sb("pages", [1, NS * NPAGE], I32)
        K.n_pool = I["pool_sel"].shape[0]
        x_place, big_place, top_place = ExitStack(), ExitStack(), ExitStack()
        x = x_place.enter_context(nc.sbuf_tensor("x", [P, TILES * D], F32, side="right"))
        K.big = big_place.enter_context(nc.sbuf_tensor("big", [P, BIG], F32, side="right"))
        K.top = top_place.enter_context(nc.sbuf_tensor("top", [P, TOP], F32))
        K.tmp = K.top[:, O_TMP:O_TMP + 2 * D]
        K.ps = ctx.enter_context(nc.psum_tensor("ps", [P, 8 * 512], F32))
        K.bank = [K.ps[:, 512 * b:512 * (b + 1)] for b in range(8)]
        K.ps4 = K.ps[:, 0:2048]
        K.junk = K.ps[:, 3072:4096]
        K.X = x[:, :].rearrange("p (t n) -> p t n", t=TILES)
        K.HT = K.big[:, O_HT:O_W].rearrange("p (k n) -> p k n", k=KD)
        K.M = K.top[:, O_M:O_FM].rearrange("p (t n) -> p t n", t=TILES)
        K.FM = K.top[:, O_FM:O_VT].rearrange("p (c n) -> p c n", c=8)
        K.VT = K.top[:, O_VT:O_TMP].rearrange("p (t n) -> p t n", t=TILES)
        cp = K.top[:, O_CP:TOP]
        K.KCP, K.VCP = cp[:, 0:63], cp[:, 64:192]
        K.KCS = cp[:, 192:696].rearrange("p (n c) -> p n c", n=NS)
        K.VCS = cp[:, 696:1720].rearrange("p (n c) -> p n c", n=NS)
        K.vec_dram = nc.dram_tensor("bias_rows", [H, VECS + VECW], F32).ap()
        K.gates_dram = nc.dram_tensor("sample_gates", [SROWS, 3 * H], F32).ap()
        K.o_dram = nc.dram_tensor("sample_out", [SROWS, DA], F32).ap()
        K.out_sem, K.gates_sem, K.wtm_sem, K.gating_sem, K.x_came = (
            ctx.enter_context(nc.semaphore(name)) for name in
            ("outputs_written", "gates_in_dram", "token_major_weights", "gating_operands", "x_came_again"))
        K.slots = [a.rearrange("p (v n) -> p v n", v=2) for a in (x[:, 0:8192], K.big[:, O_HT:O_HT + 8192])]
        K.slots_came = [K.sem(f"pages_half{i}") for i in range(2)]
        t = K.top[:, O_TMP:O_TMP + 2 * D]
        K.sample_small = (t[:, 0:128], t[:, 128:256], t[:, 256:384].rearrange("p (h n) -> p h n", h=2), t[:, 384:401],
                          t[:, 402:406], t[:, 408:416], t[:, 416:422].rearrange("p (h b) -> p h b", h=2), t[:, 424:438])
        c = K.x_tail = x[:, 8192:9216]
        K.cmp_small = ([c[:, 64 * v:64 * (v + 1)] for v in range(2)], [c[:, 128 + 16 * v:144 + 16 * v] for v in range(2)],
                       c[:, 160:162], c[:, 162:163], c[:, 192:320], c[:, 164:166])
        K.cmp_came = K.sem("compress_operands")
        K.cmp_w1 = [K.big[:, O_HT + 8192 + 2048 * v:O_HT + 10240 + 2048 * v].rearrange("p (q h) -> p q h", h=P) for v in range(2)]
        K.cmp_w1_came = [K.sem(f"cmp_w{v}_came") for v in range(2)]
        K.sample_came, K.sample_out, K.sample_back = (K.sem(f"sample_{n}") for n in ("operands", "out_dram", "out_back"))
        K.sample_o = K.big[:, BIG - 128:BIG]
        K.pools = {"cmp": I["pool_cmp"], "sel": I["pool_sel"]}
        K.windows = [(K.M[:, 0:4, DA:D], K.M[:, 4:8, DA:D]),
                     tuple(K.big[:, O_HT + 8192 + 2048 * i:O_HT + 10240 + 2048 * i].rearrange("p (n t) -> p n t", n=4) for i in range(2))]
        K.windows_came = [K.sem(f"windows{i}") for i in range(2)]

        const_came, eps_set = K.sem("const_came"), K.sem("eps_set")
        with nc.Block() as block:
            @block.sync
            def _(sp):
                sp.dma_start(K.ident[:, :], I["ident"]).then_inc(const_came, 16)
                sp.dma_start(K.gains[:, :, :], I["gains"]).then_inc(const_came, 16)
                sp.wait_ge(const_came, 32)

            @block.gpsimd
            def _(pool):
                nc.gpsimd.memset(K.eps[:, :], EPS).then_inc(eps_set, 1)
                pool.wait_ge(eps_set, 1)

        fm = Ring(K, "fm", I["w_fm"], K.top[:, O_FM - 2048:O_FM])
        beside, store_rows, rows_stored = bias_rows(nc, K, I, fm)
        norm_phase(nc, K, "mix", x_tiles(K), D, K.gains[:, 0, :], K.HT, x_loads(K, I), beside)

        def states(sp):
            sp.wait_ge(rows_stored, 16)
            for u in range(2):
                sp.wait_ge(K.fm_taken[u], 5)
            sp.dma_start(O["fm"].rearrange("c p n -> p c n"), K.FM[:, 4:8, :]).then_inc(K.out_sem, 16)
            for v in range(2):
                sp.dma_start(O["win_old"][v], I["win_old"][v][:, TS:WIN, :]).then_inc(K.out_sem, 16)
            K.outs(3)


        def small(sp):
            for to, of in gating_operands(K, I):
                sp.dma_start(to, of).then_inc(K.gating_sem, 16)

        feature_major(nc, K, fm, 8, K.HT, T, K.FM,
                      {"sync": states, ("sync", 0): store_rows, ("sync", 1): lambda sp: gather(sp, K, 0, "cmp", 0, 2),
                       ("sync", 2): lambda sp: gather(sp, K, 0, "cmp", 2, 2), ("sync", 5): small})
        gating_phase(nc, K, I, O)
        compress_phase(nc, K, I)
        sample_attention(nc, K, I)
        prompt_attention(nc, K, I)
        with nc.Block() as block:
            parts = [K.sems[i::5] for i in range(5)]

            @block.gpsimd
            def _(pool):
                for s in parts[0]:
                    pool.sem_clear(s)

            @block.sync
            def _(sp):
                for s in parts[1]:
                    sp.sem_clear(s)

            @block.scalar
            def _(act):
                for s in parts[2]:
                    act.sem_clear(s)

            @block.vector
            def _(dve):
                for s in parts[3]:
                    dve.sem_clear(s)

            @block.tensor
            def _(pe):
                for s in parts[4]:
                    pe.sem_clear(s)

        first_part.close()
        wo = projection_weights(K, "wo", I["w_o"])
        memx = K.top[:, O_FM + 4096:O_FM + 6144].rearrange("p (t n) -> p t n", t=2)
        mk = Ring(K, "mk", I["w_mk"], K.top[:, O_FM + 6144:O_FM + 8192])
        mem_came = [K.sem(f"memory_rows{t}") for t in range(2)]

        def weights_and_memory(sp, added):
            wo[2](sp)
            for t in range(2):
                sp.dma_start(memx[:, t, :], I["mem_prompt"][t]).then_inc(mem_came[t], 16)
            mk.load(sp)

        project_norm(nc, K, "wo", wo, K.HT, K.gains[:, 2, :], K.HT, K.top[:, O_FM:O_FM + 4 * D],
                     before=([(K.M[:rows_of(t), t, :], rows_of(t), t * P) for t in range(TILES)], K.gains[:, 1, :]),
                     sync=weights_and_memory, x_came=K.x_came)
        m = K.top[:, O_M:O_FM]
        memt = m[:, 2048:4096].rearrange("p (k n) -> p k n", k=KD)
        mkt = m[:, 4096:6144].rearrange("p (k n) -> p k n", k=KD)
        mv = m[:, 6144:8192].rearrange("p (t n) -> p t n", t=2)
        xq = Ring(K, "xq", I["w_xq"], K.top[:, O_TMP:O_TMP + 2048])
        w_mv = projection_weights(K, "mv", I["w_mv"])

        norm_phase(nc, K, "mem", [(memx[:, t, :], P, t * P) for t in range(2)], D, K.gains[:, 3, :], memt,
                   arrived=mem_came, extra={"sync": w_mv[2]})
        feature_major(nc, K, mk, 8, memt, MEM, mkt)
        memory_values(nc, K, I, O, memt, mkt, mv, w_mv, xq)
        feature_major(nc, K, xq, 8, K.HT, T, K.FM)
        sample, xo = CrossSample(K), projection_weights(K, "xo", I["w_xo"])
        cross_prompt(nc, K, I, K.FM, mkt, mv, sample)
        cross_sample(nc, K, I, sample, xo)
        top_place.close()
        split_mem, norm_mem = ExitStack(), ExitStack()
        high, low = (split_mem.enter_context(nc.sbuf_tensor(f"ff_in_{n}", [P, KD, T], F32R)) for n in ("high", "low"))
        landing = split_mem.enter_context(nc.sbuf_tensor("ff_weights", [P, 2, KD, P], F32))
        scratch = norm_mem.enter_context(nc.sbuf_tensor("ff_scaled", [P, 2 * D], F32))[:, :]
        whole = norm_mem.enter_context(nc.sbuf_tensor("ff_normed", [P, 2, KD, P], F32))
        ff_came = [K.sem(f"ff_{name}_came") for name in ("up", "gate")]

        def first_chunk(sp, added):
            for x, name in enumerate(("w_up", "w_gate")):
                sp.dma_start(landing[:, x], I[name][0]).then_inc(ff_came[x], 16)

        project_norm(nc, K, "xo", xo, K.HT, K.gains[:, 4, :], None, scratch, sync=first_chunk, split=(high, low, whole))
        norm_mem.close()
        big_place.close()
        with ExitStack() as mem:
            ffn(nc, K, I, O, mem, high, low, landing, ff_came)
        split_mem.close()
        x_place.close()


def bucket(dist):
    n = np.maximum(dist, 0)
    exact = BUCKETS // 2
    large = exact + (np.log(np.maximum(n, 1) / exact) / math.log(MAXDIST / exact) * (BUCKETS - exact)).astype(np.int64)
    return np.where(n < exact, n, np.minimum(large, BUCKETS - 1))


def constants():
    c = {"ident": np.eye(P)}
    oh = np.zeros((BUCKETS + 1, VECS + VECW))
    d = np.concatenate([np.arange(VECS) - 1023, np.arange(VECW) - 127])
    dead = (d < 0) | ((np.arange(len(d)) >= VECS) & (d >= WIN))
    oh[np.where(dead, BUCKETS, bucket(d)), np.arange(len(d))] = 1
    c["oh_v"] = oh
    new = np.arange(SROWS) % TS
    cmp_end = np.arange(NCMP) * CS + CL - 1
    pos = np.concatenate([np.arange(PAST), PAST + new, PAST + new, PAST - WIN + np.arange(WIN), cmp_end])
    oh = np.zeros((TS, BUCKETS, len(pos)))
    for q in range(TS):
        oh[q, bucket(PAST + q - pos), np.arange(len(pos))] = 1
    c["oh_s"] = oh.reshape(P, -1)
    r = np.arange(P)
    seq, grp, qry = r // 32, r // 16 % 2, r % 4
    c["dq"] = (r[:, None] // 32 == qry[None, :]) * 1.0
    c["gmat"] = ((seq[:, None] == seq) & (grp[:, None] == grp) & (qry[:, None] == qry)) * 1.0
    k = np.arange(SROWS)
    mask = np.zeros((P, 2, 2, SROWS))
    for half in range(2):
        ok = (seq[:, None] + 4 * half == k[None, :] // TS) & (k[None, :] % TS <= qry[:, None])
        mask[:, half, :, :] = np.where(ok, 0, NEG)[:, None, :]
    c["mask_new"] = mask.reshape(P, 2, 2 * SROWS)
    c["mask_win"] = np.where(np.arange(4)[None, :] > qry[:, None], 0, NEG)
    c0, s0 = np.arange(NCMP)[:, None] * CS, np.arange(NSEL)[None, :] * SELB
    c["overlap"] = ((c0 < s0 + SELB) & (c0 + CL > s0)) * 1.0
    c["jidx"] = np.broadcast_to(np.arange(1, 15), (P, 14))
    c["causal"] = (r[:, None] <= r[None, :]) * 1.0
    c["causal_s"] = ((k[:, None] // TS == k[None, :] // TS) & (k[:, None] <= k[None, :])) * 1.0
    c["cmp_valid"] = (r[:, None] >= CL - 1) * 1.0
    return {n: np.ascontiguousarray(a, np.float32) for n, a in c.items()}


def stationary(w):
    r, n = w.shape
    return w.reshape(r // P, P, n // P, P).transpose(2, 1, 0, 3)


def moving(w, width):
    r, n = w.shape
    return w.reshape(r // P, P, n // width, width).transpose(2, 1, 0, 3)


def kernel(**inputs):
    import concourse.bacc as bacc
    from concourse.bass_utils import run_bass_kernel_spmd

    x = {n: np.asarray(a) for n, a in inputs.items()}
    w = x["w_in"][0]
    q0, kv0, g0 = 2 * DA, 2 * DA + DA, 2 * DA + DA + 6 * KV
    q = w[:, q0:kv0].reshape(D, 2, HPG, HD).transpose(0, 2, 1, 3).reshape(D, DA)
    kv = [w[:, kv0 + i * KV:kv0 + (i + 1) * KV] for i in range(6)]
    L = {
        "x_prompt": x["x_prompt"].reshape(SEQ // P, P, D),
        "x_sample": x["x_sample"].reshape(SROWS, D),
        "mem_prompt": x["mem_prompt"].reshape(MEM // P, P, D),
        "page_table": x["page_table"].reshape(1, -1).astype(np.int32),
        "w_fm": stationary(np.concatenate([q, kv[0], kv[1], kv[2], kv[4]], 1)),
        "w_tm": np.concatenate([w[:, :q0], kv[3], kv[5], w[:, g0:]], 1).reshape(KD, P, TMW),
        "gains": np.stack([x["g_mix"][0], np.concatenate([x["g_a"][0], x["g_b"][0]]), x["g_xa"][0], x["g_mem"][0],
                           x["g_ffn"][0]]).reshape(5, KD, P).transpose(2, 0, 1),
        "ln_v_g": x["ln_v_g"], "ln_v_b": x["ln_v_b"], "g_final": x["g_final"][None],
        "ws_t": x["w_s"][0].transpose(2, 0, 1),
        "ws_s": np.tile(x["w_s"][0][:, :TS, :TS].transpose(2, 0, 1), (NS, 1, NS)),
        "bs_t": x["b_s"][0].T,
        "bs_s": np.tile(x["b_s"][0][:, :TS].T, (NS, 1)),
        "w_cmp1": np.stack([x[f"w_cmp1_{c}"][0].reshape(16, P, P).transpose(1, 0, 2) for c in "kv"]),
        "w_cmp2": np.stack([x[f"w_cmp2_{c}"][0] for c in "kv"]),
        "pe_cmp": np.stack([x[f"pe_cmp_{c}"][0].reshape(16, P).T for c in "kv"]),
        "b_cmp1": np.stack([x[f"b_cmp1_{c}"][0] for c in "kv"], 1),
        "b2k": np.tile(x["b_cmp2_k"][0], 2)[:, None],
        "b2v": np.tile(x["b_cmp2_v"][0], 2)[None],
        "pool_cmp": np.stack([x[f"cache_cmp_{c}"][0].reshape(-1, PAGE // 2, 2, HKV, HD).transpose(0, 2, 4, 3, 1).reshape(-1, P, HKV, PAGE // 2)
                              for c in "kv"], 2),
        "pool_sel": np.stack([x["cache_sel_k"][0].reshape(-1, PAGE, KV).transpose(0, 2, 1),
                              x["cache_sel_v"][0].reshape(-1, PAGE, KV)], 2),
        "win_kt": x["cache_win_k"][0].reshape(NS, WIN, KV).transpose(0, 2, 1),
        "win_v": x["cache_win_v"][0].reshape(NS, WIN, KV),
        "win_old": np.stack([x[f"cache_win_{c}"][0].reshape(NS, WIN, KV) for c in "kv"]),
        "rel_bias": x["rel_bias"],
        "w_o": moving(x["w_o"][0], 512), "w_mv": moving(x["w_mv"][0], 512), "w_xo": moving(x["w_xo"][0], 512),
        "w_mk": stationary(x["w_mk"][0]), "w_xq": stationary(x["w_xq"][0]),
        "w_up": stationary(x["w_up"][0]), "w_gate": stationary(x["w_gate"][0]),
        "w_down": moving(x["w_down"][0], 256),
        "mem_kt": x["cache_mem_k"][0].reshape(NS, MEM, KD, P).transpose(0, 3, 2, 1),
        "mem_v": x["cache_mem_v"][0].reshape(NS, MEM, D),
        "conv_prev": x["state_conv"][0].transpose(2, 0, 1).reshape(FC, P, NS * 2).transpose(1, 0, 2),
        "conv_wb": np.concatenate([x["conv_w"][0], x["conv_b"]]).reshape(4, FC, P).transpose(2, 1, 0),
    }
    L.update(constants())
    shapes = {
        "y_prompt": (SEQ // P, P, D), "y_sample": (SROWS, D), "fm": (4, P, T), "vt": (SEQ // P, P, 2 * KV),
        "vt_s": (SROWS, 2 * KV), "win_old": (2, NS, WIN - TS, KV), "gmlp_v": (SROWS, DA),
        "mem_k": (P, KD, MEM), "mem_v": (MEM // P, P, D), "conv": (P, FC, 18),
    }
    nc = bacc.Bacc("TRN2", target_bir_lowering=False, num_devices=1)
    arrays, I, O = {}, {}, {}
    for n, a in L.items():
        a = np.ascontiguousarray(a)
        arrays[f"in_{n}"] = a
        I[n] = nc.dram_tensor(f"in_{n}", a.shape, mybir.dt.from_np(a.dtype), kind="ExternalInput").ap()
    for n, s in shapes.items():
        O[n] = nc.dram_tensor(f"out_{n}", s, F32, kind="ExternalOutput").ap()
    program(nc, I, O)
    r = run_bass_kernel_spmd(nc, [arrays], core_ids=[0]).results[0]
    o = {n: np.asarray(r[f"out_{n}"]) for n in shapes}

    fm = o["fm"].transpose(0, 2, 1)
    vt = o["vt"].reshape(SEQ, 2 * KV)
    rows = lambda a: a.reshape(1, 1, -1, HKV, HD)
    srows = lambda a: a.reshape(1, NS, TS, HKV, HD)
    vs, vw = o["vt_s"][:, :KV], o["vt_s"][:, KV:]
    win = [np.concatenate([o["win_old"][i], a.reshape(NS, TS, KV)], 1).reshape(1, NS, WIN, HKV, HD)
           for i, a in enumerate((fm[3][SEQ:], vw))]
    conv = o["conv"].transpose(1, 0, 2).reshape(FF, 18)
    return (o["y_prompt"].reshape(1, SEQ, D), o["y_sample"].reshape(NS, TS, D),
            rows(fm[0][:SEQ]), rows(fm[1][:SEQ]), rows(fm[2][:SEQ]), rows(vt[:, :KV]),
            rows(fm[3][SEQ - WIN:SEQ]), rows(vt[SEQ - WIN:, KV:]),
            o["mem_k"].transpose(2, 1, 0).reshape(1, 1, MEM, XH, XHD), o["mem_v"].reshape(1, 1, MEM, XH, XHD),
            conv[:, :2].T.reshape(1, 1, 2, FF),
            srows(fm[0][SEQ:]), srows(fm[1][SEQ:]), srows(fm[2][SEQ:]), srows(vs),
            win[0], win[1], o["gmlp_v"].reshape(1, NS, TS, DA),
            conv[:, 2:].reshape(FF, NS, 2).transpose(1, 2, 0).reshape(1, NS, 2, FF))
```
